# Optimizing a Trainium2 kernel written in Bass

```python
import math
import jax, jax.numpy as jnp
from jax import lax
import numpy as np

D_MODEL = 1024
BATCH = 1
SEQ = 256
DEPTH = 2

GRID_W = 64
CTX_LEN = 256
HEAD_DIM = 64
N_Q_HEADS = 8
N_KV_HEADS = 2
Q_PER_KV = N_Q_HEADS // N_KV_HEADS
ATTN_WIDTH = N_Q_HEADS * HEAD_DIM
KV_WIDTH = N_KV_HEADS * HEAD_DIM
N_FOURIER_GROUPS = 8
FOURIER_GROUP_DIM = 64
FOURIER_WIDTH = N_FOURIER_GROUPS * FOURIER_GROUP_DIM
MIX_WIDTH = ATTN_WIDTH + FOURIER_WIDTH
IN_WIDTH = ATTN_WIDTH + 2 * KV_WIDTH + FOURIER_WIDTH
WINDOW = 128
BLOCK = 128
FFN_HIDDEN = -(-8 * D_MODEL // (3 * 256)) * 256
ROPE_THETA = 10000.0
ROPE_PAIRS_PER_AXIS = HEAD_DIM // 4
RMS_EPS = 1e-6
N_MOD = 6
NEG_INF = -1e30


def rmsnorm(x, g):
    xf = x.astype(jnp.float32)
    y = xf * lax.rsqrt(jnp.mean(xf * xf, axis=-1, keepdims=True) + RMS_EPS)
    return (y * g.astype(jnp.float32)).astype(x.dtype)

def modulate(h, shift, scale):
    return h * (1.0 + scale) + shift

def axial_rope_tables(rows):
    row = jnp.broadcast_to(jnp.arange(rows)[:, None], (rows, GRID_W)).reshape(-1).astype(jnp.float32)
    col = jnp.broadcast_to(jnp.arange(GRID_W)[None, :], (rows, GRID_W)).reshape(-1).astype(jnp.float32)
    freqs = ROPE_THETA ** (-jnp.arange(ROPE_PAIRS_PER_AXIS, dtype=jnp.float32) / ROPE_PAIRS_PER_AXIS)
    ang = jnp.concatenate([row[:, None] * freqs, col[:, None] * freqs], axis=-1)
    return jnp.cos(ang), jnp.sin(ang)

def apply_axial_rope(x, cos, sin):
    xf = x.astype(jnp.float32).reshape(*x.shape[:-1], HEAD_DIM // 2, 2)
    x1, x2 = xf[..., 0], xf[..., 1]
    c = cos[None, :, None, :]
    s = sin[None, :, None, :]
    out = jnp.stack([x1 * c - x2 * s, x1 * s + x2 * c], axis=-1).reshape(x.shape)
    return out.astype(x.dtype)

def sink_column(sink, lead_shape):
    sk = sink.astype(jnp.float32).reshape(N_KV_HEADS, Q_PER_KV)[:, :, None, None]
    return jnp.broadcast_to(sk, lead_shape + (1,))

def windowed_gqa_with_context(q, k, v, kc, vc, sink):
    B, S = q.shape[0], q.shape[1]
    nb = S // BLOCK
    scale = HEAD_DIM ** -0.5
    qb = q.reshape(B, nb, BLOCK, N_KV_HEADS, Q_PER_KV, HEAD_DIM)
    pad = ((0, 0), (BLOCK, BLOCK), (0, 0), (0, 0))
    kp = jnp.pad(k, pad).reshape(B, nb + 2, BLOCK, N_KV_HEADS, HEAD_DIM)
    vp = jnp.pad(v, pad).reshape(B, nb + 2, BLOCK, N_KV_HEADS, HEAD_DIM)
    kb = jnp.concatenate([kp[:, :-2], kp[:, 1:-1], kp[:, 2:]], axis=2)
    vb = jnp.concatenate([vp[:, :-2], vp[:, 1:-1], vp[:, 2:]], axis=2)
    s_loc = jnp.einsum('bnqkgd,bnjkd->bnkgqj', qb, kb).astype(jnp.float32) * scale
    q_pos = jnp.arange(nb)[:, None] * BLOCK + jnp.arange(BLOCK)[None, :]
    k_pos = (jnp.arange(nb)[:, None] - 1) * BLOCK + jnp.arange(3 * BLOCK)[None, :]
    valid = (jnp.abs(q_pos[:, :, None] - k_pos[:, None, :]) <= WINDOW) & (k_pos[:, None, :] >= 0) & (k_pos[:, None, :] < S)
    s_loc = jnp.where(valid[None, :, None, None], s_loc, NEG_INF)
    s_ctx = jnp.einsum('bnqkgd,bckd->bnkgqc', qb, kc).astype(jnp.float32) * scale
    logits = jnp.concatenate([s_loc, s_ctx, sink_column(sink, s_loc.shape[:-1])], axis=-1)
    p = jax.nn.softmax(logits, axis=-1)
    n_loc = 3 * BLOCK
    n_ctx = kc.shape[1]
    p_loc = p[..., :n_loc].astype(v.dtype)
    p_ctx = p[..., n_loc:n_loc + n_ctx].astype(v.dtype)
    out = jnp.einsum('bnkgqj,bnjkd->bnqkgd', p_loc, vb) + jnp.einsum('bnkgqc,bckd->bnqkgd', p_ctx, vc)
    return out.reshape(B, S, ATTN_WIDTH)

def context_gqa(qc, kc, vc, sink):
    B, C = qc.shape[0], qc.shape[1]
    scale = HEAD_DIM ** -0.5
    qg = qc.reshape(B, C, N_KV_HEADS, Q_PER_KV, HEAD_DIM)
    s = jnp.einsum('bqkgd,bckd->bkgqc', qg, kc).astype(jnp.float32) * scale
    p = jax.nn.softmax(jnp.concatenate([s, sink_column(sink, s.shape[:-1])], axis=-1), axis=-1)[..., :C]
    out = jnp.einsum('bkgqc,bckd->bqkgd', p.astype(vc.dtype), vc)
    return out.reshape(B, C, ATTN_WIDTH)

def fourier_mix(u, w_four):
    B, N = u.shape[0], u.shape[1]
    ug = u.reshape(B, N, N_FOURIER_GROUPS, FOURIER_GROUP_DIM).astype(jnp.float32)
    mixed = jnp.fft.fft2(ug, axes=(1, 3), norm='ortho').real.astype(u.dtype)
    return jnp.einsum('bngc,gcd->bngd', mixed, w_four).reshape(B, N, FOURIER_WIDTH)

def swiglu(h, w_gate, w_up, w_down):
    return (jax.nn.silu(h @ w_gate) * (h @ w_up)) @ w_down

def first_inputs(seed: int = 0) -> dict:
    key = jax.random.key(seed)
    ks = jax.random.split(key, 17)
    f32 = jnp.float32
    D = D_MODEL

    def nrm(k, shape, s):
        return jax.random.normal(k, shape, f32) * s

    return {
        'x': nrm(ks[0], (BATCH, SEQ, D), 1.0),
        'c': nrm(ks[1], (BATCH, D), 1.0),
        'ctx': nrm(ks[2], (BATCH, CTX_LEN, D), 1.0),
        'c_ctx': nrm(ks[3], (D,), 1.0),
        'w_ada': nrm(ks[4], (DEPTH, D, N_MOD * D), 0.5 * D ** -0.5),
        'b_ada': nrm(ks[5], (DEPTH, N_MOD * D), 0.02),
        'norm_pre_mix': 1.0 + nrm(ks[6], (DEPTH, D), 0.05),
        'norm_post_mix': 1.0 + nrm(ks[7], (DEPTH, D), 0.05),
        'norm_pre_ffn': 1.0 + nrm(ks[8], (DEPTH, D), 0.05),
        'norm_post_ffn': 1.0 + nrm(ks[9], (DEPTH, D), 0.05),
        'w_in': nrm(ks[10], (DEPTH, D, IN_WIDTH), D ** -0.5),
        'w_out': nrm(ks[11], (DEPTH, MIX_WIDTH, D), MIX_WIDTH ** -0.5),
        'w_fourier': nrm(ks[12], (DEPTH, N_FOURIER_GROUPS, FOURIER_GROUP_DIM, FOURIER_GROUP_DIM), FOURIER_GROUP_DIM ** -0.5),
        'sink': nrm(ks[13], (DEPTH, N_Q_HEADS), 0.5),
        'w_gate': nrm(ks[14], (DEPTH, D, FFN_HIDDEN), D ** -0.5),
        'w_up': nrm(ks[15], (DEPTH, D, FFN_HIDDEN), D ** -0.5),
        'w_down': nrm(ks[16], (DEPTH, FFN_HIDDEN, D), FFN_HIDDEN ** -0.5),
    }

def first_block(x, c, ctx, c_ctx, w_ada, b_ada, norm_pre_mix, norm_post_mix, norm_pre_ffn, norm_post_ffn,
              w_in, w_out, w_fourier, sink, w_gate, w_up, w_down):
    B, S, D = x.shape
    ROWS = S // GRID_W
    cos, sin = axial_rope_tables(ROWS)
    xc = ctx
    kv_lo, kv_hi = ATTN_WIDTH, ATTN_WIDTH + 2 * KV_WIDTH
    for i in range(DEPTH):
        update_ctx = i < DEPTH - 1
        mod_lat = jax.nn.silu(c) @ w_ada[i] + b_ada[i]
        mod_ctx = jax.nn.silu(c_ctx) @ w_ada[i] + b_ada[i]
        sh1, sc1, g1, sh2, sc2, g2 = [m[:, None, :] for m in jnp.split(mod_lat, N_MOD, axis=-1)]
        csh1, csc1, cg1, csh2, csc2, cg2 = jnp.split(mod_ctx, N_MOD, axis=-1)

        h = modulate(rmsnorm(x, norm_pre_mix[i]), sh1, sc1)
        hc = modulate(rmsnorm(xc, norm_pre_mix[i]), csh1, csc1)
        p = h @ w_in[i]
        q = apply_axial_rope(p[..., :ATTN_WIDTH].reshape(B, S, N_Q_HEADS, HEAD_DIM), cos, sin)
        k = apply_axial_rope(p[..., kv_lo:kv_lo + KV_WIDTH].reshape(B, S, N_KV_HEADS, HEAD_DIM), cos, sin)
        v = p[..., kv_lo + KV_WIDTH:kv_hi].reshape(B, S, N_KV_HEADS, HEAD_DIM)
        u = p[..., kv_hi:]
        kvc = hc @ w_in[i][:, kv_lo:kv_hi]
        C = xc.shape[1]
        kc = kvc[..., :KV_WIDTH].reshape(B, C, N_KV_HEADS, HEAD_DIM)
        vc = kvc[..., KV_WIDTH:].reshape(B, C, N_KV_HEADS, HEAD_DIM)

        attn = windowed_gqa_with_context(q, k, v, kc, vc, sink[i])
        four = fourier_mix(u, w_fourier[i])
        mix = jnp.concatenate([attn, four], axis=-1) @ w_out[i]
        x_mid = x + g1 * rmsnorm(mix, norm_post_mix[i])

        hf = modulate(rmsnorm(x_mid, norm_pre_ffn[i]), sh2, sc2)
        x = x_mid + g2 * rmsnorm(swiglu(hf, w_gate[i], w_up[i], w_down[i]), norm_post_ffn[i])

        if update_ctx:
            qc = (hc @ w_in[i][:, :ATTN_WIDTH]).reshape(B, C, N_Q_HEADS, HEAD_DIM)
            uc = hc @ w_in[i][:, kv_hi:]
            attn_c = context_gqa(qc, kc, vc, sink[i])
            four_c = fourier_mix(uc, w_fourier[i])
            mix_c = jnp.concatenate([attn_c, four_c], axis=-1) @ w_out[i]
            xc_mid = xc + cg1 * rmsnorm(mix_c, norm_post_mix[i])
            hfc = modulate(rmsnorm(xc_mid, norm_pre_ffn[i]), csh2, csc2)
            xc = xc_mid + cg2 * rmsnorm(swiglu(hfc, w_gate[i], w_up[i], w_down[i]), norm_post_ffn[i])
    return x


CHUNK = 64
D_RWKV = D_MODEL // 2
RWKV_HEAD = 64
RWKV_HEADS = D_RWKV // RWKV_HEAD
LORA_W = 64
LORA_A = 64
LORA_V = 32
LORA_G = 160
RWKV_GN_EPS = 64e-5
D_MLSTM = D_MODEL // 2
MLSTM_HEADS = 4
MLSTM_HEAD = D_MLSTM // MLSTM_HEADS
CONV_W = 4
MLSTM_NORM_EPS = 1e-5
D_FF = ((8 * D_MODEL // 3 + 255) // 256) * 256
NORM_EPS = 1e-6
HALF = 0.5

RW_SPLITS = (D_RWKV, D_RWKV, D_RWKV, LORA_W, LORA_A, LORA_G)
ML_SPLITS = (D_MLSTM, D_MLSTM, D_MLSTM, D_MLSTM, MLSTM_HEADS, MLSTM_HEADS)
N_RW_IN = 3 * D_RWKV + LORA_W + LORA_A + LORA_G
N_ML_IN = 4 * D_MLSTM + 2 * MLSTM_HEADS
N_GATE = 2 * D_MODEL
N_IN = N_RW_IN + N_ML_IN + N_GATE


def _rmsnorm(x, g):
    xf = x.astype(jnp.float32)
    y = xf * lax.rsqrt(jnp.mean(xf * xf, axis=-1, keepdims=True) + NORM_EPS)
    return (y * g.astype(jnp.float32)).astype(x.dtype)

def _swiglu(x, w_in, w_out):
    gate, up = jnp.split(x @ w_in, 2, axis=-1)
    return (jax.nn.silu(gate) * up) @ w_out

def _time_shift(z):
    return jnp.pad(z, ((0, 0), (1, 0), (0, 0)))[:, :-1]

def _causal_dwconv(z, w, b):
    K, T = w.shape[0], z.shape[1]
    zp = jnp.pad(z, ((0, 0), (K - 1, 0), (0, 0)))
    out = b
    for j in range(K):
        out = out + w[j] * zp[:, j:j + T]
    return out

def _split_cols(z, sizes):
    out, start = [], 0
    for s in sizes:
        out.append(z[..., start:start + s])
        start += s
    return out

def _head_standardize(y, eps):
    yf = y.astype(jnp.float32)
    mu = jnp.mean(yf, axis=-1, keepdims=True)
    var = jnp.mean(jnp.square(yf - mu), axis=-1, keepdims=True)
    yn = (yf - mu) * lax.rsqrt(var + eps)
    return yn.reshape(y.shape[0], y.shape[1], -1)

def _rwkv7_recurrence(r, w, k, v, kk, b):
    Bn, T, H, N = r.shape
    xs = tuple(jnp.moveaxis(t.astype(jnp.float32), 1, 0) for t in (r, w, k, v, kk, b))

    def step(S, inp):
        r_t, w_t, k_t, v_t, kk_t, b_t = inp
        sa = jnp.einsum('bhvk,bhk->bhv', S, kk_t)
        S = (S * w_t[:, :, None, :]
             - sa[..., :, None] * b_t[:, :, None, :]
             + v_t[..., :, None] * k_t[:, :, None, :])
        return S, jnp.einsum('bhvk,bhk->bhv', S, r_t)

    S0 = jnp.zeros((Bn, H, N, N), jnp.float32)
    _, ys = lax.scan(step, S0, xs)
    return jnp.moveaxis(ys, 0, 1)

def _rwkv7_mixer(r, k, v, xw, xa, xg, w0, w_up, a0, a_up, g_up, k_k, k_a, r_k, gn_w, gn_b):
    Bn, T, _ = r.shape
    heads = lambda t: t.reshape(Bn, T, RWKV_HEADS, RWKV_HEAD)
    w_log = -jax.nn.softplus(-(w0 + jnp.tanh(xw) @ w_up)) - 0.5
    decay = jnp.exp(-jnp.exp(w_log.astype(jnp.float32)))
    a = jax.nn.sigmoid(a0 + xa @ a_up)
    g = jax.nn.sigmoid(xg) @ g_up
    kk = heads(k * k_k).astype(jnp.float32)
    kk = kk / jnp.maximum(jnp.sqrt(jnp.sum(kk * kk, axis=-1, keepdims=True)), 1e-12)
    k = k * (1.0 + (a - 1.0) * k_a)
    rh, kh, vh, ah = heads(r), heads(k), heads(v), heads(a)
    y = _rwkv7_recurrence(rh, heads(decay), kh, vh, kk, kk * ah.astype(jnp.float32))
    y = _head_standardize(y, RWKV_GN_EPS) * gn_w + gn_b
    bonus = (jnp.sum(rh * kh * r_k, axis=-1, keepdims=True) * vh).reshape(Bn, T, -1)
    return ((y + bonus) * g).astype(r.dtype)

def _mlstm_chunkwise(q, k, v, i_pre, f_pre):
    Bn, T, H, d = q.shape
    nc = T // CHUNK
    to_chunks = lambda t: t.astype(jnp.float32).reshape(Bn, nc, CHUNK, H, -1).transpose(1, 0, 3, 2, 4)
    qc = to_chunks(q) * (d ** -0.5)
    kc, vc = to_chunks(k), to_chunks(v)
    lic = to_chunks(i_pre[..., None])[..., 0]
    lfc = jax.nn.log_sigmoid(to_chunks(f_pre[..., None])[..., 0])
    causal = jnp.tril(jnp.ones((CHUNK, CHUNK), bool))

    def step(carry, inp):
        C, n, m = carry
        q_, k_, v_, li, lf = inp
        bcum = jnp.cumsum(lf, axis=-1)
        Dm = jnp.where(causal, bcum[..., :, None] - bcum[..., None, :] + li[..., None, :], -jnp.inf)
        inter = bcum + m[..., None]
        m_t = jnp.maximum(inter, jnp.max(Dm, axis=-1))
        inter_w = jnp.exp(inter - m_t)
        s = jnp.einsum('bhtd,bhsd->bhts', q_, k_) * jnp.exp(Dm - m_t[..., None])
        num = inter_w[..., None] * jnp.einsum('bhvk,bhtk->bhtv', C, q_) + jnp.einsum('bhts,bhsv->bhtv', s, v_)
        den = inter_w * jnp.einsum('bhk,bhtk->bht', n, q_) + jnp.sum(s, axis=-1)
        h = num / jnp.maximum(jnp.abs(den), jnp.exp(-m_t))[..., None]
        bL = bcum[..., -1]
        ws_log = bL[..., None] - bcum + li
        m_new = jnp.maximum(bL + m, jnp.max(ws_log, axis=-1))
        sdec = jnp.exp(bL + m - m_new)
        ws = jnp.exp(ws_log - m_new[..., None])
        C_new = sdec[..., None, None] * C + jnp.einsum('bhs,bhsv,bhsk->bhvk', ws, v_, k_)
        n_new = sdec[..., None] * n + jnp.einsum('bhs,bhsk->bhk', ws, k_)
        return (C_new, n_new, m_new), h

    carry0 = (jnp.zeros((Bn, H, d, d), jnp.float32), jnp.zeros((Bn, H, d), jnp.float32),
              jnp.zeros((Bn, H), jnp.float32))
    _, hs = lax.scan(step, carry0, (qc, kc, vc, lic, lfc))
    return hs.transpose(1, 0, 3, 2, 4).reshape(Bn, T, H, d)

def _mlstm_mixer(mq, mk, mv, mo, mi, mf, conv_w, conv_b, i_bias, f_bias, norm_w):
    Bn, T, _ = mq.shape
    heads = lambda t: t.reshape(Bn, T, MLSTM_HEADS, MLSTM_HEAD)
    qk = jax.nn.silu(_causal_dwconv(jnp.concatenate([mq, mk], axis=-1), conv_w, conv_b))
    q, k = jnp.split(qk, 2, axis=-1)
    h = _mlstm_chunkwise(heads(q), heads(k), heads(mv), mi + i_bias, mf + f_bias)
    h = _head_standardize(h, MLSTM_NORM_EPS) * norm_w
    return (jax.nn.sigmoid(mo) * h).astype(mq.dtype)

def second_inputs(seed: int = 0) -> dict:
    key = jax.random.key(seed)
    ks = iter(jax.random.split(key, 48))
    f32 = jnp.float32
    L = DEPTH

    def nrm(shape, scale):
        return jax.random.normal(next(ks), shape, f32) * scale

    def gain(shape):
        return 1.0 + nrm(shape, 0.05)

    return {
        "x": nrm((BATCH, SEQ, D_MODEL), 1.0),
        "ffn1_norm": gain((L, D_MODEL)),
        "ffn1_w_in": nrm((L, D_MODEL, 2 * D_FF), D_MODEL ** -0.5),
        "ffn1_w_out": nrm((L, D_FF, D_MODEL), D_FF ** -0.5),
        "mix_norm": gain((L, D_MODEL)),
        "w_in": nrm((L, D_MODEL, N_IN), D_MODEL ** -0.5),
        "shift_mu": jax.random.uniform(next(ks), (L, N_RW_IN), f32, 0.1, 0.9),
        "rw_w0": jnp.linspace(-6.0, -1.0, D_RWKV, dtype=f32)[None, :] + nrm((L, D_RWKV), 0.1),
        "rw_w_up": nrm((L, LORA_W, D_RWKV), 0.5 * LORA_W ** -0.5),
        "rw_a0": nrm((L, D_RWKV), 0.1),
        "rw_a_up": nrm((L, LORA_A, D_RWKV), 0.5 * LORA_A ** -0.5),
        "rw_g_up": nrm((L, LORA_G, D_RWKV), LORA_G ** -0.5),
        "rw_k_k": 0.85 + nrm((L, D_RWKV), 0.05),
        "rw_k_a": gain((L, D_RWKV)),
        "rw_r_k": nrm((L, RWKV_HEADS, RWKV_HEAD), 0.1),
        "rw_gn_w": gain((L, D_RWKV)),
        "rw_gn_b": nrm((L, D_RWKV), 0.02),
        "vres_down": nrm((L - 1, D_MODEL, LORA_V), D_MODEL ** -0.5),
        "vres_up": nrm((L - 1, LORA_V, D_RWKV), 0.5 * LORA_V ** -0.5),
        "vres_bias": 1.0 + nrm((L - 1, D_RWKV), 0.1),
        "ml_conv_w": nrm((L, CONV_W, 2 * D_MLSTM), CONV_W ** -0.5),
        "ml_conv_b": nrm((L, 2 * D_MLSTM), 0.02),
        "ml_i_bias": nrm((L, MLSTM_HEADS), 0.1),
        "ml_f_bias": jnp.linspace(3.0, 6.0, MLSTM_HEADS, dtype=f32)[None, :] + nrm((L, MLSTM_HEADS), 0.1),
        "ml_norm_w": gain((L, D_MLSTM)),
        "br_a": nrm((L, D_RWKV, D_MODEL), D_RWKV ** -0.5),
        "br_b": nrm((L, D_MLSTM, D_MODEL), D_MLSTM ** -0.5),
        "w_out": nrm((L, D_MODEL, D_MODEL), D_MODEL ** -0.5),
        "ffn2_norm": gain((L, D_MODEL)),
        "ffn2_w_in": nrm((L, D_MODEL, 2 * D_FF), D_MODEL ** -0.5),
        "ffn2_w_out": nrm((L, D_FF, D_MODEL), D_FF ** -0.5),
        "final_norm": gain((D_MODEL,)),
    }

def second_block(x, ffn1_norm, ffn1_w_in, ffn1_w_out, mix_norm, w_in, shift_mu,
              rw_w0, rw_w_up, rw_a0, rw_a_up, rw_g_up, rw_k_k, rw_k_a, rw_r_k, rw_gn_w, rw_gn_b,
              vres_down, vres_up, vres_bias,
              ml_conv_w, ml_conv_b, ml_i_bias, ml_f_bias, ml_norm_w,
              br_a, br_b, w_out, ffn2_norm, ffn2_w_in, ffn2_w_out, final_norm):
    h = x
    v_first = None
    for l in range(DEPTH):
        h = h + HALF * _swiglu(_rmsnorm(h, ffn1_norm[l]), ffn1_w_in[l], ffn1_w_out[l])

        xn = _rmsnorm(h, mix_norm[l])
        z = xn @ w_in[l]
        z_rw = z[..., :N_RW_IN]
        z_ml = z[..., N_RW_IN:N_RW_IN + N_ML_IN]
        z_gate = z[..., N_RW_IN + N_ML_IN:]

        z_rw = z_rw + shift_mu[l] * (_time_shift(z_rw) - z_rw)
        r, k, v, xw, xa, xg = _split_cols(z_rw, RW_SPLITS)
        if l == 0:
            v_first = v
        else:
            vg = jax.nn.sigmoid(vres_bias[l - 1] + (xn @ vres_down[l - 1]) @ vres_up[l - 1])
            v = v + (v_first - v) * vg
        y_a = _rwkv7_mixer(r, k, v, xw, xa, xg, rw_w0[l], rw_w_up[l], rw_a0[l], rw_a_up[l],
                           rw_g_up[l], rw_k_k[l], rw_k_a[l], rw_r_k[l], rw_gn_w[l], rw_gn_b[l])

        mq, mk, mv, mo, mi, mf = _split_cols(z_ml, ML_SPLITS)
        y_b = _mlstm_mixer(mq, mk, mv, mo, mi, mf, ml_conv_w[l], ml_conv_b[l],
                           ml_i_bias[l], ml_f_bias[l], ml_norm_w[l])

        g_a, g_b = jnp.split(z_gate, 2, axis=-1)
        u = jax.nn.sigmoid(g_a) * (y_a @ br_a[l]) + jax.nn.sigmoid(g_b) * (y_b @ br_b[l])
        h = h + u @ w_out[l]

        h = h + HALF * _swiglu(_rmsnorm(h, ffn2_norm[l]), ffn2_w_in[l], ffn2_w_out[l])
    return _rmsnorm(h, final_norm)


def setup_inputs(seed=0):
    out = dict(first_inputs(seed))
    for name, value in second_inputs(seed + 1).items():
        if name != "x":
            out[name + "_2"] = value
    return out


def reference(
    x, c, ctx, c_ctx, w_ada, b_ada, norm_pre_mix, norm_post_mix, norm_pre_ffn, norm_post_ffn,
    w_in, w_out, w_fourier, sink, w_gate, w_up, w_down, ffn1_norm_2, ffn1_w_in_2, ffn1_w_out_2,
    mix_norm_2, w_in_2, shift_mu_2, rw_w0_2, rw_w_up_2, rw_a0_2, rw_a_up_2, rw_g_up_2, rw_k_k_2,
    rw_k_a_2, rw_r_k_2, rw_gn_w_2, rw_gn_b_2, vres_down_2, vres_up_2, vres_bias_2, ml_conv_w_2,
    ml_conv_b_2, ml_i_bias_2, ml_f_bias_2, ml_norm_w_2, br_a_2, br_b_2, w_out_2, ffn2_norm_2,
    ffn2_w_in_2, ffn2_w_out_2, final_norm_2,
):
    x = first_block(
        x, c, ctx, c_ctx, w_ada, b_ada, norm_pre_mix, norm_post_mix, norm_pre_ffn,
        norm_post_ffn, w_in, w_out, w_fourier, sink, w_gate, w_up, w_down,
    )
    return second_block(
        x, ffn1_norm_2, ffn1_w_in_2, ffn1_w_out_2, mix_norm_2, w_in_2, shift_mu_2, rw_w0_2,
        rw_w_up_2, rw_a0_2, rw_a_up_2, rw_g_up_2, rw_k_k_2, rw_k_a_2, rw_r_k_2, rw_gn_w_2,
        rw_gn_b_2, vres_down_2, vres_up_2, vres_bias_2, ml_conv_w_2, ml_conv_b_2, ml_i_bias_2,
        ml_f_bias_2, ml_norm_w_2, br_a_2, br_b_2, w_out_2, ffn2_norm_2, ffn2_w_in_2,
        ffn2_w_out_2, final_norm_2,
    )


_drawn_inputs = setup_inputs


def setup_inputs(seed=0):
    import zlib

    import numpy as np

    out = dict(_drawn_inputs(seed))
    spreads = {}
    factors = {'sink': 8.0,
     'rw_w_up_2': 4.106,
     'rw_a0_2': 3.311,
     'rw_k_k_2': 4.796,
     'rw_k_a_2': 2.863,
     'rw_gn_w_2': 3.502,
     'rw_gn_b_2': 7.171,
     'vres_bias_2': 62.32,
     'ml_conv_b_2': 8.0,
     'ml_i_bias_2': 64.0,
     'ml_norm_w_2': 3.248,
     'vres_down_2': 8.0,
     'vres_up_2': 8.0,
     'ffn2_norm_2': 3.263}
    for name, (base, spread) in spreads.items():
        noise = np.random.default_rng([zlib.crc32(name.encode()), seed]).standard_normal(out[name].shape)
        drawn = base * np.exp(spread * noise) if base else spread * noise
        out[name] = __import__('jax').numpy.asarray(drawn.astype(out[name].dtype))
    for name, factor in factors.items():
        out[name] = (out[name] * factor).astype(out[name].dtype)
    return out
```

```python
from contextlib import ExitStack

import numpy as np

import concourse.bass as bass
from concourse import mybir

F32 = mybir.dt.float32
ALU = mybir.AluOpType
ACT = mybir.ActivationFunctionType
AX_X = mybir.AxisListType.X

P = 128
D = 1024
T = 256
KD = D // P
LAYERS = 2
FFN = 2816
FT = FFN // P
NMOD = 6 * KD
HD = 64
QT = 4
CHUNK = 64
NC_ = T // CHUNK
UNITS = QT * NC_
RMS_EPS, GN_EPS, ML_EPS = 1e-6, 64e-5, 1e-5

R0, K0, V0, XWA, XG, MISC, MQ, MK, MO, GA, GB, MV = 0, 4, 8, 12, 13, 14, 15, 19, 23, 27, 35, 43
ZT = MV
MIXED = MISC + 1
XG2, IROW, FROW, VROW = 0, 32, 64, 96

A_ADA = 0
A_B1 = [LAYERS * NMOD // 2]
PROJ1, OUT1 = 5, 4
B1_LAYER = PROJ1 + OUT1 + FT
A_B1.append(A_B1[0] + B1_LAYER)
PROJ2, BR2, OUT2 = 24, 4, 4
B2_LAYER = FT + PROJ2 + BR2 + OUT2 + FT
A_B2 = [A_B1[1] + B1_LAYER, A_B1[1] + B1_LAYER + B2_LAYER]
N_A = A_B2[1] + B2_LAYER


WORK = 33200


def spans(widths):
    at, out = 0, {}
    for name, w in widths:
        out[name] = (at, at + w)
        at += w
    return out, at


C1, C1_N = spans([("cos", T), ("sin", T), ("rot", P), ("dft", 2 * 2 * T), ("chc", P), ("chs", P),
                  ("win", 2 * 2 * T)])
LEVELS = [2, 4, 8, 16, 32]
C2, C2_N = spans([("ident", P), ("ones", P), ("headones", P), ("headsum", QT * 8), ("headrow", QT * P),
                  ("restart", T), ("strict", CHUNK), ("incl", CHUNK), ("low1", CHUNK), ("up1", CHUNK),
                  ("eye", CHUNK)] + [(f"lev{m}", CHUNK) for m in LEVELS]
                 + [("tri", T + P), ("seli", 4), ("self", 4),
                    ("eps_rms", 1), ("eps_gn", 1), ("eps_ml", 1), ("one", 1)])
V, V_N = spans([("c", 2 * KD), ("b_ada", LAYERS * NMOD)]
               + [(f"{n}{l}", KD) for n in ("pre_mix", "post_mix", "pre_ffn", "post_ffn", "ffn1", "mix", "ffn2",
                                            "conv_b", "tap0", "tap1", "tap2", "tap3") for l in range(LAYERS)]
               + [("final", KD)]
               + [(f"mu{l}", MIXED) for l in range(LAYERS)]
               + [(f"{n}{l}", QT) for n in ("w0", "a0", "k_k", "k_a", "r_k", "gn_w", "gn_b", "ml_w")
                  for l in range(LAYERS)]
               + [("vbias1", QT)] + [(f"{n}{l}", 1) for n in ("ib", "fb") for l in range(LAYERS)]
               + [("sink", LAYERS * 8)])
SM, SM_N = spans([("waup", 512), ("gup", 512), ("mup", 512)])


def constants():
    pos = np.arange(T)
    rows = T // 64
    row = np.repeat(np.arange(rows), 64).astype(np.float32)
    col = np.tile(np.arange(64), rows).astype(np.float32)
    freqs = (np.float32(10000.0) ** (-np.arange(16, dtype=np.float32) / np.float32(16))).astype(np.float32)
    ang = np.concatenate([row[:, None] * freqs, col[:, None] * freqs], axis=-1)
    pair = (np.arange(P) % HD) // 2
    rot = np.zeros((P, P))
    even = np.arange(0, P, 2)
    rot[even + 1, even] = -1.0
    rot[even, even + 1] = 1.0
    turn = 2 * np.pi * np.outer(pos, pos) % (2 * np.pi * T) / T
    dft = np.concatenate([np.cos(turn), np.sin(turn)], 1).reshape(2, P, 2 * T).transpose(1, 0, 2).reshape(P, -1)
    ch = 2 * np.pi * (np.outer(np.arange(HD), np.arange(HD)) % HD) / HD
    norm = 1.0 / np.sqrt(T * HD)
    two = np.kron(np.eye(2), np.ones((HD, HD)))
    chc, chs = (np.kron(np.eye(2), f(ch) * norm) for f in (np.cos, np.sin))
    win = np.zeros((P, 2, 2 * T))
    for b in range(2):
        q = b * P + np.arange(P)
        win[:, b, :T] = np.where(np.abs(q[:, None] - pos[None]) <= 128, 0.0, -1e30)
    c1 = dict(cos=np.cos(ang).T[pair], sin=np.sin(ang).T[pair], rot=rot, dft=dft, chc=chc, chs=-chs,
              win=win.reshape(P, -1))
    s = (np.arange(P) % CHUNK)[:, None]
    t = np.arange(CHUNK)[None]
    tall = lambda m: np.broadcast_to(m, (P, CHUNK)).astype(np.float32)
    block = lambda m: tall((s // (2 * m) == t // (2 * m)) & (s // m % 2 == 0) & (t // m % 2 == 1))
    headsum = np.zeros((P, QT, 8))
    headrow = np.zeros((P, QT, P))
    for j in range(QT):
        for h in range(2):
            headsum[h * HD:(h + 1) * HD, j, 2 * j + h] = 1.0
            headrow[2 * j + h, j, h * HD:(h + 1) * HD] = 1.0
    tri = np.zeros((P, T + P))
    later = np.where(np.arange(P)[:, None] <= np.arange(P)[None], 0.0, -1e30)
    tri[:, :P] = later
    tri[:, T:] = later
    seli, self_ = np.zeros((P, 4)), np.zeros((P, 4))
    for h in range(4):
        seli[IROW + h, h] = 1.0
        self_[FROW + h, h] = 1.0
    c2 = dict(ident=np.eye(P), ones=np.ones((P, P)), headones=two, headsum=headsum.reshape(P, -1),
              headrow=headrow.reshape(P, -1),
              restart=np.broadcast_to((pos % CHUNK != 0).astype(np.float32), (P, T)),
              strict=tall(s < t), incl=tall(s <= t), low1=tall((s == t + 1) & (t % 2 == 0)), up1=block(1),
              eye=tall(s == t), tri=tri, seli=seli,
              eps_rms=np.full((P, 1), RMS_EPS), eps_gn=np.full((P, 1), GN_EPS), eps_ml=np.full((P, 1), ML_EPS),
              one=np.ones((P, 1)), **{f"lev{m}": block(m) for m in LEVELS}, **{"self": self_})
    side = lambda part, where: np.concatenate([part[n] for n in where], 1).astype(np.float32)
    return side(c1, C1), side(c2, C2)


class Steps:

    def __init__(self, names):
        self.place = {n: i + 1 for i, n in enumerate(names)}
        self.count = len(names)

    def at(self, name, rnd):
        return rnd * self.count + self.place[name]


def program(nc, wa, wd, c1_in, c2_in, vec_in, small_in, four_in, x_in, ctx_in, out):
    with ExitStack() as ctx:
        def sb(name, *shape):
            return ctx.enter_context(nc.sbuf_tensor(name, [P, *shape], F32))

        def sem(name):
            return ctx.enter_context(nc.semaphore(name))

        ring_a = sb("ring_a", 2, 2, KD, P)
        ring_d = sb("ring_d", 2, KD, P)
        x = sb("x", KD, T)
        hn = sb("hn", KD, T)
        nsq = sb("nsq", KD, T)
        nrt = sb("nrt", T)
        rstd = sb("rstd", T)
        sg = sb("sg", 2, T)
        hid = sb("hid", 2, T)
        c2 = sb("c2", C2_N)
        vec = sb("vec", V_N)
        mod = sb("mod", LAYERS * NMOD, 2)
        gain = sb("gain", LAYERS, 4, KD, 2)
        cs = sb("cs", KD, 2)
        omka = sb("omka", LAYERS * QT)
        vfirst = sb("vfirst", QT, T)
        work = sb("work", WORK)
        ps = ctx.enter_context(nc.psum_tensor("ps", [P, 8, 512], F32))

        def const(name):
            return c2[:, C2[name][0]:C2[name][1]]

        def vcol(name, k):
            return vec[:, V[name][0] + k:V[name][0] + k + 1]

        top = [0]

        def place(*shape):
            n = int(np.prod(shape))
            v = work[:, top[0]:top[0] + n]
            top[0] += n
            assert top[0] <= WORK, top[0]
            if len(shape) == 1:
                return v
            if len(shape) == 2:
                return v.rearrange("p (a b) -> p a b", b=shape[1])
            return v.rearrange("p (a b c) -> p a b c", b=shape[1], c=shape[2])

        def units(v):
            return v.rearrange("p j (c t) -> p (j c) t", t=CHUNK)

        xc = place(KD, T)
        h2 = place(KD, 2 * T)
        shared = top[0]
        raw = place(5, 2 * T)
        u_tok = place(4, 512)
        top[0] = max(top[0], shared + KD * 2 * T)
        mix = work[:, shared:shared + KD * 2 * T].rearrange("p (a b) -> p a b", b=2 * T)
        rtmp = place(5, T)
        qr = place(QT, T)
        kall = place(2 * T)
        v_tok = place(4, P)
        s_sb = place(2, 2 * T)
        probs = place(2, 2 * T)
        pn = place(2, 2 * T)
        pt = place(2, 4, P)
        tiny = place(2, 8)
        fu = place(QT, 2 * T)
        fm = place(QT, T)
        mixin = place(KD, 2 * T)
        c1 = place(C1_N)
        wfour = place(LAYERS * QT, P)

        def const1(name):
            return c1[:, C1[name][0]:C1[name][1]]

        top[0] = 0
        z = place(ZT, T + 1)
        mv = place(2, 512)
        small = place(SM_N)
        S_ = [place(QT, T) for _ in range(12)]
        lw, aa, vg, gg, bon, lcum, e1, e2, e0, kk, bb, tmp = S_
        slot0 = top[0]
        diff = work[:, slot0:slot0 + 15 * T].rearrange("p (a b) -> p a b", b=T)
        at_, mt, mrt, art, ws, aoff = (place(QT, T) for _ in range(6))
        state = place(2, QT, HD)
        sdec = place(QT, HD)
        kt, bh, kh, khc, bhc = kk, bb, e0, lw, aa
        khc_t, bhc_t, v_t = vg, lcum, e2
        xs, xt = tmp, khc
        rr, nu, yy, yq = ws, aoff, at_, xs
        small_y = place(8, UNITS)
        am = work[:, slot0:slot0 + 2 * 384].rearrange("p (a b) -> p a b", b=384)
        ee = work[:, slot0 + 768:slot0 + 2 * 768].rearrange("p (a b) -> p a b", b=384)
        pm = work[:, slot0 + 1536:slot0 + 3 * 768].rearrange("p (a b) -> p a b", b=384)
        dn = work[:, slot0 + 2304:slot0 + 2304 + 512].rearrange("p (a b) -> p a b", b=T)
        ems = work[:, slot0 + 2816:slot0 + 2816 + 512].rearrange("p (a b) -> p a b", b=T)
        hN = work[:, slot0 + 3328:slot0 + 3328 + 1024].rearrange("p (a b) -> p a b", b=T)
        hc = work[:, slot0 + 4352:slot0 + 4352 + 1024].rearrange("p (a b) -> p a b", b=T)
        rows4 = z[:, MQ:MQ + 2 * QT, 1:T + 1]
        ya, yb = gg, bhc
        inv_norm = rows4[0:8, 0, :]
        umix = nsq

        a_loaded = [sem("a_loaded0"), sem("a_loaded1")]
        d_loaded = [sem("d_loaded0"), sem("d_loaded1")]
        a_used, d_used = sem("a_used"), sem("d_used")
        in_loaded, const_loaded, small_loaded, out_stored = (
            sem(n) for n in ("in_loaded", "const_loaded", "small_loaded", "out_stored"))
        cs_ready, ada_free, gain_ready = (sem(n) for n in ("cs_ready", "ada_free", "gain_ready"))
        norm_sq, norm_sum, norm_rt, norm_rstd, norm_scaled, norm_out = (
            sem(n) for n in ("norm_sq", "norm_sum", "norm_rt", "norm_rstd", "norm_scaled", "norm_out"))
        proj_ready, proj_free = sem("proj_ready"), sem("proj_free")
        sg_ready, hid_ready, ffn_out = sem("sg_ready"), sem("hid_ready"), sem("ffn_out")
        resid = sem("resid")
        rope_rot, rope_sin, rope_cos, rope_out = (sem(n) for n in ("rope_rot", "rope_sin", "rope_cos", "rope_out"))
        fo_dft, fo_fu, fo_ch, fo_fm, fo_w, fo_out = (
            sem(n) for n in ("fo_dft", "fo_fu", "fo_ch", "fo_fm", "fo_w", "fo_out"))
        at_sc, at_s, at_mx, at_nm, at_exp, at_den, at_rd, at_pn, at_tr, at_pt, at_pv, at_o = (
            sem(f"at_{n}") for n in ("sc", "s", "mx", "nm", "exp", "den", "rd", "pn", "tr", "pt", "pv", "o"))
        z_zero, kab = sem("z_zero"), sem("kab")
        rw_v, rw_a, rw_p, vres_v, vres_a, vres_p, lev_v, lev_a, lev_p, lev_g, ch_v, ch_a, ch_p = (
            sem(n) for n in ("rw_v", "rw_a", "rw_p", "vres_v", "vres_a", "vres_p", "lev_v", "lev_a", "lev_p", "lev_g",
                             "ch_v", "ch_a", "ch_p"))
        ml_v, ml_a, ml_p = (sem(n) for n in ("ml_v", "ml_a", "ml_p"))
        mh_arg, mh_s, mh_em, mh_nd, mh_am, mh_pm, mh_ee, mh_ems, mh_dn, mh_abs, mh_rc, mh_h = (
            sem(f"mh_{n}") for n in ("arg", "s", "em", "nd", "am", "pm", "ee", "ems", "dn", "abs", "rc", "h"))
        br_ready, br_part, br_free = (sem(n) for n in ("br_ready", "br_part", "br_free"))

        RV = Steps(["diff", "mix", "lw", "scan", "kk", "kq", "rnmax", "rn", "kkn", "b", "ka", "kp", "rkr", "bon", "l0",
                    "kt", "bh", "kh", "rt", "khc", "bhc", "at", "x1", "xt1", "mt", "x", "xt",
                    "mrt", "art", "s1", "ym", "yc", "yq", "s2", "yr", "yn", "gn", "gb", "ya"])
        RA = Steps(["tanh", "sgx", "sw", "aa", "gg", "rsq", "e0", "e1", "e2", "vt", "khct", "bhct", "ysd", "yT"])
        RP = Steps(["lw", "la", "lg", "ss", "rnb", "bon", "vt", "khct", "bhct", "at", "a", "mt", "mrt", "art", "yT"])
        VV = Steps(["d", "m", "v"])
        LP = Steps(["w0", "w1", "x0", "x1"])
        LV = Steps(["x0", "xt0", "x1", "xt1"])
        LA = Steps(["w0", "w1"])
        CP = Steps(["r", "u", "s", "y"])
        CV = Steps(["dec", "nu", "s"])
        MVS = Steps(["c0", "c1", "c2", "c3", "mn", "lf", "F", "g", "M", "nm", "fm", "hc", "rec", "hs", "yb"])
        MA = Steps(["silu", "so", "ab", "ex", "ln", "hq", "hsd", "gates"])
        MP = Steps(["if", "mu", "var"])

        n_id = {}
        order = []
        for l in range(LAYERS):
            order += [("pre_mix", l, 0), ("pre_mix", l, 1)]
            order += [("post_mix", l, 0), ("pre_ffn", l, 0), ("post_ffn", l, 0)]
            if l == 0:
                order += [("post_mix", l, 1), ("pre_ffn", l, 1), ("post_ffn", l, 1)]
        for l in range(LAYERS):
            order += [("ffn1", l, 0), ("mix", l, 0), ("ffn2", l, 0)]
        order.append(("final", 0, 0))
        two_step = {"pre_mix", "post_mix", "pre_ffn", "post_ffn"}
        n_two = {}
        for i, key in enumerate(order):
            n_id[key] = i
            n_two[key] = len(n_two)
        ffns = [(0, 0), (0, 1), (1, 0)] + [(2, 0), (3, 0), (4, 0), (5, 0)]
        a_dram_ffn = [A_B1[0] + PROJ1 + OUT1, A_B1[1] + PROJ1 + OUT1,
                      A_B2[0], A_B2[0] + FT + PROJ2 + BR2 + OUT2, A_B2[1], A_B2[1] + FT + PROJ2 + BR2 + OUT2]
        stages = [("ada", A_ADA, LAYERS * NMOD // 2, None)]
        for l in range(LAYERS):
            stages += [(f"proj1{l}", A_B1[l], PROJ1, None), (f"out1{l}", A_B1[l] + PROJ1, OUT1, None)]
            for call in ([0, 1] if l == 0 else [2]):
                stages.append((f"ffn{call}", a_dram_ffn[ffns[call][0]], FT, call))
        for l in range(LAYERS):
            base = A_B2[l] + FT
            stages += [(f"ffn{3 + 2 * l}", A_B2[l], FT, 3 + 2 * l),
                       (f"proj2{l}", base, PROJ2, None), (f"br{l}", base + PROJ2, BR2, None),
                       (f"out2{l}", base + PROJ2 + BR2, OUT2, None),
                       (f"ffn{4 + 2 * l}", base + PROJ2 + BR2 + OUT2, FT, 4 + 2 * l)]
        chunk0, n = {}, 0
        for name, _, count, _ in stages:
            chunk0[name] = n
            n += count
        tile0, first0, n, m = {}, {}, 0, 0
        for name, count in ([(f"{s}1{l}", t) for l in range(LAYERS) for s, t in (("proj", 10), ("out", KD))]
                            + [(f"proj2{l}", ZT + QT) for l in range(LAYERS)]):
            tile0[name], first0[name] = n, m
            n += count
            m += count // 2

        def token_cols(l, which):
            return slice(which * T, which * T + T)

        block = ctx.enter_context(nc.Block())

        @block.sync
        def _(sp):
            sp.dma_start(x[:, :, :], x_in).then_inc(in_loaded, 16)
            sp.dma_start(xc, ctx_in).then_inc(in_loaded, 16)

            def load_a(c, slot, src, wait=True):
                if wait:
                    sp.wait_ge(a_used, c - 1)
                sp.dma_start(ring_a[:, slot].rearrange("p a b c -> p (a b c)"), src).then_inc(a_loaded[slot], 16)

            def load_d(d, slot, src, wait=True):
                if wait:
                    sp.wait_ge(d_used, d - 1)
                sp.dma_start(ring_d[:, slot].rearrange("p a b -> p (a b)"), src).then_inc(d_loaded[slot], 16)

            for name, first, count, call in stages:
                c0 = chunk0[name]
                if call is None:
                    i = 0
                    if c0 == 0:
                        load_a(0, 0, wa[first], wait=False)
                        load_a(1, 1, wa[first + 1], wait=False)
                        i = 2
                    pairs = (count - i) // 2
                    if pairs:
                        with sp.Fori(0, pairs) as n:
                            for u in range(2):
                                load_a(n * 2 + (c0 + i + u), (c0 + i + u) % 2,
                                       wa[bass.ds(n * 2 + (first + i + u), 1)].rearrange("a p n -> (a p) n"))
                    if (count - i) % 2:
                        load_a(c0 + count - 1, (c0 + count - 1) % 2, wa[first + count - 1])
                    continue
                d0, dd = call * FT, ffns[call][0] * FT
                load_a(c0, c0 % 2, wa[first])
                load_a(c0 + 1, (c0 + 1) % 2, wa[first + 1])
                load_d(d0, d0 % 2, wd[dd], wait=call > 0)
                load_a(c0 + 2, c0 % 2, wa[first + 2])
                load_d(d0 + 1, (d0 + 1) % 2, wd[dd + 1], wait=call > 0)
                with sp.Fori(0, (FT - 4) // 2) as n:
                    for u in range(2):
                        load_a(n * 2 + (c0 + 3 + u), (c0 + 3 + u) % 2,
                               wa[bass.ds(n * 2 + (first + 3 + u), 1)].rearrange("a p n -> (a p) n"))
                        load_d(n * 2 + (d0 + 2 + u), (d0 + 2 + u) % 2,
                               wd[bass.ds(n * 2 + (dd + 2 + u), 1)].rearrange("a p n -> (a p) n"))
                load_a(c0 + FT - 1, (c0 + FT - 1) % 2, wa[first + FT - 1])
                for f in (FT - 2, FT - 1):
                    load_d(d0 + f, (d0 + f) % 2, wd[dd + f])
            sp.wait_ge(norm_out, n_id[("final", 0, 0)] + 1)
            sp.dma_start(out, hn[:, :, :]).then_inc(out_stored, 16)
            sp.wait_ge(out_stored, 16)

        @block.gpsimd
        def _(pool):
            pool.wait_ge(norm_out, n_id[("post_ffn", 1, 0)] + 1)
            pool.wait_ge(fo_out, 3 * QT)
            nc.gpsimd.memset(z[:, :, 0:1], 0.0).then_inc(z_zero, 1)
            for l in range(LAYERS):
                if l:
                    pool.wait_ge(rw_p, RP.at("lg", l - 1))
                pool.dma_start(small, small_in[l]).then_inc(small_loaded, 16)
                for i, m in enumerate(LEVELS):
                    step = l * len(LEVELS) + i
                    if step:
                        pool.wait_ge(lev_p, LP.at("w1", step - 1))
                    if i == 0:
                        pool.wait_ge(rw_v, RV.at("art", l))
                    nc.gpsimd.tensor_tensor(
                        units(aoff), units(at_), const(f"lev{m}")[:, None, :].to_broadcast([P, UNITS, CHUNK]),
                        ALU.mult).then_inc(lev_g, 1)

        @block.scalar
        def _(act):
            act.dma_start(c2[:, :], c2_in).then_inc(const_loaded, 16)
            act.dma_start(vec[:, :], vec_in).then_inc(const_loaded, 16)
            act.dma_start(c1, c1_in).then_inc(const_loaded, 16)
            act.dma_start(wfour.rearrange("p a b -> p (a b)"), four_in).then_inc(const_loaded, 16)
            act.wait_ge(const_loaded, 64)
            nc.scalar.activation(cs[:, :, :].rearrange("p k w -> p (k w)"),
                                 vec[:, V["c"][0]:V["c"][1]], ACT.Silu).then_inc(cs_ready, 1)

            def norm(key, src):
                n = n_id[key]
                nc.scalar.activation(nsq[:, :, :], src, ACT.Square).then_inc(norm_sq, 1)
                act.wait_ge(norm_sum, n + 1)
                if n:
                    act.wait_ge(norm_rstd, n)
                nc.scalar.activation(nrt[:, :], ps[:, 6, 0:T], ACT.Sqrt, bias=const("eps_rms"),
                                     scale=1.0 / D).then_inc(norm_rt, 1)

            def ffn(call):
                with act.Fori(0, FT // 2) as i:
                    for u in range(2):
                        f0 = chunk0[f"ffn{call}"] + u
                        act.wait_ge(a_used, i * 2 + (f0 + 1))
                        if call or u > 1:
                            act.wait_ge(hid_ready, i * 2 + (call * FT + u - 1))
                        nc.scalar.activation(sg[:, u, :], ps[:, 4 + u, 0:T], ACT.Silu).then_inc(sg_ready, 1)

            def ffn_first():
                for u in range(2):
                    act.wait_ge(a_used, chunk0["ffn0"] + u + 1)
                    nc.scalar.activation(sg[:, u, :], ps[:, 4 + u, 0:T], ACT.Silu).then_inc(sg_ready, 1)
                with act.Fori(1, FT // 2) as i:
                    for u in range(2):
                        act.wait_ge(a_used, i * 2 + (chunk0["ffn0"] + u + 1))
                        act.wait_ge(hid_ready, i * 2 + (u - 1))
                        nc.scalar.activation(sg[:, u, :], ps[:, 4 + u, 0:T], ACT.Silu).then_inc(sg_ready, 1)

            def tile_ready(stage, i):
                if i % 2 or i == ZT + QT - 1:
                    act.wait_ge(a_used, chunk0[stage] + i // 2 + 1)
                else:
                    act.wait_ge(proj_ready, first0[stage] + i // 2 + 1)

            def empty(stage, i, dst, cols=slice(0, T)):
                tile_ready(stage, i)
                src = ps[:, 4 + (tile0[stage] + i) % 2, cols]
                if len(dst.shape) == 3:
                    src = src.rearrange("p (a b) -> p a b", b=P)
                nc.scalar.copy(dst, src).then_inc(proj_free, 1)

            def fourier(call, l, which):
                for j in range(QT):
                    act.wait_ge(fo_dft, call * QT + j + 1)
                    nc.scalar.copy(fu[:, j, :], ps[:, j, :]).then_inc(fo_fu, 1)
                for j in range(QT):
                    act.wait_ge(fo_ch, call * QT + j + 1)
                    nc.scalar.copy(fm[:, j, :], ps[:, j, 0:T]).then_inc(fo_fm, 1)
                for j in range(QT):
                    act.wait_ge(fo_w, call * QT + j + 1)
                    nc.scalar.copy(mixin[:, QT + j, token_cols(l, which)], ps[:, j, T:2 * T]).then_inc(fo_out, 1)

            def attention(call, l, which):
                n_keys = 2 * T if which == 0 else T

                def exps(u):
                    g, h = call * 16 + u, (u % 2) * 4 + (u // 2) % 4
                    act.wait_ge(at_nm, g + 1)
                    if g >= 2:
                        act.wait_ge(at_pn, g - 1)
                    nc.scalar.activation(probs[:, u % 2, 0:n_keys], s_sb[:, u % 2, 0:n_keys], ACT.Exp,
                                         bias=tiny[:, u % 2, 1:2], accum_out=tiny[:, u % 2, 2:3])
                    nc.scalar.activation(tiny[:, u % 2, 3:4], vcol("sink", l * 8 + h), ACT.Exp,
                                         bias=tiny[:, u % 2, 1:2]).then_inc(at_exp, 1)

                def turned(u):
                    g = call * 16 + u
                    act.wait_ge(at_tr, g + 1)
                    if g >= 2:
                        act.wait_ge(at_pv, g - 1)
                    nc.scalar.copy(pt[:, u % 2, 0:n_keys // P, :],
                                   ps[:, 2 + u % 2, 0:n_keys].rearrange("p (a b) -> p a b", b=P)).then_inc(at_pt, 1)

                def out_pair(w):
                    blk, j = w // 4, w % 4
                    act.wait_ge(at_pv, call * 16 + 2 * w + 2)
                    nc.scalar.copy(mixin[:, j, which * T + blk * P:which * T + (blk + 1) * P],
                                   ps[:, 6 + w % 2, 0:P]).then_inc(at_o, 1)

                for u in range(16 + 4):
                    if u < 16:
                        exps(u)
                    if 1 <= u <= 16:
                        turned(u - 1)
                    if u >= 4 and (u - 3) % 2:
                        out_pair((u - 4) // 2)

            act.wait_ge(in_loaded, 32)
            fcall = acall = 0
            for l in range(LAYERS):
                if l:
                    act.wait_ge(norm_out, n_id[("post_ffn", 0, 0)] + 1)
                norm(("pre_mix", l, 0), x[:, :, :])
                if l:
                    act.wait_ge(norm_out, n_id[("post_ffn", 0, 1)] + 1)
                norm(("pre_mix", l, 1), xc)
                stage, n_q, n_blk = f"proj1{l}", (2 * T, T)[l], (4, 2)[l]
                tile_ready(stage, 0)
                bank = 4 + tile0[stage] % 2
                nc.scalar.copy(raw[:, 0, 0:T], ps[:, bank, 0:T])
                nc.scalar.copy(kall[:, T:2 * T], ps[:, bank, T:2 * T]).then_inc(proj_free, 1)
                for j in range(QT):
                    empty(stage, 1 + j, raw[:, 1 + j, 0:n_q], slice(0, n_q))
                empty(stage, 1 + QT, v_tok, slice(0, 2 * T))
                for j in range(QT):
                    empty(stage, 2 + QT + j, u_tok[:, 0:n_blk, j * P:(j + 1) * P], slice(0, n_blk * P))
                for which in ([0, 1] if l == 0 else [0]):
                    fourier(fcall, l, which)
                    attention(acall, l, which)
                    fcall += 1
                    acall += 1
                for j in range(KD):
                    empty(f"out1{l}", j, mix[:, j, 0:n_q], slice(0, n_q))
                for which in ([0, 1] if l == 0 else [0]):
                    act.wait_ge(proj_free, tile0[f"out1{l}"] + KD)
                    norm(("post_mix", l, which), mix[:, :, token_cols(l, which)])
                    act.wait_ge(norm_out, n_id[("post_mix", l, which)] + 1)
                    norm(("pre_ffn", l, which), x[:, :, :] if which == 0 else xc)
                    call = 2 * l + which
                    if call == 0:
                        ffn_first()
                    else:
                        ffn(call)
                    act.wait_ge(d_used, (call + 1) * FT)
                    nc.scalar.copy(mix[:, :, token_cols(l, which)],
                                   ps[:, 0:4, :].rearrange("p a (b t) -> p (a b) t", t=T)).then_inc(ffn_out, 1)
                    act.wait_ge(ffn_out, call + 1)
                    norm(("post_ffn", l, which), mix[:, :, token_cols(l, which)])

            for l in range(LAYERS):
                if l == 0:
                    act.wait_ge(norm_out, n_id[("post_ffn", 1, 0)] + 1)
                else:
                    act.wait_ge(resid, 3 * l)
                norm(("ffn1", l, 0), x[:, :, :])
                ffn(3 + 2 * l)
                act.wait_ge(resid, 3 * l + 1)
                norm(("mix", l, 0), x[:, :, :])

                stage = f"proj2{l}"
                p0, c0, f0 = tile0[stage], chunk0[stage], first0[stage]
                if l == 0:
                    act.wait_ge(z_zero, 1)
                else:
                    act.wait_ge(br_free, KD * l)

                def tiles(first, count):
                    with act.Fori(0, count // 2) as i:
                        for u in range(2):
                            if u == 0:
                                act.wait_ge(proj_ready, i + (f0 + first // 2 + 1))
                            else:
                                act.wait_ge(a_used, i + (c0 + first // 2 + 1))
                            nc.scalar.activation(
                                z[:, bass.ds(i * 2 + (first + u), 1), 1:T + 1],
                                ps[:, 4 + (p0 + first + u) % 2, 0:T].rearrange("p (a b) -> p a b", a=1),
                                ACT.Copy).then_inc(proj_free, 1)

                tiles(0, 24)
                act.wait_ge(rw_v, RV.at("mix", l))
                nc.scalar.activation(tmp[0:64, 0, :], z[0:64, XWA, 1:T + 1], ACT.Tanh).then_inc(rw_a, 1)
                nc.scalar.activation(tmp[:, 1, :], z[:, XG, 1:T + 1], ACT.Sigmoid)
                nc.scalar.activation(tmp[0:32, 2, :], z[0:32, MISC, 1:T + 1], ACT.Sigmoid).then_inc(rw_a, 1)
                tiles(24, 8)
                act.wait_ge(rw_p, RP.at("lw", l))
                for j in range(QT):
                    ins = nc.scalar.activation(lw[:, j, :], ps[:, j // 2, j % 2 * T:j % 2 * T + T], ACT.Sigmoid,
                                               bias=vcol(f"w0{l}", j))
                ins.then_inc(rw_a, 1)
                act.wait_ge(rw_p, RP.at("la", l))
                for j in range(QT):
                    ins = nc.scalar.activation(aa[:, j, :], ps[:, 2 + j // 2, j % 2 * T:j % 2 * T + T], ACT.Sigmoid,
                                               bias=vcol(f"a0{l}", j))
                ins.then_inc(rw_a, 1)
                act.wait_ge(rw_p, RP.at("lg", l))
                nc.scalar.copy(gg, ps[:, 6:8, :].rearrange("p a (b t) -> p (a b) t", t=T)).then_inc(rw_a, 1)
                tiles(32, 4)
                if l:
                    act.wait_ge(vres_p, 1)
                    for j in range(QT):
                        ins = nc.scalar.activation(vg[:, j, :], ps[:, j // 2, j % 2 * T:j % 2 * T + T], ACT.Sigmoid,
                                                   bias=vcol("vbias1", j))
                    ins.then_inc(vres_a, 1)
                act.wait_ge(rw_p, RP.at("ss", l))
                nc.scalar.activation(tmp[0:8, 3, :], ps[0:8, 2, 0:T], ACT.Sqrt).then_inc(rw_a, 1)
                tiles(36, 6)
                empty(stage, ZT - 1, z[:, ZT - 1, 1:T + 1])
                for j in range(QT):
                    empty(stage, ZT + j, mv[:, :, j * P:(j + 1) * P])
                act.wait_ge(rw_v, RV.at("l0", l))
                nc.scalar.activation(e0, e0, ACT.Exp).then_inc(rw_a, 1)
                nc.scalar.activation(e1, lcum, ACT.Exp).then_inc(rw_a, 1)
                nc.scalar.activation(e2, lcum, ACT.Exp, scale=-1.0).then_inc(rw_a, 1)

                def to_tokens(dst, banks):
                    src = ps[:, banks:banks + 2, :].rearrange("p b (u c) -> p (b u) c", c=P)
                    d = units(dst).rearrange("p (u o) c -> p u o c", o=2)
                    for odd in range(2):
                        for h in range(2):
                            ins = nc.scalar.copy(d[h * 64:h * 64 + 64, :, odd, :],
                                                 src[odd * 64:odd * 64 + 64, :, h * 64:h * 64 + 64])
                    return ins

                act.wait_ge(ml_v, MVS.at("c3", l))
                nc.scalar.activation(nsq[:, :, :], nsq[:, :, :], ACT.Silu).then_inc(ml_a, 1)
                nc.scalar.activation(z[:, MO:MO + QT, 1:T + 1], z[:, MO:MO + QT, 1:T + 1], ACT.Sigmoid)\
                    .then_inc(ml_a, 1)
                act.wait_ge(rw_p, RP.at("vt", l))
                act.wait_ge(rw_v, RV.at("kh", l))
                to_tokens(v_t, 2).then_inc(rw_a, 1)
                act.wait_ge(ml_p, MP.at("if", l))
                nc.scalar.activation(rows4[0:4, 0, :], ps[0:4, 6, T:2 * T], ACT.Abs, bias=vcol(f"fb{l}", 0)[0:4])\
                    .then_inc(ml_a, 1)
                act.wait_ge(ml_a, MA.at("ab", l))
                nc.scalar.activation(rows4[0:4, 1, :], rows4[0:4, 0, :], ACT.Exp, scale=-1.0).then_inc(ml_a, 1)
                act.wait_ge(ml_a, MA.at("ex", l))
                nc.scalar.activation(rows4[0:4, 2, :], rows4[0:4, 1, :], ACT.Ln, bias=const("one")[0:4])\
                    .then_inc(ml_a, 1)
                act.wait_ge(rw_p, RP.at("khct", l))
                to_tokens(khc_t, 0).then_inc(rw_a, 1)
                act.wait_ge(rw_p, RP.at("bhct", l))
                to_tokens(bhc_t, 4).then_inc(rw_a, 1)
                for h in range(4):
                    r = l * 4 + h
                    act.wait_ge(mh_am, r + 1)
                    if r >= 2:
                        act.wait_ge(mh_pm, r - 1)
                    nc.scalar.activation(ee[:, h % 2, :], am[:, h % 2, :], ACT.Exp).then_inc(mh_ee, 1)
                    act.wait_ge(mh_em, r + 1)
                    if r >= 2:
                        act.wait_ge(mh_dn, r - 1)
                    nc.scalar.activation(ems[:, h % 2, :], ps[:, 4 + h % 2, 0:T], ACT.Exp, scale=-1.0)\
                        .then_inc(mh_ems, 1)
                act.wait_ge(ml_v, MVS.at("hc", l))
                nc.scalar.activation(hN, hc, ACT.Square).then_inc(ml_a, 1)
                act.wait_ge(ml_p, MP.at("var", l))
                nc.scalar.activation(yb, ps[:, 2:4, :].rearrange("p a (b t) -> p (a b) t", t=T), ACT.Sqrt,
                                     bias=const("eps_ml"), scale=1.0 / P).then_inc(ml_a, 1)
                nc.scalar.activation(z[:, GA:GA + 2 * KD, 1:T + 1], z[:, GA:GA + 2 * KD, 1:T + 1], ACT.Sigmoid)\
                    .then_inc(ml_a, 1)
                for i in range(len(LEVELS)):
                    step = l * len(LEVELS) + i
                    for half in range(2):
                        act.wait_ge(lev_p, LP.at(f"w{half}", step))
                        nc.scalar.copy(units(ws)[:, half * 8:half * 8 + 8, :],
                                       ps[:, half, :].rearrange("p (u t) -> p u t", t=CHUNK)).then_inc(lev_a, 1)
                for c in range(NC_):
                    step = l * NC_ + c
                    act.wait_ge(ch_p, CP.at("r", step))
                    nc.scalar.copy(rr[:, :, c * CHUNK:(c + 1) * CHUNK],
                                   ps[:, 0, 0:QT * HD].rearrange("p (j v) -> p j v", v=HD)).then_inc(ch_a, 1)
                act.wait_ge(rw_v, RV.at("s2", l))
                nc.scalar.activation(small_y[:, 4, :], small_y[:, 3, :], ACT.Sqrt, bias=const("eps_gn"),
                                     scale=1.0 / HD).then_inc(rw_a, 1)
                act.wait_ge(rw_p, RP.at("yT", l))
                src = ps[0:64, 4:8, :].rearrange("p b (u c) -> p (b u) c", c=P)
                for h in range(2):
                    ins = nc.scalar.copy(units(tmp)[h * 64:h * 64 + 64, :, :], src[:, :, h * 64:h * 64 + 64])
                ins.then_inc(rw_a, 1)

                act.wait_ge(resid, 3 * l + 2)
                norm(("ffn2", l, 0), x[:, :, :])
                ffn(4 + 2 * l)
            act.wait_ge(resid, 3 * LAYERS)
            norm(("final", 0, 0), x[:, :, :])

        @block.vector
        def _(dve):
            dve.wait_ge(const_loaded, 64)
            for l in range(LAYERS):
                ka0, ka1 = V[f"k_a{l}"]
                ins = nc.vector.tensor_scalar(omka[:, l * QT:(l + 1) * QT], vec[:, ka0:ka1], -1.0, 1.0,
                                              ALU.mult, ALU.add)
            ins.then_inc(kab, 1)
            c0 = chunk0["ada"]
            b0 = V["b_ada"][0]
            with dve.Fori(0, LAYERS * NMOD // 4) as i:
                for u in range(2):
                    dve.wait_ge(a_used, i * 2 + (c0 + u + 1))
                    nc.vector.tensor_tensor(
                        mod[:, bass.ds(i * 4 + 2 * u, 2), :], ps[:, 4 + u, 0:4].rearrange("p (a b) -> p a b", b=2),
                        vec[:, bass.ds(i * 4 + (b0 + 2 * u), 2)][:, :, None].to_broadcast([P, 2, 2]),
                        ALU.add).then_inc(ada_free, 1)
            dve.wait_ge(ada_free, LAYERS * NMOD // 2)
            for l in range(LAYERS):
                for i, (part, name, plus) in enumerate([(1, "pre_mix", 1.0), (2, "post_mix", 0.0),
                                                        (4, "pre_ffn", 1.0), (5, "post_ffn", 0.0)]):
                    v0, v1 = V[f"{name}{l}"]
                    ins = nc.vector.scalar_tensor_tensor(
                        gain[:, l, i], mod[:, l * NMOD + part * KD:l * NMOD + (part + 1) * KD, :], plus,
                        vec[:, v0:v1][:, :, None].to_broadcast([P, KD, 2]), ALU.add, ALU.mult)
            ins.then_inc(gain_ready, 1)
            dve.wait_ge(gain_ready, 1)

            def shift_of(l, part, which):
                return lambda k: mod[:, l * NMOD + part * KD + k, which:which + 1]

            def norm(key, src, gains, dst, shift=None, onto=None, last=None):
                n = n_id[key]
                dve.wait_ge(norm_rt, n + 1)
                nc.vector.reciprocal(rstd[:, :], nrt[:, :]).then_inc(norm_rstd, 1)
                dve.wait_ge(norm_rstd, n + 1)
                for k in range(KD):
                    ins = nc.vector.scalar_tensor_tensor(dst[:, k, :], src[:, k, :], gains(k), rstd[:, :],
                                                         ALU.mult, ALU.mult)
                if shift is None and onto is None:
                    ins.then_inc(norm_out, 1)
                    return
                ins.then_inc(norm_scaled, 1)
                dve.wait_ge(norm_scaled, n_two[key] + 1)
                if shift is not None:
                    to, add = shift
                    for k in range(KD):
                        ins = nc.vector.tensor_scalar(to[:, k, :], dst[:, k, :], add(k), None, ALU.add)
                    ins.then_inc(norm_out, 1)
                else:
                    nc.vector.tensor_tensor(onto, onto, dst[:, :, :], ALU.add).then_inc(norm_out, 1)

            def ffn(call):
                with dve.Fori(0, FT // 2) as i:
                    for u in range(2):
                        dve.wait_ge(sg_ready, i * 2 + (call * FT + u + 1))
                        nc.vector.tensor_tensor(hid[:, u, :], sg[:, u, :], ps[:, 4 + u, T:2 * T], ALU.mult)\
                            .then_inc(hid_ready, 1)

            def gain_of(l, i, which):
                return lambda k: gain[:, l, i, k, which:which + 1]

            def attention(call, l, which):
                n_keys = 2 * T if which == 0 else T

                def scores(u):
                    g, h, blk, r = call * 16 + u, (u % 2) * 4 + (u // 2) % 4, u // 8, u % 2
                    dve.wait_ge(at_sc, g + 1)
                    if g >= 2:
                        dve.wait_ge(at_exp, g - 1)
                    if which == 0:
                        ins = nc.vector.scalar_tensor_tensor(
                            s_sb[:, r, :], ps[:, r, :], HD ** -0.5, const1("win")[:, blk * 2 * T:(blk + 1) * 2 * T],
                            ALU.mult, ALU.add)
                    else:
                        ins = nc.vector.tensor_scalar(s_sb[:, r, 0:T], ps[:, r, 0:T], HD ** -0.5, None, ALU.mult)
                    ins.then_inc(at_s, 1)
                    dve.wait_ge(at_s, g + 1)
                    nc.vector.reduce_max(tiny[:, r, 0:1], s_sb[:, r, 0:n_keys], AX_X).then_inc(at_mx, 1)
                    dve.wait_ge(at_mx, g + 1)
                    nc.vector.tensor_scalar(tiny[:, r, 1:2], tiny[:, r, 0:1], vcol("sink", l * 8 + h), -1.0,
                                            ALU.max, ALU.mult).then_inc(at_nm, 1)

                def normalise(u):
                    g, r = call * 16 + u, u % 2
                    dve.wait_ge(at_exp, g + 1)
                    nc.vector.tensor_tensor(tiny[:, r, 4:5], tiny[:, r, 2:3], tiny[:, r, 3:4], ALU.add)\
                        .then_inc(at_den, 1)
                    dve.wait_ge(at_den, g + 1)
                    nc.vector.reciprocal(tiny[:, r, 5:6], tiny[:, r, 4:5]).then_inc(at_rd, 1)
                    dve.wait_ge(at_rd, g + 1)
                    if g >= 2:
                        dve.wait_ge(at_tr, g - 1)
                    nc.vector.tensor_scalar(pn[:, r, 0:n_keys], probs[:, r, 0:n_keys], tiny[:, r, 5:6], None,
                                            ALU.mult).then_inc(at_pn, 1)

                for u in range(17):
                    if u < 16:
                        scores(u)
                    if u >= 1:
                        normalise(u - 1)

            acall = 0
            for l in range(LAYERS):
                if l == 0:
                    dve.wait_ge(in_loaded, 32)
                norm(("pre_mix", l, 0), x, gain_of(l, 0, 0), hn, shift=(h2[:, :, 0:T], shift_of(l, 0, 0)))
                norm(("pre_mix", l, 1), xc, gain_of(l, 0, 1), hn, shift=(h2[:, :, T:2 * T], shift_of(l, 0, 1)))
                cos, sin = (const1(n)[:, None, :].to_broadcast([P, 5, T]) for n in ("cos", "sin"))
                dve.wait_ge(rope_rot, l + 1)
                rot = ps[:, 0:3, :].rearrange("p a (b t) -> p (a b) t", t=T)[:, 0:5, :]
                nc.vector.tensor_tensor(rtmp, rot, sin, ALU.mult).then_inc(rope_sin, 1)
                nc.vector.tensor_tensor(raw[:, :, 0:T], raw[:, :, 0:T], cos, ALU.mult).then_inc(rope_cos, 1)
                dve.wait_ge(rope_sin, l + 1)
                dve.wait_ge(rope_cos, l + 1)
                nc.vector.tensor_tensor(kall[:, 0:T], raw[:, 0, 0:T], rtmp[:, 0, :], ALU.add)
                nc.vector.tensor_tensor(qr, raw[:, 1:5, 0:T], rtmp[:, 1:5, :], ALU.add).then_inc(rope_out, 1)
                for which in ([0, 1] if l == 0 else [0]):
                    attention(acall, l, which)
                    acall += 1
                for which in ([0, 1] if l == 0 else [0]):
                    res = x[:, :, :] if which == 0 else xc
                    mixed = mix[:, :, token_cols(l, which)]
                    norm(("post_mix", l, which), mixed, gain_of(l, 1, which), hn, onto=res)
                    dve.wait_ge(norm_out, n_id[("post_mix", l, which)] + 1)
                    norm(("pre_ffn", l, which), res, gain_of(l, 2, which), hn,
                         shift=(h2[:, :, 0:T], shift_of(l, 3, which)))
                    ffn(2 * l + which)
                    norm(("post_ffn", l, which), mixed, gain_of(l, 3, which), hn, onto=res)

            def per_channel(name, l):
                return lambda k: vcol(f"{name}{l}", k)

            def v(name, l):
                dve.wait_ge(rw_v, RV.at(name, l))

            def wide(bank):
                return ps[:, bank:bank + 2, :].rearrange("p a (b t) -> p (a b) t", t=T)

            dve.wait_ge(norm_out, n_id[("post_ffn", 1, 0)] + 1)
            for l in range(LAYERS):
                norm(("ffn1", l, 0), x, per_channel("ffn1", l), hn)
                ffn(3 + 2 * l)
                dve.wait_ge(d_used, (4 + 2 * l) * FT)
                acc = ps[:, 0:4, :].rearrange("p a (b t) -> p (a b) t", t=T)
                nc.vector.scalar_tensor_tensor(x[:, :, :], acc, 0.5, x[:, :, :], ALU.mult, ALU.add).then_inc(resid, 1)
                dve.wait_ge(resid, 3 * l + 1)
                norm(("mix", l, 0), x, per_channel("mix", l), hn)

                zr, zk, zv = (z[:, a:a + QT, 1:T + 1] for a in (R0, K0, V0))
                p0 = tile0[f"proj2{l}"]
                dve.wait_ge(proj_free, p0 + MIXED)
                nc.vector.tensor_tensor(diff, z[:, 0:MIXED, 0:T], z[:, 0:MIXED, 1:T + 1], ALU.subtract)\
                    .then_inc(rw_v, 1)
                v("diff", l)
                for k in range(MIXED):
                    rows = slice(0, P) if k != MISC else slice(0, 32)
                    zz = z[rows, k, 1:T + 1]
                    ins = nc.vector.scalar_tensor_tensor(zz, diff[rows, k, :], vcol(f"mu{l}", k)[rows], zz,
                                                         ALU.mult, ALU.add)
                ins.then_inc(rw_v, 1)
                dve.wait_ge(proj_free, p0 + MK + QT)
                for tap in range(4):
                    if tap:
                        dve.wait_ge(ml_v, MVS.at(f"c{tap - 1}", l))
                    for k in range(2 * QT):
                        zz = z[:, MQ + k, 1:T + 1 - tap]
                        if tap == 0:
                            ins = nc.vector.tensor_scalar(nsq[:, k, :], zz, vcol(f"tap3{l}", k),
                                                          vcol(f"conv_b{l}", k), ALU.mult, ALU.add)
                        else:
                            ins = nc.vector.scalar_tensor_tensor(nsq[:, k, tap:T], zz, vcol(f"tap{3 - tap}{l}", k),
                                                                 nsq[:, k, tap:T], ALU.mult, ALU.add)
                    ins.then_inc(ml_v, 1)
                dve.wait_ge(rw_a, RA.at("sw", l))
                nc.vector.tensor_scalar(lw, lw, -float(np.exp(-0.5)), None, ALU.mult).then_inc(rw_v, 1)
                v("lw", l)
                for j in range(QT):
                    ins = nc.vector.tensor_tensor_scan(lcum[:, j, :], const("restart"), lw[:, j, :], 0.0,
                                                       ALU.mult, ALU.add)
                ins.then_inc(rw_v, 1)
                v("mix", l)
                for j in range(QT):
                    ins = nc.vector.tensor_scalar(kk[:, j, :], zk[:, j, :], vcol(f"k_k{l}", j), None, ALU.mult)
                ins.then_inc(rw_v, 1)
                v("kk", l)
                nc.vector.tensor_tensor(bon, kk, kk, ALU.mult).then_inc(rw_v, 1)
                if l == 0:
                    nc.vector.tensor_copy(vfirst[:, :, :], zv)
                else:
                    dve.wait_ge(vres_a, 1)
                    nc.vector.tensor_tensor(e1, vfirst[:, :, :], zv, ALU.subtract).then_inc(vres_v, 1)
                    dve.wait_ge(vres_v, VV.at("d", 0))
                    nc.vector.tensor_tensor(e1, e1, vg, ALU.mult).then_inc(vres_v, 1)
                    dve.wait_ge(vres_v, VV.at("m", 0))
                    nc.vector.tensor_tensor(zv, zv, e1, ALU.add).then_inc(vres_v, 1)
                dve.wait_ge(rw_a, RA.at("rsq", l))
                nc.vector.tensor_scalar(tmp[0:8, 3, :], tmp[0:8, 3, :], 1e-12, None, ALU.max).then_inc(rw_v, 1)
                v("rnmax", l)
                nc.vector.reciprocal(inv_norm, tmp[0:8, 3, :]).then_inc(rw_v, 1)
                dve.wait_ge(rw_p, RP.at("rnb", l))
                nc.vector.tensor_tensor(kk, kk, wide(0), ALU.mult).then_inc(rw_v, 1)
                v("kkn", l)
                dve.wait_ge(rw_a, RA.at("aa", l))
                nc.vector.tensor_tensor(bb, kk, aa, ALU.mult).then_inc(rw_v, 1)
                v("b", l)
                dve.wait_ge(kab, 1)
                for j in range(QT):
                    ins = nc.vector.tensor_scalar(aa[:, j, :], aa[:, j, :], vcol(f"k_a{l}", j),
                                                  omka[:, l * QT + j:l * QT + j + 1], ALU.mult, ALU.add)
                ins.then_inc(rw_v, 1)
                v("ka", l)
                nc.vector.tensor_tensor(zk, zk, aa, ALU.mult).then_inc(rw_v, 1)
                v("kp", l)
                dve.wait_ge(rw_p, RP.at("ss", l))
                for j in range(QT):
                    ins = nc.vector.scalar_tensor_tensor(bon[:, j, :], zr[:, j, :], vcol(f"r_k{l}", j), zk[:, j, :],
                                                         ALU.mult, ALU.mult)
                ins.then_inc(rw_v, 1)
                if l:
                    dve.wait_ge(vres_v, VV.at("v", 0))
                dve.wait_ge(rw_p, RP.at("bon", l))
                nc.vector.tensor_tensor(bon, wide(2), zv, ALU.mult).then_inc(rw_v, 1)
                v("scan", l)
                nc.vector.tensor_tensor(e0, lcum, lw, ALU.subtract).then_inc(rw_v, 1)
                dve.wait_ge(rw_a, RA.at("e2", l))
                nc.vector.tensor_tensor(kt, kk, e0, ALU.mult).then_inc(rw_v, 1)
                nc.vector.tensor_tensor(bh, bb, e2, ALU.mult).then_inc(rw_v, 1)
                v("kt", l)
                nc.vector.tensor_tensor(kh, zk, e2, ALU.mult).then_inc(rw_v, 1)
                nc.vector.tensor_tensor(zr, zr, e1, ALU.mult).then_inc(rw_v, 1)
                v("kh", l)
                pc = units(e1)[:, :, CHUNK - 1:CHUNK].to_broadcast([P, UNITS, CHUNK])
                nc.vector.tensor_tensor(units(khc), units(kh), pc, ALU.mult).then_inc(rw_v, 1)
                nc.vector.tensor_tensor(units(bhc), units(bh), pc, ALU.mult).then_inc(rw_v, 1)

                def m(name):
                    dve.wait_ge(ml_v, MVS.at(name, l))
                row = lambda i: rows4[0:4, i, :]
                dve.wait_ge(ml_a, MA.at("ab", l))
                nc.vector.tensor_scalar(row(3), ps[0:4, 6, T:2 * T], vcol(f"fb{l}", 0)[0:4], 0.0, ALU.add, ALU.min)\
                    .then_inc(ml_v, 1)
                m("mn")
                dve.wait_ge(ml_a, MA.at("ln", l))
                nc.vector.tensor_tensor(row(4), row(3), row(2), ALU.subtract).then_inc(ml_v, 1)
                m("lf")
                ones_row = const("one")[0:4].to_broadcast([4, T])
                nc.vector.tensor_tensor_scan(row(5), ones_row, row(4), 0.0, ALU.mult, ALU.add).then_inc(ml_v, 1)
                m("F")
                nc.vector.scalar_tensor_tensor(row(6), ps[0:4, 6, 0:T], vcol(f"ib{l}", 0)[0:4], row(5),
                                               ALU.add, ALU.subtract).then_inc(ml_v, 1)
                m("g")
                nc.vector.tensor_tensor_scan(row(7), ones_row, row(6), 0.0, ALU.mult, ALU.max).then_inc(ml_v, 1)
                m("M")
                nc.vector.tensor_scalar(row(0), row(7), -1.0, None, ALU.mult).then_inc(ml_v, 1)
                nc.vector.tensor_tensor(row(1), row(5), row(7), ALU.add).then_inc(ml_v, 1)
                for h in range(5):
                    r = l * 4 + h
                    if h < 4:
                        dve.wait_ge(mh_arg, r + 1)
                        if r >= 2:
                            dve.wait_ge(mh_ee, r - 1)
                        nc.vector.tensor_tensor(am[:, h % 2, :], ps[:, h % 2, 0:T + P], const("tri"), ALU.add)\
                            .then_inc(mh_am, 1)
                        dve.wait_ge(mh_ee, r + 1)
                        dve.wait_ge(mh_s, r + 1)
                        if r >= 2:
                            dve.wait_ge(mh_nd, r - 1)
                        nc.vector.scalar_tensor_tensor(pm[:, h % 2, :], ps[:, 2 + h % 2, 0:T + P], float(P) ** -0.5,
                                                       ee[:, h % 2, :], ALU.mult, ALU.mult).then_inc(mh_pm, 1)
                    if h >= 1:
                        r, o = r - 1, (h - 1) % 2
                        dve.wait_ge(mh_ems, r + 1)
                        dve.wait_ge(mh_nd, r + 1)
                        nc.vector.scalar_tensor_tensor(dn[:, o, :], ps[:, 6 + o, T:2 * T], -1.0, ems[:, o, :],
                                                       ALU.mult, ALU.max).then_inc(mh_dn, 1)
                        dve.wait_ge(mh_dn, r + 1)
                        nc.vector.tensor_tensor(dn[:, o, :], ps[:, 6 + o, T:2 * T], dn[:, o, :], ALU.max)\
                            .then_inc(mh_abs, 1)
                        dve.wait_ge(mh_abs, r + 1)
                        nc.vector.reciprocal(dn[:, o, :], dn[:, o, :]).then_inc(mh_rc, 1)
                        dve.wait_ge(mh_rc, r + 1)
                        nc.vector.tensor_tensor(hN[:, h - 1, :], ps[:, 6 + o, 0:T], dn[:, o, :], ALU.mult)\
                            .then_inc(mh_h, 1)
                dve.wait_ge(ml_p, MP.at("mu", l))
                nc.vector.scalar_tensor_tensor(hc, wide(0), -1.0 / P, hN, ALU.mult, ALU.add).then_inc(ml_v, 1)
                dve.wait_ge(ml_a, MA.at("hsd", l))
                nc.vector.reciprocal(yb, yb).then_inc(ml_v, 1)
                m("rec")
                nc.vector.tensor_tensor(hc, hc, yb, ALU.mult).then_inc(ml_v, 1)
                m("hs")
                for j in range(QT):
                    ins = nc.vector.scalar_tensor_tensor(yb[:, j, :], hc[:, j, :], vcol(f"ml_w{l}", j),
                                                         z[:, MO + j, 1:T + 1], ALU.mult, ALU.mult)
                ins.then_inc(ml_v, 1)
                m("yb")

                def masked(dst, bank, mask, op=ALU.mult):
                    return nc.vector.tensor_tensor(
                        units(dst), ps[:, bank:bank + 2, :].rearrange("p b (u t) -> p (b u) t", t=CHUNK),
                        const(mask)[:, None, :].to_broadcast([P, UNITS, CHUNK]), op)

                eye = const("eye")[:, None, :].to_broadcast([P, UNITS, CHUNK])
                dve.wait_ge(rw_p, RP.at("at", l))
                masked(at_, 4, "strict").then_inc(rw_v, 1)
                dve.wait_ge(rw_p, RP.at("a", l))
                masked(xs, 0, "low1").then_inc(rw_v, 1)
                v("at", l)
                nc.vector.tensor_tensor(units(xt), units(at_),
                                        const("up1")[:, None, :].to_broadcast([P, UNITS, CHUNK]), ALU.mult)\
                    .then_inc(rw_v, 1)
                dve.wait_ge(rw_p, RP.at("mt", l))
                masked(mt, 6, "strict").then_inc(rw_v, 1)
                v("xt1", l)
                nc.vector.tensor_tensor(units(xs), eye, units(xs), ALU.subtract).then_inc(rw_v, 1)
                nc.vector.tensor_tensor(units(xt), eye, units(xt), ALU.subtract).then_inc(rw_v, 1)
                dve.wait_ge(rw_p, RP.at("mrt", l))
                masked(mrt, 2, "incl").then_inc(rw_v, 1)
                dve.wait_ge(rw_p, RP.at("art", l))
                masked(art, 4, "incl").then_inc(rw_v, 1)
                for i in range(len(LEVELS)):
                    step = l * len(LEVELS) + i
                    for half in range(2):
                        us = slice(half * 8, half * 8 + 8)
                        dve.wait_ge(lev_p, LP.at(f"x{half}", step))
                        for buf, bank in ((xs, 2), (xt, 4)):
                            nc.vector.tensor_tensor(
                                units(buf)[:, us, :], units(buf)[:, us, :],
                                ps[:, bank + half, :].rearrange("p (u t) -> p u t", t=CHUNK), ALU.subtract)\
                                .then_inc(lev_v, 1)
                pcs = units(e1)[:, :, CHUNK - 1:CHUNK]
                for c in range(NC_):
                    step = l * NC_ + c
                    if c == 0:
                        nc.vector.memset(state[:, 0], 0.0).then_inc(ch_v, 1)
                    else:
                        dve.wait_ge(ch_v, CV.at("s", step - 1))
                        nc.vector.tensor_tensor(
                            sdec, state[:, c % 2],
                            e1[:, :, c * CHUNK + CHUNK - 1:c * CHUNK + CHUNK].to_broadcast([P, QT, HD]),
                            ALU.mult).then_inc(ch_v, 1)
                    dve.wait_ge(ch_p, CP.at("u", step))
                    nc.vector.tensor_scalar(nu[:, :, c * CHUNK:(c + 1) * CHUNK],
                                            ps[:, 1, 0:QT * HD].rearrange("p (j v) -> p j v", v=HD), -1.0, None,
                                            ALU.mult).then_inc(ch_v, 1)
                    dve.wait_ge(ch_p, CP.at("s", step))
                    sp_ = ps[:, 4, 0:QT * HD].rearrange("p (j v) -> p j v", v=HD)
                    if c:
                        dve.wait_ge(ch_v, CV.at("nu", step))
                        nc.vector.tensor_tensor(state[:, (c + 1) % 2], sp_, sdec, ALU.add).then_inc(ch_v, 1)
                    else:
                        nc.vector.tensor_copy(state[:, 1], sp_).then_inc(ch_v, 1)
                yps = ps[:, 2:4, :].rearrange("p b (u t) -> p (b u) t", t=HD)
                stat = lambda i: small_y[:, i, :]
                wide_stat = lambda i: small_y[:, i, :][:, :, None].to_broadcast([P, UNITS, HD])
                dve.wait_ge(ch_p, CP.at("y", l * NC_ + NC_ - 1))
                nc.vector.reduce_sum(stat(0), yps, AX_X).then_inc(rw_v, 1)
                v("s1", l)
                nc.vector.tensor_scalar(stat(1), stat(0), -1.0 / HD, None, ALU.mult).then_inc(rw_v, 1)
                v("ym", l)
                nc.vector.tensor_tensor(units(yy), yps, wide_stat(1), ALU.add).then_inc(rw_v, 1)
                v("yc", l)
                nc.vector.tensor_tensor(units(yq), units(yy), units(yy), ALU.mult).then_inc(rw_v, 1)
                v("yq", l)
                nc.vector.reduce_sum(stat(3), units(yq), AX_X).then_inc(rw_v, 1)
                dve.wait_ge(rw_a, RA.at("ysd", l))
                nc.vector.reciprocal(stat(5), stat(4)).then_inc(rw_v, 1)
                v("yr", l)
                nc.vector.tensor_tensor(units(yy), units(yy), wide_stat(5), ALU.mult).then_inc(rw_v, 1)
                dve.wait_ge(rw_a, RA.at("yT", l))
                for j in range(QT):
                    ins = nc.vector.tensor_scalar(tmp[:, j, :], tmp[:, j, :], vcol(f"gn_w{l}", j),
                                                  vcol(f"gn_b{l}", j), ALU.mult, ALU.add)
                ins.then_inc(rw_v, 1)
                v("gn", l)
                nc.vector.tensor_tensor(tmp, tmp, bon, ALU.add).then_inc(rw_v, 1)
                v("gb", l)
                nc.vector.tensor_tensor(ya, tmp, gg, ALU.mult).then_inc(rw_v, 1)

                dve.wait_ge(ml_a, MA.at("gates", l))
                for n in range(KD):
                    r = l * KD + n
                    if n % 2:
                        dve.wait_ge(a_used, chunk0[f"br{l}"] + n // 2 + 1)
                    else:
                        dve.wait_ge(br_ready, r // 2 + 1)
                    nc.vector.tensor_tensor(umix[:, n, :], ps[:, 4 + n % 2, 0:T], z[:, GA + n, 1:T + 1], ALU.mult)\
                        .then_inc(br_part, 1)
                    nc.vector.tensor_tensor(xs[:, n % 2, :], ps[:, 4 + n % 2, T:2 * T], z[:, GB + n, 1:T + 1], ALU.mult)\
                        .then_inc(br_part, 1)
                    dve.wait_ge(br_part, 2 * r + 2)
                    nc.vector.tensor_tensor(umix[:, n, :], umix[:, n, :], xs[:, n % 2, :], ALU.add).then_inc(br_free, 1)
                for n in range(KD // 2):
                    dve.wait_ge(a_used, chunk0[f"out2{l}"] + n + 1)
                    xx = x[:, 2 * n:2 * n + 2, :]
                    ins = nc.vector.tensor_tensor(xx, xx, ps[:, n, :].rearrange("p (a b) -> p a b", b=T), ALU.add)
                ins.then_inc(resid, 1)
                dve.wait_ge(resid, 3 * l + 2)
                norm(("ffn2", l, 0), x, per_channel("ffn2", l), hn)
                ffn(4 + 2 * l)
                dve.wait_ge(d_used, (5 + 2 * l) * FT)
                nc.vector.scalar_tensor_tensor(x[:, :, :], acc, 0.5, x[:, :, :], ALU.mult, ALU.add).then_inc(resid, 1)
                dve.wait_ge(resid, 3 * l + 3)
            norm(("final", 0, 0), x, lambda k: vcol("final", k), hn)

        @block.tensor
        def _(pe):
            pe.wait_ge(const_loaded, 64)
            ones, ident = const("ones"), const("ident")

            def chunk_here(c, slot, i=None):
                n = 16 * (c // 2 + 1)
                pe.wait_ge(a_loaded[slot], n if i is None else i * 16 + n)

            pe.wait_ge(cs_ready, 1)

            def ada(c, u, i=None):
                chunk_here(c, u, i)
                if i is not None:
                    pe.wait_ge(ada_free, i * 2 + (c - 1))
                for n in range(2):
                    for k in range(KD):
                        mm = nc.tensor.matmul(ps[:, 4 + u, 2 * n:2 * n + 2], ring_a[:, u, n, k, :], cs[:, k, :],
                                              start=(k == 0), stop=(k == KD - 1))
                mm.then_inc(a_used, 1)

            ada(0, 0)
            ada(1, 1)
            with pe.Fori(0, LAYERS * NMOD // 4 - 1) as i:
                ada(2, 0, i)
                ada(3, 1, i)

            def norm(key):
                n = n_id[key]
                pe.wait_ge(norm_sq, n + 1)
                if n:
                    pe.wait_ge(norm_rt, n)
                for k in range(KD):
                    mm = nc.tensor.matmul(ps[:, 6, 0:T], ones, nsq[:, k, :], start=(k == 0), stop=(k == KD - 1))
                mm.then_inc(norm_sum, 1)

            def ffn(call, h):
                c0, d0 = chunk0[f"ffn{call}"], call * FT

                def gate_up(f, i=None):
                    bank, c = 4 + f % 2, c0 + f
                    slot = c % 2
                    chunk_here(c, slot, i)
                    if i is not None or f >= 2 or call:
                        v = call * FT + f - 1
                        pe.wait_ge(hid_ready, v if i is None else i * 2 + v)
                    for part in range(2):
                        for k in range(KD):
                            mm = nc.tensor.matmul(ps[:, bank, part * T:part * T + T], ring_a[:, slot, part, k, :],
                                                  h[:, k, 0:T], start=(k == 0), stop=(k == KD - 1))
                    mm.then_inc(a_used, 1)

                def down(f, i=None):
                    d = d0 + f
                    slot = d % 2
                    n = 16 * (d // 2 + 1)
                    pe.wait_ge(d_loaded[slot], n if i is None else i * 16 + n)
                    pe.wait_ge(hid_ready, d + 1 if i is None else i * 2 + (d + 1))
                    for n in range(KD):
                        mm = nc.tensor.matmul(ps[:, n // 2, n % 2 * T:n % 2 * T + T], ring_d[:, slot, n, :],
                                              hid[:, f % 2, :], start=(f == 0 and n % 2 == 0), stop=(f == FT - 1),
                                              skip_group_check=True)
                    mm.then_inc(d_used, 1)

                gate_up(0)
                gate_up(1)
                down(0)
                with pe.Fori(0, (FT - 2) // 2) as i:
                    for u in range(2):
                        gate_up(2 + u, i)
                        down(1 + u, i)
                down(FT - 1)

            def tile_done(mm, stage, i):
                mm.then_inc(a_used if i % 2 or i == ZT + QT - 1 else proj_ready, 1)

            def project(stage, i, h, cols):
                p, slot = tile0[stage] + i, (chunk0[stage] + i // 2) % 2
                if i % 2 == 0:
                    chunk_here(chunk0[stage] + i // 2, slot)
                if p >= 2:
                    pe.wait_ge(proj_free, p - 1)
                for k in range(KD):
                    mm = nc.tensor.matmul(ps[:, 4 + p % 2, 0:cols.stop - cols.start], ring_a[:, slot, i % 2, k, :],
                                          h[:, k, cols], start=(k == 0), stop=(k == KD - 1))
                tile_done(mm, stage, i)

            def project_tokens(stage, i, h, blocks):
                p, slot = tile0[stage] + i, (chunk0[stage] + i // 2) % 2
                if i % 2 == 0:
                    chunk_here(chunk0[stage] + i // 2, slot)
                if p >= 2:
                    pe.wait_ge(proj_free, p - 1)
                for b in range(blocks):
                    for k in range(KD):
                        mm = nc.tensor.matmul(ps[:, 4 + p % 2, b * P:(b + 1) * P], h[:, k, b * P:(b + 1) * P],
                                              ring_a[:, slot, i % 2, k, :], start=(k == 0), stop=(k == KD - 1))
                tile_done(mm, stage, i)

            def fourier(call, l, which):
                wait_u = tile0[f"proj1{l}"] + 10
                pe.wait_ge(proj_free, wait_u)
                pe.wait_ge(rope_sin, l + 1)
                if call:
                    pe.wait_ge(fo_out, call * QT)
                if which:
                    pe.wait_ge(at_pt, (call) * 16)
                    pe.wait_ge(at_s, (call) * 16)
                for j in range(QT):
                    for b in range(2):
                        mm = nc.tensor.matmul(ps[:, j, :], u_tok[:, 2 * which + b, j * P:(j + 1) * P],
                                              const1("dft")[:, b * 2 * T:(b + 1) * 2 * T], start=(b == 0), stop=(b == 1))
                    mm.then_inc(fo_dft, 1)
                for j in range(QT):
                    pe.wait_ge(fo_fu, call * QT + j + 1)
                    nc.tensor.matmul(ps[:, j, 0:T], const1("chc"), fu[:, j, 0:T], start=True, stop=False)
                    nc.tensor.matmul(ps[:, j, 0:T], const1("chs"), fu[:, j, T:2 * T], start=False, stop=True)\
                        .then_inc(fo_ch, 1)
                for j in range(QT):
                    pe.wait_ge(fo_fm, call * QT + j + 1)
                    nc.tensor.matmul(ps[:, j, T:2 * T], wfour[:, l * QT + j, :], fm[:, j, :], start=True, stop=True)\
                        .then_inc(fo_w, 1)

            def attention(call, l, which):
                n_keys = 2 * T if which == 0 else T
                keys = kall if which == 0 else kall[:, T:2 * T]
                pe.wait_ge(fo_out, (call + 1) * QT)
                pe.wait_ge(rope_out, l + 1)

                def scores(u):
                    g, blk, j, kv = call * 16 + u, u // 8, u // 2 % 4, u % 2
                    half = slice(kv * HD, kv * HD + HD)
                    if g >= 2:
                        pe.wait_ge(at_s, g - 1)
                    q = qr[half, j, blk * P:(blk + 1) * P] if which == 0 else \
                        raw[half, 1 + j, T + blk * P:T + (blk + 1) * P]
                    nc.tensor.matmul(ps[:, u % 2, 0:n_keys], q, keys[half, :], start=True, stop=True).then_inc(at_sc, 1)

                def turn(u):
                    g = call * 16 + u
                    pe.wait_ge(at_pn, g + 1)
                    if g >= 2:
                        pe.wait_ge(at_pt, g - 1)
                    for b in range(n_keys // P):
                        mm = nc.tensor.transpose(ps[:, 2 + u % 2, b * P:(b + 1) * P], pn[:, u % 2, b * P:(b + 1) * P],
                                                 ident)
                    mm.then_inc(at_tr, 1)

                def values(u):
                    g, w, kv = call * 16 + u, u // 2, u % 2
                    half = slice(kv * HD, kv * HD + HD)
                    pe.wait_ge(at_pt, g + 1)
                    if call * 8 + w >= 2:
                        pe.wait_ge(at_o, call * 8 + w - 1)
                    nb = n_keys // P
                    for b in range(nb):
                        mm = nc.tensor.matmul(ps[half, 6 + w % 2, 0:P], v_tok[:, 4 - nb + b, half], pt[:, u % 2, b, :],
                                              start=(b == 0), stop=(b == nb - 1))
                    mm.then_inc(at_pv, 1)

                for u in range(18):
                    if u < 16:
                        scores(u)
                    if 1 <= u <= 16:
                        turn(u - 1)
                    if u >= 2:
                        values(u - 2)

            fcall = 0
            for l in range(LAYERS):
                norm(("pre_mix", l, 0))
                norm(("pre_mix", l, 1))
                pe.wait_ge(norm_out, n_id[("pre_mix", l, 1)] + 1)
                stage, n_q = f"proj1{l}", (2 * T, T)[l]
                for i in range(10):
                    if i == 0:
                        project(stage, i, h2, slice(0, 2 * T))
                    elif i <= QT:
                        project(stage, i, h2, slice(0, n_q))
                    else:
                        project_tokens(stage, i, h2, 4 if i == QT + 1 else n_q // P)
                    if i == 6:
                        pe.wait_ge(proj_free, tile0[stage] + 5)
                        for j in range(5):
                            mm = nc.tensor.matmul(ps[:, j // 2, j % 2 * T:j % 2 * T + T], const1("rot"), raw[:, j, 0:T],
                                                  start=True, stop=True)
                        mm.then_inc(rope_rot, 1)
                for which in ([0, 1] if l == 0 else [0]):
                    fourier(fcall, l, which)
                    attention(fcall, l, which)
                    fcall += 1
                pe.wait_ge(at_o, fcall * 8)
                for i in range(KD):
                    project(f"out1{l}", i, mixin, slice(0, n_q))
                for which in ([0, 1] if l == 0 else [0]):
                    norm(("post_mix", l, which))
                    norm(("pre_ffn", l, which))
                    pe.wait_ge(norm_out, n_id[("pre_ffn", l, which)] + 1)
                    ffn(2 * l + which, h2)
                    norm(("post_ffn", l, which))

            heads = [(slice(0, 64), 0), (slice(64, 128), 1)]

            for l in range(LAYERS):
                norm(("ffn1", l, 0))
                pe.wait_ge(norm_out, n_id[("ffn1", l, 0)] + 1)
                ffn(3 + 2 * l, hn)
                norm(("mix", l, 0))
                pe.wait_ge(norm_out, n_id[("mix", l, 0)] + 1)
                p0, c0 = tile0[f"proj2{l}"], chunk0[f"proj2{l}"]

                def tiles(first, count):
                    with pe.Fori(0, count // 4) as i:
                        for u in range(4):
                            t, c = first + u, c0 + (first + u) // 2
                            slot = c % 2
                            if u % 2 == 0:
                                chunk_here(c, slot, i)
                            pe.wait_ge(proj_free, i * 4 + (p0 + t - 1))
                            for k in range(KD):
                                mm = nc.tensor.matmul(ps[:, 4 + (p0 + t) % 2, 0:T], ring_a[:, slot, u % 2, k, :],
                                                      hn[:, k, :], start=(k == 0), stop=(k == KD - 1))
                            tile_done(mm, f"proj2{l}", u)

                tiles(0, 28)
                wa_up, g_up, m_up = (small[:, SM[n][0]:SM[n][1]] for n in ("waup", "gup", "mup"))
                pe.wait_ge(rw_a, RA.at("sgx", l))
                pe.wait_ge(small_loaded, 16 * (l + 1))
                half = lambda j: slice(j % 2 * T, j % 2 * T + T)
                cols = lambda j: slice(j * P, j * P + P)
                for j in range(QT):
                    mm = nc.tensor.matmul(ps[:, j // 2, half(j)], wa_up[0:64, cols(j)], tmp[0:64, 0, :],
                                          start=True, stop=True)
                mm.then_inc(rw_p, 1)
                for j in range(QT):
                    mm = nc.tensor.matmul(ps[:, 2 + j // 2, half(j)], wa_up[64:128, cols(j)], z[64:128, XWA, 1:T + 1],
                                          start=True, stop=True)
                mm.then_inc(rw_p, 1)
                for j in range(QT):
                    nc.tensor.matmul(ps[:, 6 + j // 2, half(j)], g_up[:, cols(j)], tmp[:, 1, :], start=True, stop=False)
                    mm = nc.tensor.matmul(ps[:, 6 + j // 2, half(j)], m_up[0:32, cols(j)], tmp[0:32, 2, :],
                                          start=False, stop=True)
                mm.then_inc(rw_p, 1)
                tiles(28, 8)
                if l:
                    pe.wait_ge(rw_a, RA.at("sw", l))
                    for j in range(QT):
                        mm = nc.tensor.matmul(ps[:, j // 2, half(j)], m_up[VROW:P, cols(j)], z[VROW:P, MISC, 1:T + 1],
                                              start=True, stop=True, tile_position=(VROW, 0))
                    mm.then_inc(vres_p, 1)
                pe.wait_ge(rw_v, RV.at("kq", l))
                pe.wait_ge(rw_a, RA.at("aa", l))
                hs = const("headsum")
                for j in range(QT):
                    mm = nc.tensor.matmul(ps[0:8, 2, 0:T], hs[:, j * 8:(j + 1) * 8], bon[:, j, :],
                                          start=(j == 0), stop=(j == QT - 1))
                mm.then_inc(rw_p, 1)
                tiles(36, 4)
                pe.wait_ge(rw_v, RV.at("rn", l))
                if l:
                    pe.wait_ge(vres_a, 1)
                hr = const("headrow")
                for j in range(QT):
                    mm = nc.tensor.matmul(ps[:, j // 2, half(j)], hr[0:8, cols(j)], inv_norm, start=True, stop=True)
                mm.then_inc(rw_p, 1)
                for t in range(40, ZT + QT):
                    if t < ZT:
                        project(f"proj2{l}", t, hn, slice(0, T))
                    else:
                        project_tokens(f"proj2{l}", t, hn, 2)
                pe.wait_ge(rw_v, RV.at("rkr", l))
                for j in range(QT):
                    mm = nc.tensor.matmul(ps[:, 2 + j // 2, half(j)], const("headones"), bon[:, j, :],
                                          start=True, stop=True)
                mm.then_inc(rw_p, 1)

                def to_tokens(src, bank):
                    for j in range(QT):
                        for b in range(2):
                            mm = nc.tensor.transpose(ps[:, bank + j // 2, (j % 2 * 2 + b) * P:(j % 2 * 2 + b + 1) * P],
                                                     src[:, j, b * P:(b + 1) * P], ident)
                    return mm

                pe.wait_ge(rw_v, RV.at("bon", l))
                to_tokens(z[:, V0:V0 + QT, 1:T + 1], 2).then_inc(rw_p, 1)
                pe.wait_ge(rw_a, RA.at("gg", l))
                pe.wait_ge(proj_free, p0 + ZT + QT)
                nc.tensor.matmul(ps[0:4, 6, 0:T], const("seli"), z[:, MISC, 1:T + 1], start=True, stop=True)
                nc.tensor.matmul(ps[0:4, 6, T:2 * T], const("self"), z[:, MISC, 1:T + 1], start=True, stop=True)\
                    .then_inc(ml_p, 1)
                pe.wait_ge(rw_v, RV.at("bhc", l))
                to_tokens(khc, 0).then_inc(rw_p, 1)
                to_tokens(bhc, 4).then_inc(rw_p, 1)

                pe.wait_ge(ml_v, MVS.at("fm", l))
                pe.wait_ge(ml_a, MA.at("silu", l))
                pe.wait_ge(rw_a, RA.at("bhct", l))

                def front(h):
                    r, o = l * 4 + h, h % 2
                    pick = ident[0:4, h:h + 1]
                    g, neg_m, f_m = (rows4[0:4, i, :] for i in (6, 0, 1))
                    if h >= 2:
                        pe.wait_ge(mh_am, r - 1)
                    for b in range(2):
                        c = slice(0, T) if b == 0 else slice(T, T + P)
                        w = c.stop - c.start
                        nc.tensor.matmul(ps[:, o, c], g[:, b * P:(b + 1) * P], pick.to_broadcast([4, w]),
                                         start=True, stop=False)
                        mm = nc.tensor.matmul(ps[:, o, c], pick.to_broadcast([4, P]), neg_m[:, b * P:T],
                                              start=False, stop=True)
                    mm.then_inc(mh_arg, 1)
                    if h >= 2:
                        pe.wait_ge(mh_pm, r - 1)
                    for b in range(2):
                        c = slice(0, T) if b == 0 else slice(T, T + P)
                        mm = nc.tensor.matmul(ps[:, 2 + o, c], nsq[:, QT + h, b * P:(b + 1) * P], nsq[:, h, b * P:T],
                                              start=True, stop=True)
                    mm.then_inc(mh_s, 1)
                    if h >= 2:
                        pe.wait_ge(mh_ems, r - 1)
                    nc.tensor.matmul(ps[:, 4 + o, 0:T], pick.to_broadcast([4, P]), f_m, start=True, stop=True)\
                        .then_inc(mh_em, 1)

                front(0)
                for h in range(4):
                    r, o = l * 4 + h, h % 2
                    if h < 3:
                        front(h + 1)
                    pe.wait_ge(mh_pm, r + 1)
                    if h >= 2:
                        pe.wait_ge(mh_h, r - 1)
                    for c0_, left in ((0, lambda b: mv[:, b, h * P:(h + 1) * P]), (T, lambda b: ones)):
                        nc.tensor.matmul(ps[:, 6 + o, c0_:c0_ + T], left(0), pm[:, o, 0:T], start=True, stop=False)
                        mm = nc.tensor.matmul(ps[:, 6 + o, c0_ + P:c0_ + T], left(1), pm[:, o, T:T + P],
                                              start=False, stop=True)
                    mm.then_inc(mh_nd, 1)
                pe.wait_ge(mh_h, l * 4 + 4)
                for j in range(QT):
                    mm = nc.tensor.matmul(ps[:, j // 2, half(j)], ones, hN[:, j, :], start=True, stop=True)
                mm.then_inc(ml_p, 1)
                pe.wait_ge(ml_a, MA.at("hq", l))
                for j in range(QT):
                    mm = nc.tensor.matmul(ps[:, 2 + j // 2, half(j)], ones, hN[:, j, :], start=True, stop=True)
                mm.then_inc(ml_p, 1)

                pe.wait_ge(rw_v, RV.at("bhc", l))

                def unit(v, u, h):
                    j, c = u // NC_, u % NC_
                    return v[h * HD:h * HD + HD, j, c * CHUNK:(c + 1) * CHUNK]

                def out_unit(bank, u, h):
                    return ps[h * HD:h * HD + HD, bank + u // 8, u % 8 * CHUNK:(u % 8 + 1) * CHUNK]

                def per_unit(bank, left, right, us=range(UNITS)):
                    for u in us:
                        for h in range(2):
                            mm = nc.tensor.matmul(out_unit(bank, u, h), unit(left, u, h), unit(right, u, h),
                                                  start=True, stop=True)
                    return mm

                rt = z[:, R0:R0 + QT, 1:T + 1]
                per_unit(4, bh, kt).then_inc(rw_p, 1)
                pe.wait_ge(ml_v, MVS.at("hc", l))
                per_unit(0, kt, bh).then_inc(rw_p, 1)
                per_unit(6, kh, kt).then_inc(rw_p, 1)
                pe.wait_ge(ml_a, MA.at("hsd", l))
                per_unit(2, kh, rt).then_inc(rw_p, 1)
                pe.wait_ge(rw_v, RV.at("at", l))
                per_unit(4, bh, rt).then_inc(rw_p, 1)

                pe.wait_ge(rw_v, RV.at("art", l))
                for i in range(len(LEVELS)):
                    step = l * len(LEVELS) + i
                    pe.wait_ge(lev_g, step + 1)
                    for b in range(2):
                        if i:
                            pe.wait_ge(lev_v, LV.at(f"xt{b}", step - 1))
                        per_unit(0, aoff, xs, range(b * 8, b * 8 + 8)).then_inc(lev_p, 1)
                    for b in range(2):
                        us = range(b * 8, b * 8 + 8)
                        pe.wait_ge(lev_a, LA.at(f"w{b}", step))
                        per_unit(2, xt, ws, us)
                        per_unit(4, ws, xt, us).then_inc(lev_p, 1)

                pe.wait_ge(lev_v, LV.at("xt1", l * len(LEVELS) + len(LEVELS) - 1))
                pe.wait_ge(rw_a, RA.at("bhct", l))
                for c in range(NC_):
                    step = l * NC_ + c

                    def sums(out, pairs):
                        for j in range(QT):
                            for h in range(2):
                                rows = slice(h * HD, h * HD + HD)
                                for i, (left, right) in enumerate(pairs):
                                    mm = nc.tensor.matmul(out(j, rows), left(j, rows), right(j, rows), start=(i == 0),
                                                          stop=(i == len(pairs) - 1))
                        return mm

                    def here(v):
                        return lambda j, rows: v[rows, j, c * CHUNK:(c + 1) * CHUNK]

                    old = lambda j, rows: state[rows, c % 2, j, :]
                    narrow = lambda bank: lambda j, rows: ps[rows, bank, j * HD:(j + 1) * HD]
                    if c:
                        pe.wait_ge(ch_v, CV.at("s", step - 1))
                    carried = [(here(kt), old)] if c else []
                    sums(narrow(0), [(here(mt), here(v_t))] + carried).then_inc(ch_p, 1)
                    pe.wait_ge(ch_a, step + 1)
                    sums(narrow(1), [(here(xt), here(rr))]).then_inc(ch_p, 1)
                    pe.wait_ge(ch_v, CV.at("nu", step))
                    sums(narrow(4), [(here(khc_t), here(v_t)), (here(bhc_t), here(nu))]).then_inc(ch_p, 1)
                    carried = [(here(rt), old)] if c else []
                    sums(lambda j, rows: ps[rows, 2 + j // 2, j % 2 * T + c * CHUNK:j % 2 * T + (c + 1) * CHUNK],
                         carried + [(here(mrt), here(v_t)), (here(art), here(nu))]).then_inc(ch_p, 1)
                pe.wait_ge(rw_v, RV.at("yn", l))
                for u in range(UNITS):
                    j, c = u // NC_, u % NC_
                    mm = nc.tensor.transpose(ps[0:64, 4 + u // 4, u % 4 * P:(u % 4 + 1) * P],
                                             yy[:, j, c * CHUNK:(c + 1) * CHUNK], ident)
                mm.then_inc(rw_p, 1)

                pe.wait_ge(rw_v, RV.at("ya", l))
                pe.wait_ge(ml_v, MVS.at("yb", l))
                for n in range(KD):
                    c = chunk0[f"br{l}"] + n // 2
                    if n % 2 == 0:
                        chunk_here(c, c % 2)
                    if n >= 2:
                        pe.wait_ge(br_free, l * KD + n - 1)
                    for part, y in enumerate((ya, yb)):
                        for k in range(QT):
                            mm = nc.tensor.matmul(ps[:, 4 + n % 2, part * T:(part + 1) * T],
                                                  ring_a[:, c % 2, n % 2, part * QT + k, :], y[:, k, :],
                                                  start=(k == 0), stop=(k == QT - 1))
                    mm.then_inc(a_used if n % 2 else br_ready, 1)
                pe.wait_ge(br_free, (l + 1) * KD)
                for n in range(KD // 2):
                    c = chunk0[f"out2{l}"] + n
                    chunk_here(c, c % 2)
                    for i in range(2):
                        for k in range(KD):
                            mm = nc.tensor.matmul(ps[:, n, i * T:(i + 1) * T], ring_a[:, c % 2, i, k, :], umix[:, k, :],
                                                  start=(k == 0), stop=(k == KD - 1))
                    mm.then_inc(a_used, 1)
                norm(("ffn2", l, 0))
                pe.wait_ge(norm_out, n_id[("ffn2", l, 0)] + 1)
                ffn(4 + 2 * l, hn)
            norm(("final", 0, 0))


def tiles_of(w):
    k, n = w.shape
    return w.reshape(k // P, P, n // P, P).transpose(2, 1, 0, 3)


def chunks_of(tiles):
    if len(tiles) % 2:
        tiles = np.concatenate([tiles, np.zeros_like(tiles[:1])])
    n, p, k, c = tiles.shape
    return tiles.reshape(n // 2, 2, p, k, c).transpose(0, 2, 1, 3, 4).reshape(n // 2, p, -1)


def columns(v):
    return np.asarray(v).reshape(-1, P).T


def lay_out(a):
    zeros = lambda *s: np.zeros(s, np.float32)
    ffn_chunks = lambda g, u: np.stack([tiles_of(g), tiles_of(u)], 1).reshape(-1, P, KD, P)
    wa = [chunks_of(tiles_of(a["w_ada"][l])) for l in range(LAYERS)]
    q_heads = [h for j in range(4) for h in (j, j + 4)]
    q_cols = np.concatenate([np.arange(h * HD, h * HD + HD) for h in q_heads])
    for l in range(LAYERS):
        w = a["w_in"][l]
        w = np.concatenate([w[:, 512:640], w[:, q_cols], w[:, 640:768], w[:, 768:1280]], 1)
        w_out = np.concatenate([a["w_out"][l][q_cols], a["w_out"][l][512:]], 0)
        wa += [chunks_of(tiles_of(w)), chunks_of(tiles_of(w_out)),
               chunks_of(ffn_chunks(a["w_gate"][l], a["w_up"][l]))]
    small, mus = [], []
    for l in range(LAYERS):
        w = a["w_in_2"][l]
        at = 0
        part = {}
        for name, n in (("r", 512), ("k", 512), ("v", 512), ("xw", 64), ("xa", 64), ("xg", 160), ("mq", 512),
                        ("mk", 512), ("mv", 512), ("mo", 512), ("mi", 4), ("mf", 4), ("g", 2048)):
            part[name] = w[:, at:at + n]
            at += n
        down = a["vres_down_2"][l - 1] if l else zeros(D, 32)
        misc = np.concatenate([part["xg"][:, P:], part["mi"], zeros(D, 28), part["mf"], zeros(D, 28), down], 1)
        w = np.concatenate([part["r"], part["k"], part["v"], part["xw"], part["xa"], part["xg"][:, :P], misc,
                            part["mq"], part["mk"], part["mo"], part["g"], part["mv"]], 1)
        br = np.concatenate([tiles_of(a["br_a_2"][l]), tiles_of(a["br_b_2"][l])], 2)
        f1, f2 = a["ffn1_w_in_2"][l], a["ffn2_w_in_2"][l]
        wa += [chunks_of(ffn_chunks(f1[:, :FFN], f1[:, FFN:])), chunks_of(tiles_of(w)), chunks_of(br),
               chunks_of(tiles_of(a["w_out_2"][l])), chunks_of(ffn_chunks(f2[:, :FFN], f2[:, FFN:]))]
        up = a["vres_up_2"][l - 1] if l else zeros(32, 512)
        g_up = a["rw_g_up_2"][l]
        small.append(np.concatenate([np.concatenate([a["rw_w_up_2"][l], a["rw_a_up_2"][l]], 0), g_up[:P],
                                     np.concatenate([g_up[P:], zeros(64, 512), up], 0)], 1))
        mu = a["shift_mu_2"][l]
        mus.append(np.concatenate([mu, zeros(96)]))
    wd = np.concatenate([a["w_down"], np.stack([a[f"ffn{i}_w_out_2"][l] for l in range(LAYERS) for i in (1, 2)])])
    wd = wd.reshape(-1, P, D)

    vec = {"c": np.stack([a["c"][0].reshape(KD, P), a["c_ctx"].reshape(KD, P)], 1).reshape(-1, P).T,
           "b_ada": columns(a["b_ada"].reshape(-1)), "final": columns(a["final_norm_2"]),
           "vbias1": columns(a["vres_bias_2"][0]),
           "sink": np.broadcast_to(a["sink"].reshape(1, -1), (P, LAYERS * 8))}
    for l in range(LAYERS):
        for name, src in (("pre_mix", "norm_pre_mix"), ("post_mix", "norm_post_mix"), ("pre_ffn", "norm_pre_ffn"),
                          ("post_ffn", "norm_post_ffn"), ("ffn1", "ffn1_norm_2"), ("mix", "mix_norm_2"),
                          ("ffn2", "ffn2_norm_2"), ("conv_b", "ml_conv_b_2"), ("w0", "rw_w0_2"), ("a0", "rw_a0_2"),
                          ("k_k", "rw_k_k_2"), ("k_a", "rw_k_a_2"), ("r_k", "rw_r_k_2"), ("gn_w", "rw_gn_w_2"),
                          ("gn_b", "rw_gn_b_2"), ("ml_w", "ml_norm_w_2")):
            vec[f"{name}{l}"] = columns(a[src][l].reshape(-1))
        for t in range(4):
            vec[f"tap{t}{l}"] = columns(a["ml_conv_w_2"][l, t])
        vec[f"mu{l}"] = columns(mus[l])
        for name, src in (("ib", "ml_i_bias_2"), ("fb", "ml_f_bias_2")):
            vec[f"{name}{l}"] = np.concatenate([a[src][l], zeros(P - 4)])[:, None]
    vec = np.concatenate([vec[n] for n in V], 1)
    four = np.zeros((LAYERS, QT, 2, HD, 2, HD), np.float32)
    w4 = a["w_fourier"].reshape(LAYERS, QT, 2, HD, HD)
    for h in range(2):
        four[:, :, h, :, h, :] = w4[:, :, h]
    four = four.reshape(LAYERS * QT, P, P).transpose(1, 0, 2).reshape(P, -1)
    c1, c2 = constants()
    rows = lambda v: np.asarray(v[0]).T.reshape(KD, P, T).transpose(1, 0, 2)
    full = np.ascontiguousarray
    return {"wa": full(np.concatenate(wa)), "wd": full(wd), "c1": full(c1), "c2": full(c2), "vec": full(vec),
            "small": full(np.stack(small)), "four": full(four), "x": full(rows(a["x"])), "ctx": full(rows(a["ctx"]))}


def kernel(**inputs):
    import concourse.bacc as bacc
    from concourse.bass_utils import run_bass_kernel_spmd

    arrays = lay_out({n: np.asarray(v) for n, v in inputs.items()})
    nc = bacc.Bacc("TRN2", target_bir_lowering=False, num_devices=1)
    args = [nc.dram_tensor(f"in_{n}", v.shape, F32, kind="ExternalInput").ap() for n, v in arrays.items()]
    out = nc.dram_tensor("out", (P, KD, T), F32, kind="ExternalOutput").ap()
    program(nc, *args, out)
    got = run_bass_kernel_spmd(nc, [{f"in_{n}": v for n, v in arrays.items()}], core_ids=[0])
    return np.ascontiguousarray(got.results[0]["out"].transpose(2, 1, 0).reshape(1, T, D))
```

```python
from contextlib import ExitStack

import numpy as np

import concourse.bass as bass
from concourse import mybir

F32 = mybir.dt.float32
F32R = mybir.dt.float32r
ALU = mybir.AluOpType
ACT = mybir.ActivationFunctionType
AX_X = mybir.AxisListType.X

P = 128
D = 1024
T = 256
KD = D // P
LAYERS = 2
FFN = 2816
FT = FFN // P
NMOD = 6 * KD
HD = 64
QT = 4
CHUNK = 64
NC_ = T // CHUNK
UNITS = QT * NC_
RMS_EPS, GN_EPS, ML_EPS = 1e-6, 64e-5, 1e-5

R0, K0, V0, XWA, XG, MISC, MQ, MK, MO, GA, GB, MV = 0, 4, 8, 12, 13, 14, 15, 19, 23, 27, 35, 43
ZT = MV
MIXED = MISC + 1
XG2, IROW, FROW, VROW = 0, 32, 64, 96

A_ADA = 0
ADA = NMOD // 2
A_B1 = [LAYERS * NMOD // 2]
PROJ1, OUT1 = 5, 4
B1_LAYER = PROJ1 + OUT1 + FT
A_B1.append(A_B1[0] + B1_LAYER)
PROJ2, BR2, OUT2 = 24, 4, 4
B2_LAYER = FT + PROJ2 + BR2 + OUT2 + FT
A_B2 = [A_B1[1] + B1_LAYER, A_B1[1] + B1_LAYER + B2_LAYER]
N_A = A_B2[1] + B2_LAYER


WORK = 33200


def spans(widths):
    at, out = 0, {}
    for name, w in widths:
        out[name] = (at, at + w)
        at += w
    return out, at


C1, C1_N = spans([("cos", T), ("sin", T), ("rot", P), ("dft", 2 * 2 * T), ("chc", P), ("chs", P),
                  ("win", 2 * 2 * T)])
LEVELS = [2, 4, 8, 16, 32]
C2, C2_N = spans([("ident", P), ("ones", P), ("headones", P), ("headsum", QT * 8), ("headrow", QT * P),
                  ("restart", T), ("strict", CHUNK), ("incl", CHUNK), ("low1", CHUNK), ("up1", CHUNK),
                  ("eye", CHUNK)] + [(f"lev{m}", CHUNK) for m in LEVELS]
                 + [("tri", T + P), ("seli", 4), ("self", 4),
                    ("eps_rms", 1), ("eps_gn", 1), ("eps_ml", 1), ("one", 1)])
V, V_N = spans([("c", 2 * KD), ("b_ada", LAYERS * NMOD)]
               + [(f"{n}{l}", KD) for n in ("pre_mix", "post_mix", "pre_ffn", "post_ffn", "ffn1", "mix", "ffn2",
                                            "conv_b", "tap0", "tap1", "tap2", "tap3") for l in range(LAYERS)]
               + [("final", KD)]
               + [(f"mu{l}", MIXED) for l in range(LAYERS)]
               + [(f"{n}{l}", QT) for n in ("w0", "a0", "k_k", "k_a", "r_k", "gn_w", "gn_b", "ml_w")
                  for l in range(LAYERS)]
               + [("vbias1", QT)] + [(f"{n}{l}", 1) for n in ("ib", "fb") for l in range(LAYERS)]
               + [("sink", LAYERS * 8)])
SM, SM_N = spans([("waup", 512), ("gup", 512), ("mup", 512)])


def constants():
    pos = np.arange(T)
    rows = T // 64
    row = np.repeat(np.arange(rows), 64).astype(np.float32)
    col = np.tile(np.arange(64), rows).astype(np.float32)
    freqs = (np.float32(10000.0) ** (-np.arange(16, dtype=np.float32) / np.float32(16))).astype(np.float32)
    ang = np.concatenate([row[:, None] * freqs, col[:, None] * freqs], axis=-1)
    pair = (np.arange(P) % HD) // 2
    rot = np.zeros((P, P))
    even = np.arange(0, P, 2)
    rot[even + 1, even] = -1.0
    rot[even, even + 1] = 1.0
    turn = 2 * np.pi * np.outer(pos, pos) % (2 * np.pi * T) / T
    dft = np.concatenate([np.cos(turn), np.sin(turn)], 1).reshape(2, P, 2 * T).transpose(1, 0, 2).reshape(P, -1)
    ch = 2 * np.pi * (np.outer(np.arange(HD), np.arange(HD)) % HD) / HD
    norm = 1.0 / np.sqrt(T * HD)
    two = np.kron(np.eye(2), np.ones((HD, HD)))
    chc, chs = (np.kron(np.eye(2), f(ch) * norm) for f in (np.cos, np.sin))
    win = np.zeros((P, 2, 2 * T))
    for b in range(2):
        q = b * P + np.arange(P)
        win[:, b, :T] = np.where(np.abs(q[:, None] - pos[None]) <= 128, 0.0, -1e30)
    c1 = dict(cos=np.cos(ang).T[pair], sin=np.sin(ang).T[pair], rot=rot, dft=dft, chc=chc, chs=-chs,
              win=win.reshape(P, -1))
    s = (np.arange(P) % CHUNK)[:, None]
    t = np.arange(CHUNK)[None]
    tall = lambda m: np.broadcast_to(m, (P, CHUNK)).astype(np.float32)
    block = lambda m: tall((s // (2 * m) == t // (2 * m)) & (s // m % 2 == 0) & (t // m % 2 == 1))
    headsum = np.zeros((P, QT, 8))
    headrow = np.zeros((P, QT, P))
    for j in range(QT):
        for h in range(2):
            headsum[h * HD:(h + 1) * HD, j, 2 * j + h] = 1.0
            headrow[2 * j + h, j, h * HD:(h + 1) * HD] = 1.0
    tri = np.zeros((P, T + P))
    later = np.where(np.arange(P)[:, None] <= np.arange(P)[None], 0.0, -1e30)
    tri[:, :P] = later
    tri[:, T:] = later
    seli, self_ = np.zeros((P, 4)), np.zeros((P, 4))
    for h in range(4):
        seli[IROW + h, h] = 1.0
        self_[FROW + h, h] = 1.0
    c2 = dict(ident=np.eye(P), ones=np.ones((P, P)), headones=two, headsum=headsum.reshape(P, -1),
              headrow=headrow.reshape(P, -1),
              restart=np.broadcast_to((pos % CHUNK != 0).astype(np.float32), (P, T)),
              strict=tall(s < t), incl=tall(s <= t), low1=tall((s == t + 1) & (t % 2 == 0)), up1=block(1),
              eye=tall(s == t), tri=tri, seli=seli,
              eps_rms=np.full((P, 1), RMS_EPS), eps_gn=np.full((P, 1), GN_EPS), eps_ml=np.full((P, 1), ML_EPS),
              one=np.ones((P, 1)), **{f"lev{m}": block(m) for m in LEVELS}, **{"self": self_})
    side = lambda part, where: np.concatenate([part[n] for n in where], 1).astype(np.float32)
    return side(c1, C1), side(c2, C2)


class Steps:

    def __init__(self, names):
        self.place = {n: i + 1 for i, n in enumerate(names)}
        self.count = len(names)

    def at(self, name, rnd):
        return rnd * self.count + self.place[name]


def program(nc, wa, wd, c1_in, c2_in, vec_in, small_in, four_in, x_in, ctx_in, out):
    with ExitStack() as ctx:
        def sb(name, *shape, dtype=F32):
            return ctx.enter_context(nc.sbuf_tensor(name, [P, *shape], dtype))

        def sem(name):
            return ctx.enter_context(nc.semaphore(name))

        ring_a = sb("ring_a", 2, 2, KD, P)
        ring_d = sb("ring_d", 2, KD, P)
        x = sb("x", KD, T)
        hn = sb("hn", KD, T)
        nsq = sb("nsq", KD, T)
        nrt = sb("nrt", T)
        rstd = sb("rstd", T)
        sg = sb("sg", 2, T)
        hid = sb("hid", 2, T)
        c2 = sb("c2", C2_N)
        vec = sb("vec", V_N)
        mod = sb("mod", LAYERS * NMOD, 2)
        gain = sb("gain", LAYERS, 4, KD, 2)
        cs = sb("cs", KD, 2)
        omka = sb("omka", LAYERS * QT)
        ada_rows = sb("ada_rows", 2, 2 * P)
        vfirst = sb("vfirst", QT, T)
        with nc.sbuf_tensor("work", [P, WORK], F32) as work:
            pass
        w_hi, w_lo = (sb(n, 2, 2, KD, P, dtype=F32R) for n in ("w_hi", "w_lo"))
        d_hi, d_lo = (sb(n, 2, KD, P, dtype=F32R) for n in ("d_hi", "d_lo"))
        h_hi, h_lo = (sb(n, KD, T, dtype=F32R) for n in ("h_hi", "h_lo"))
        hid_hi, hid_lo = (sb(n, 2, T, dtype=F32R) for n in ("hid_hi", "hid_lo"))
        SPLIT = 3 * 2 * 2 * KD * P + 2 * KD * T + 2 * 2 * T
        ps = ctx.enter_context(nc.psum_tensor("ps", [P, 8, 512], F32))

        def const(name):
            return c2[:, C2[name][0]:C2[name][1]]

        def vcol(name, k):
            return vec[:, V[name][0] + k:V[name][0] + k + 1]

        top = [0]

        def place(*shape):
            n = int(np.prod(shape))
            v = work[:, top[0]:top[0] + n]
            top[0] += n
            assert top[0] <= WORK, top[0]
            if len(shape) == 1:
                return v
            if len(shape) == 2:
                return v.rearrange("p (a b) -> p a b", b=shape[1])
            return v.rearrange("p (a b c) -> p a b c", b=shape[1], c=shape[2])

        def units(v):
            return v.rearrange("p j (c t) -> p (j c) t", t=CHUNK)

        h2 = place(KD, 2 * T)
        rtmp = place(5, T)
        qr = place(QT, T)
        kall = place(2 * T)
        v_tok = place(4, P)
        s_sb = place(2, 2 * T)
        probs = place(2, 2 * T)
        pn = place(2, 2 * T)
        pt = place(2, 4, P)
        tiny = place(2, 8)
        fu = place(QT, 2 * T)
        fm = place(QT, T)
        mixin = place(KD, 2 * T)
        assert top[0] >= SPLIT
        xc = place(KD, T)
        shared = top[0]
        raw = place(5, 2 * T)
        u_tok = place(4, 512)
        top[0] = max(top[0], shared + KD * 2 * T)
        mix = work[:, shared:shared + KD * 2 * T].rearrange("p (a b) -> p a b", b=2 * T)
        c1 = place(C1_N)
        wfour = place(LAYERS * QT, P)

        def const1(name):
            return c1[:, C1[name][0]:C1[name][1]]

        top[0] = 0
        S_ = [place(QT, T) for _ in range(12)]
        lw, aa, vg, gg, bon, lcum, e1, e2, e0, kk, bb, tmp = S_
        slot0 = top[0]
        diff = work[:, slot0:slot0 + 15 * T].rearrange("p (a b) -> p a b", b=T)
        at_, mt, mrt, art, ws, aoff = (place(QT, T) for _ in range(6))
        assert top[0] >= SPLIT
        z = place(ZT, T + 1)
        mv = place(2, 512)
        small = place(SM_N)
        state = place(2, QT, HD)
        sdec = place(QT, HD)
        kt, bh, kh, khc, bhc = kk, bb, e0, lw, aa
        khc_t, bhc_t, v_t = vg, lcum, e2
        xs, xt = tmp, khc
        rr, nu, yy, yq = ws, aoff, at_, xs
        small_y = place(8, UNITS)
        am = work[:, slot0:slot0 + 2 * 384].rearrange("p (a b) -> p a b", b=384)
        ee = work[:, slot0 + 768:slot0 + 2 * 768].rearrange("p (a b) -> p a b", b=384)
        pm = work[:, slot0 + 1536:slot0 + 3 * 768].rearrange("p (a b) -> p a b", b=384)
        dn = work[:, slot0 + 2304:slot0 + 2304 + 512].rearrange("p (a b) -> p a b", b=T)
        ems = work[:, slot0 + 2816:slot0 + 2816 + 512].rearrange("p (a b) -> p a b", b=T)
        hN = work[:, slot0 + 3328:slot0 + 3328 + 1024].rearrange("p (a b) -> p a b", b=T)
        hc = work[:, slot0 + 4352:slot0 + 4352 + 1024].rearrange("p (a b) -> p a b", b=T)
        rows4 = z[:, MQ:MQ + 2 * QT, 1:T + 1]
        ya, yb = gg, bhc
        inv_norm = rows4[0:8, 0, :]
        umix = nsq

        a_loaded = [sem("a_loaded0"), sem("a_loaded1")]
        d_loaded = [sem("d_loaded0"), sem("d_loaded1")]
        a_used, d_used = sem("a_used"), sem("d_used")
        in_loaded, const_loaded, small_loaded, out_stored = (
            sem(n) for n in ("in_loaded", "const_loaded", "small_loaded", "out_stored"))
        cs_ready, ada_row, ada_turned, ada_free, gain_ready = (
            sem(n) for n in ("cs_ready", "ada_row", "ada_turned", "ada_free", "gain_ready"))
        norm_sq, norm_sum, norm_rt, norm_rstd, norm_scaled, norm_out = (
            sem(n) for n in ("norm_sq", "norm_sum", "norm_rt", "norm_rstd", "norm_scaled", "norm_out"))
        proj_ready, proj_free = sem("proj_ready"), sem("proj_free")
        hi_a, hi_d, v_ready, hh_ready, hl_ready = (
            sem(n) for n in ("hi_a", "hi_d", "v_ready", "hh_ready", "hl_ready"))
        gu_done, dn_done, sg_ready, hid_mul, hid_rounded, hid_ready, ffn_out = (
            sem(n) for n in ("gu_done", "dn_done", "sg_ready", "hid_mul", "hid_rounded", "hid_ready", "ffn_out"))
        resid = sem("resid")
        rope_rot, rope_sin, rope_cos, rope_out = (sem(n) for n in ("rope_rot", "rope_sin", "rope_cos", "rope_out"))
        fo_dft, fo_fu, fo_ch, fo_fm, fo_w, fo_out = (
            sem(n) for n in ("fo_dft", "fo_fu", "fo_ch", "fo_fm", "fo_w", "fo_out"))
        at_sc, at_s, at_mx, at_nm, at_exp, at_den, at_rd, at_pn, at_tr, at_pt, at_pv, at_o = (
            sem(f"at_{n}") for n in ("sc", "s", "mx", "nm", "exp", "den", "rd", "pn", "tr", "pt", "pv", "o"))
        z_zero, kab = sem("z_zero"), sem("kab")
        rw_v, rw_a, rw_p, vres_v, vres_a, vres_p, lev_v, lev_a, lev_p, lev_g, ch_v, ch_a, ch_p = (
            sem(n) for n in ("rw_v", "rw_a", "rw_p", "vres_v", "vres_a", "vres_p", "lev_v", "lev_a", "lev_p", "lev_g",
                             "ch_v", "ch_a", "ch_p"))
        ml_v, ml_a, ml_p = (sem(n) for n in ("ml_v", "ml_a", "ml_p"))
        mh_arg, mh_s, mh_em, mh_nd, mh_am, mh_pm, mh_ee, mh_ems, mh_dn, mh_abs, mh_rc, mh_h = (
            sem(f"mh_{n}") for n in ("arg", "s", "em", "nd", "am", "pm", "ee", "ems", "dn", "abs", "rc", "h"))
        br_ready, br_part, br_free = (sem(n) for n in ("br_ready", "br_part", "br_free"))

        RV = Steps(["diff", "mix", "lw", "scan", "kk", "kq", "rnmax", "rn", "kkn", "b", "ka", "kp", "rkr", "bon", "l0",
                    "kt", "bh", "kh", "rt", "khc", "bhc", "at", "x1", "xt1", "mt", "x", "xt",
                    "mrt", "art", "s1", "ym", "yc", "yq", "s2", "yr", "yn", "gn", "gb", "ya"])
        RA = Steps(["tanh", "sgx", "sw", "aa", "gg", "rsq", "e0", "e1", "e2", "vt", "khct", "bhct", "ysd", "yT"])
        RP = Steps(["lw", "la", "lg", "ss", "rnb", "bon", "vt", "khct", "bhct", "at", "a", "mt", "mrt", "art", "yT"])
        VV = Steps(["d", "m", "v"])
        LP = Steps(["w0", "w1", "x0", "x1"])
        LV = Steps(["x0", "xt0", "x1", "xt1"])
        LA = Steps(["w0", "w1"])
        CP = Steps(["r", "u", "s", "y"])
        CV = Steps(["dec", "nu", "s"])
        MVS = Steps(["c0", "c1", "c2", "c3", "mn", "lf", "F", "g", "M", "nm", "fm", "hc", "rec", "hs", "yb"])
        MA = Steps(["silu", "so", "ab", "ex", "ln", "hq", "hsd", "gates"])
        MP = Steps(["if", "mu", "var"])

        n_id = {}
        order = []
        for l in range(LAYERS):
            order += [("pre_mix", l, 0), ("pre_mix", l, 1)]
            order += [("post_mix", l, 0), ("pre_ffn", l, 0), ("post_ffn", l, 0)]
            if l == 0:
                order += [("post_mix", l, 1), ("pre_ffn", l, 1), ("post_ffn", l, 1)]
        for l in range(LAYERS):
            order += [("ffn1", l, 0), ("mix", l, 0), ("ffn2", l, 0)]
        order.append(("final", 0, 0))
        n_two = {}
        for i, key in enumerate(order):
            n_id[key] = i
            if key[0] in ("pre_mix", "post_mix", "post_ffn"):
                n_two[key] = len(n_two)
        ffns = [(0, 0), (0, 1), (1, 0)] + [(2, 0), (3, 0), (4, 0), (5, 0)]
        a_dram_ffn = [A_B1[0] + PROJ1 + OUT1, A_B1[1] + PROJ1 + OUT1,
                      A_B2[0], A_B2[0] + FT + PROJ2 + BR2 + OUT2, A_B2[1], A_B2[1] + FT + PROJ2 + BR2 + OUT2]
        stages = [("ada0", A_ADA, ADA, None)]
        for l in range(LAYERS):
            stages.append((f"proj1{l}", A_B1[l], PROJ1, None))
            if l == 0:
                stages.append(("ada1", A_ADA + ADA, ADA, None))
            stages.append((f"out1{l}", A_B1[l] + PROJ1, OUT1, None))
            for call in ([0, 1] if l == 0 else [2]):
                stages.append((f"ffn{call}", a_dram_ffn[ffns[call][0]], FT, call))
        for l in range(LAYERS):
            base = A_B2[l] + FT
            stages += [(f"ffn{3 + 2 * l}", A_B2[l], FT, 3 + 2 * l),
                       (f"proj2{l}", base, PROJ2, None), (f"br{l}", base + PROJ2, BR2, None),
                       (f"out2{l}", base + PROJ2 + BR2, OUT2, None),
                       (f"ffn{4 + 2 * l}", base + PROJ2 + BR2 + OUT2, FT, 4 + 2 * l)]
        chunk0, n = {}, 0
        for name, _, count, _ in stages:
            chunk0[name] = n
            n += count
        tile0, first0, n, m = {}, {}, 0, 0
        for name, count in ([(f"{s}1{l}", t) for l in range(LAYERS) for s, t in (("proj", 10), ("out", KD))]
                            + [(f"proj2{l}", ZT + QT) for l in range(LAYERS)]):
            tile0[name], first0[name] = n, m
            n += count
            m += count // 2

        ADA_STEPS = range(2, 2 + ADA // 2)

        def ada_chunk(which, u):
            return which * (ADA // 2) + u - 2

        def wait(eng, semaphore, value, i=None):
            if i is not None:
                eng.wait_ge(semaphore, i * 2 + value)
            elif value > 0:
                eng.wait_ge(semaphore, value)

        def shift_of(l, part, which):
            return lambda k: mod[:, l * NMOD + part * KD + k, which:which + 1]

        def gain_of(l, i, which):
            return lambda k: gain[:, l, i, k, which:which + 1]

        def token_cols(l, which):
            return slice(which * T, which * T + T)

        block = ctx.enter_context(nc.Block())

        @block.sync
        def _(sp):
            sp.dma_start(x[:, :, :], x_in).then_inc(in_loaded, 16)
            sp.dma_start(xc, ctx_in).then_inc(in_loaded, 16)

            def load_a(c, slot, src, wait=True):
                if wait:
                    sp.wait_ge(a_used, c - 1)
                sp.dma_start(ring_a[:, slot].rearrange("p a b c -> p (a b c)"), src).then_inc(a_loaded[slot], 16)

            def load_d(d, slot, src, wait=True):
                if wait:
                    sp.wait_ge(d_used, d - 1)
                sp.dma_start(ring_d[:, slot].rearrange("p a b -> p (a b)"), src).then_inc(d_loaded[slot], 16)

            for name, first, count, call in stages:
                c0 = chunk0[name]
                if call is None:
                    i = 0
                    if c0 == 0:
                        load_a(0, 0, wa[first], wait=False)
                        load_a(1, 1, wa[first + 1], wait=False)
                        i = 2
                    pairs = (count - i) // 2
                    if pairs:
                        with sp.Fori(0, pairs) as n:
                            for u in range(2):
                                load_a(n * 2 + (c0 + i + u), (c0 + i + u) % 2,
                                       wa[bass.ds(n * 2 + (first + i + u), 1)].rearrange("a p n -> (a p) n"))
                    if (count - i) % 2:
                        load_a(c0 + count - 1, (c0 + count - 1) % 2, wa[first + count - 1])
                    continue
                d0, dd = call * FT, ffns[call][0] * FT
                load_a(c0, c0 % 2, wa[first])
                load_a(c0 + 1, (c0 + 1) % 2, wa[first + 1])
                load_d(d0, d0 % 2, wd[dd], wait=call > 0)
                load_a(c0 + 2, c0 % 2, wa[first + 2])
                load_d(d0 + 1, (d0 + 1) % 2, wd[dd + 1], wait=call > 0)
                with sp.Fori(0, (FT - 4) // 2) as n:
                    for u in range(2):
                        load_a(n * 2 + (c0 + 3 + u), (c0 + 3 + u) % 2,
                               wa[bass.ds(n * 2 + (first + 3 + u), 1)].rearrange("a p n -> (a p) n"))
                        load_d(n * 2 + (d0 + 2 + u), (d0 + 2 + u) % 2,
                               wd[bass.ds(n * 2 + (dd + 2 + u), 1)].rearrange("a p n -> (a p) n"))
                load_a(c0 + FT - 1, (c0 + FT - 1) % 2, wa[first + FT - 1])
                for f in (FT - 2, FT - 1):
                    load_d(d0 + f, (d0 + f) % 2, wd[dd + f])
            sp.wait_ge(norm_out, n_id[("final", 0, 0)] + 1)
            sp.dma_start(out, hn[:, :, :]).then_inc(out_stored, 16)
            sp.wait_ge(out_stored, 16)

        @block.gpsimd
        def _(pool):
            pool.wait_ge(norm_out, n_id[("post_ffn", 1, 0)] + 1)
            pool.wait_ge(fo_out, 3 * QT)
            nc.gpsimd.memset(z[:, :, 0:1], 0.0).then_inc(z_zero, 1)
            for l in range(LAYERS):
                if l:
                    pool.wait_ge(rw_p, RP.at("lg", l - 1))
                pool.dma_start(small, small_in[l]).then_inc(small_loaded, 16)
                for i, m in enumerate(LEVELS):
                    step = l * len(LEVELS) + i
                    if step:
                        pool.wait_ge(lev_p, LP.at("w1", step - 1))
                    if i == 0:
                        pool.wait_ge(rw_v, RV.at("art", l))
                    nc.gpsimd.tensor_tensor(
                        units(aoff), units(at_), const(f"lev{m}")[:, None, :].to_broadcast([P, UNITS, CHUNK]),
                        ALU.mult).then_inc(lev_g, 1)

        @block.scalar
        def _(act):
            act.dma_start(c2[:, :], c2_in).then_inc(const_loaded, 16)
            act.dma_start(vec[:, :], vec_in).then_inc(const_loaded, 16)
            act.dma_start(c1, c1_in).then_inc(const_loaded, 16)
            act.dma_start(wfour.rearrange("p a b -> p (a b)"), four_in).then_inc(const_loaded, 16)
            act.wait_ge(const_loaded, 64)
            nc.scalar.activation(cs[:, :, :].rearrange("p k w -> p (k w)"),
                                 vec[:, V["c"][0]:V["c"][1]], ACT.Silu).then_inc(cs_ready, 1)

            def norm(key, src, call=None):
                n = n_id[key]
                nc.scalar.activation(nsq[:, :, :], src, ACT.Square).then_inc(norm_sq, 1)
                if call is not None:
                    round_a(call, 0)
                act.wait_ge(norm_sum, n + 1)
                if n:
                    act.wait_ge(norm_rstd, n)
                nc.scalar.activation(nrt[:, :], ps[:, 6, 0:T], ACT.Sqrt, bias=const("eps_rms"),
                                     scale=1.0 / D).then_inc(norm_rt, 1)

            def round_a(call, f, i=None):
                c, t = chunk0[f"ffn{call}"] + f, call * FT + f
                n = 16 * (c // 2 + 1)
                act.wait_ge(a_loaded[c % 2], n if i is None else i * 16 + n)
                wait(act, gu_done, t - 1, i)
                for part in range(2):
                    nc.scalar.copy(w_hi[:, f % 2, part], ring_a[:, c % 2, part]).then_inc(hi_a, 1)

            def round_d(call, f, i=None):
                d = call * FT + f
                n = 16 * (d // 2 + 1)
                act.wait_ge(d_loaded[d % 2], n if i is None else i * 16 + n)
                wait(act, dn_done, d - 1, i)
                nc.scalar.copy(d_hi[:, f % 2], ring_d[:, d % 2]).then_inc(hi_d, 1)

            def ffn(call, modulated=None):
                for k in range(KD):
                    act.wait_ge(v_ready, call * KD + k + 1)
                    if modulated is None:
                        nc.scalar.copy(h_hi[:, k, :], hn[:, k, :]).then_inc(hh_ready, 1)
                    else:
                        gains, shift = modulated
                        nc.scalar.activation(nsq[:, k, :], hn[:, k, :], ACT.Identity, scale=gains(k), bias=shift(k))
                        nc.scalar.activation(h_hi[:, k, :], hn[:, k, :], ACT.Identity, scale=gains(k), bias=shift(k))\
                            .then_inc(hh_ready, 1)
                round_a(call, 1)
                round_d(call, 0)

                def tile(f, i=None):
                    t = call * FT + f
                    wait(act, gu_done, t + 1, i)
                    wait(act, hid_mul, t - 1, i)
                    nc.scalar.activation(sg[:, f % 2, :], ps[:, 4 + f % 2, 0:T], ACT.Silu).then_inc(sg_ready, 1)
                    if f + 2 < FT:
                        round_a(call, f + 2, i)
                    if f + 1 < FT:
                        round_d(call, f + 1, i)

                tile(0)
                tile(1)
                with act.Fori(0, FT // 2 - 2) as i:
                    tile(2, i)
                    tile(3, i)
                tile(FT - 2)
                tile(FT - 1)

            def tile_ready(stage, i):
                if i % 2 or i == ZT + QT - 1:
                    act.wait_ge(a_used, chunk0[stage] + i // 2 + 1)
                else:
                    act.wait_ge(proj_ready, first0[stage] + i // 2 + 1)

            def empty(stage, i, dst, cols=slice(0, T)):
                tile_ready(stage, i)
                src = ps[:, 4 + (tile0[stage] + i) % 2, cols]
                if len(dst.shape) == 3:
                    src = src.rearrange("p (a b) -> p a b", b=P)
                nc.scalar.copy(dst, src).then_inc(proj_free, 1)

            def fourier(call, l, which):
                for j in range(QT):
                    act.wait_ge(fo_dft, call * QT + j + 1)
                    nc.scalar.copy(fu[:, j, :], ps[:, j, :]).then_inc(fo_fu, 1)
                for j in range(QT):
                    act.wait_ge(fo_ch, call * QT + j + 1)
                    nc.scalar.copy(fm[:, j, :], ps[:, j, 0:T]).then_inc(fo_fm, 1)
                for j in range(QT):
                    act.wait_ge(fo_w, call * QT + j + 1)
                    nc.scalar.copy(mixin[:, QT + j, token_cols(l, which)], ps[:, j, T:2 * T]).then_inc(fo_out, 1)

            def attention(call, l, which):
                n_keys = 2 * T if which == 0 else T

                def exps(u):
                    g, h = call * 16 + u, (u % 2) * 4 + (u // 2) % 4
                    act.wait_ge(at_nm, g + 1)
                    if g >= 2:
                        act.wait_ge(at_pn, g - 1)
                    nc.scalar.activation(probs[:, u % 2, 0:n_keys], s_sb[:, u % 2, 0:n_keys], ACT.Exp,
                                         bias=tiny[:, u % 2, 1:2], accum_out=tiny[:, u % 2, 2:3])
                    nc.scalar.activation(tiny[:, u % 2, 3:4], vcol("sink", l * 8 + h), ACT.Exp,
                                         bias=tiny[:, u % 2, 1:2]).then_inc(at_exp, 1)

                def turned(u):
                    g = call * 16 + u
                    act.wait_ge(at_tr, g + 1)
                    if g >= 2:
                        act.wait_ge(at_pv, g - 1)
                    nc.scalar.copy(pt[:, u % 2, 0:n_keys // P, :],
                                   ps[:, 2 + u % 2, 0:n_keys].rearrange("p (a b) -> p a b", b=P)).then_inc(at_pt, 1)

                def out_pair(w):
                    blk, j = w // 4, w % 4
                    act.wait_ge(at_pv, call * 16 + 2 * w + 2)
                    nc.scalar.copy(mixin[:, j, which * T + blk * P:which * T + (blk + 1) * P],
                                   ps[:, 6 + w % 2, 0:P]).then_inc(at_o, 1)

                for u in range(16 + 4):
                    if u < 16:
                        exps(u)
                    if 1 <= u <= 16:
                        turned(u - 1)
                    if u >= 4 and (u - 3) % 2:
                        out_pair((u - 4) // 2)
                    if l == 0 and u in ADA_STEPS:
                        ada(1, ada_chunk(which, u))

            def ada(l, n, i=None):
                c, u = chunk0[f"ada{l}"] + n, n % 2
                act.wait_ge(a_used, c + 1 if i is None else i * 2 + (c + 1))
                nc.scalar.copy(ada_rows[0:2, u, :], ps[0:2, 4 + u, 0:T]).then_inc(ada_row, 1)

            with act.Fori(0, ADA // 2) as i:
                ada(0, 0, i)
                ada(0, 1, i)
            act.wait_ge(in_loaded, 32)
            fcall = acall = 0
            for l in range(LAYERS):
                if l:
                    act.wait_ge(norm_out, n_id[("post_ffn", 0, 0)] + 1)
                norm(("pre_mix", l, 0), x[:, :, :])
                if l:
                    act.wait_ge(norm_out, n_id[("post_ffn", 0, 1)] + 1)
                norm(("pre_mix", l, 1), xc)
                stage, n_q, n_blk = f"proj1{l}", (2 * T, T)[l], (4, 2)[l]
                tile_ready(stage, 0)
                bank = 4 + tile0[stage] % 2
                nc.scalar.copy(raw[:, 0, 0:T], ps[:, bank, 0:T])
                nc.scalar.copy(kall[:, T:2 * T], ps[:, bank, T:2 * T]).then_inc(proj_free, 1)
                for j in range(QT):
                    empty(stage, 1 + j, raw[:, 1 + j, 0:n_q], slice(0, n_q))
                empty(stage, 1 + QT, v_tok, slice(0, 2 * T))
                for j in range(QT):
                    empty(stage, 2 + QT + j, u_tok[:, 0:n_blk, j * P:(j + 1) * P], slice(0, n_blk * P))
                for which in ([0, 1] if l == 0 else [0]):
                    fourier(fcall, l, which)
                    attention(acall, l, which)
                    fcall += 1
                    acall += 1
                for j in range(KD):
                    empty(f"out1{l}", j, mix[:, j, 0:n_q], slice(0, n_q))
                for which in ([0, 1] if l == 0 else [0]):
                    act.wait_ge(proj_free, tile0[f"out1{l}"] + KD)
                    norm(("post_mix", l, which), mix[:, :, token_cols(l, which)])
                    act.wait_ge(norm_out, n_id[("post_mix", l, which)] + 1)
                    call = 2 * l + which
                    norm(("pre_ffn", l, which), x[:, :, :] if which == 0 else xc, call)
                    ffn(call, (gain_of(l, 2, which), shift_of(l, 3, which)))
                    act.wait_ge(dn_done, (call + 1) * FT)
                    nc.scalar.copy(mix[:, :, token_cols(l, which)],
                                   ps[:, 0:4, :].rearrange("p a (b t) -> p (a b) t", t=T)).then_inc(ffn_out, 1)
                    act.wait_ge(ffn_out, call + 1)
                    norm(("post_ffn", l, which), mix[:, :, token_cols(l, which)])

            for l in range(LAYERS):
                if l == 0:
                    act.wait_ge(norm_out, n_id[("post_ffn", 1, 0)] + 1)
                else:
                    act.wait_ge(resid, 3 * l)
                norm(("ffn1", l, 0), x[:, :, :], 3 + 2 * l)
                ffn(3 + 2 * l)
                act.wait_ge(resid, 3 * l + 1)
                norm(("mix", l, 0), x[:, :, :])

                stage = f"proj2{l}"
                p0, c0, f0 = tile0[stage], chunk0[stage], first0[stage]
                if l == 0:
                    act.wait_ge(z_zero, 1)
                else:
                    act.wait_ge(br_free, KD * l)

                def tiles(first, count):
                    with act.Fori(0, count // 2) as i:
                        for u in range(2):
                            if u == 0:
                                act.wait_ge(proj_ready, i + (f0 + first // 2 + 1))
                            else:
                                act.wait_ge(a_used, i + (c0 + first // 2 + 1))
                            nc.scalar.activation(
                                z[:, bass.ds(i * 2 + (first + u), 1), 1:T + 1],
                                ps[:, 4 + (p0 + first + u) % 2, 0:T].rearrange("p (a b) -> p a b", a=1),
                                ACT.Copy).then_inc(proj_free, 1)

                tiles(0, 24)
                act.wait_ge(rw_v, RV.at("mix", l))
                nc.scalar.activation(tmp[0:64, 0, :], z[0:64, XWA, 1:T + 1], ACT.Tanh).then_inc(rw_a, 1)
                nc.scalar.activation(tmp[:, 1, :], z[:, XG, 1:T + 1], ACT.Sigmoid)
                nc.scalar.activation(tmp[0:32, 2, :], z[0:32, MISC, 1:T + 1], ACT.Sigmoid).then_inc(rw_a, 1)
                tiles(24, 8)
                act.wait_ge(rw_p, RP.at("lw", l))
                for j in range(QT):
                    ins = nc.scalar.activation(lw[:, j, :], ps[:, j // 2, j % 2 * T:j % 2 * T + T], ACT.Sigmoid,
                                               bias=vcol(f"w0{l}", j))
                ins.then_inc(rw_a, 1)
                act.wait_ge(rw_p, RP.at("la", l))
                for j in range(QT):
                    ins = nc.scalar.activation(aa[:, j, :], ps[:, 2 + j // 2, j % 2 * T:j % 2 * T + T], ACT.Sigmoid,
                                               bias=vcol(f"a0{l}", j))
                ins.then_inc(rw_a, 1)
                act.wait_ge(rw_p, RP.at("lg", l))
                nc.scalar.copy(gg, ps[:, 6:8, :].rearrange("p a (b t) -> p (a b) t", t=T)).then_inc(rw_a, 1)
                tiles(32, 4)
                if l:
                    act.wait_ge(vres_p, 1)
                    for j in range(QT):
                        ins = nc.scalar.activation(vg[:, j, :], ps[:, j // 2, j % 2 * T:j % 2 * T + T], ACT.Sigmoid,
                                                   bias=vcol("vbias1", j))
                    ins.then_inc(vres_a, 1)
                act.wait_ge(rw_p, RP.at("ss", l))
                nc.scalar.activation(tmp[0:8, 3, :], ps[0:8, 2, 0:T], ACT.Sqrt).then_inc(rw_a, 1)
                tiles(36, 6)
                empty(stage, ZT - 1, z[:, ZT - 1, 1:T + 1])
                for j in range(QT):
                    empty(stage, ZT + j, mv[:, :, j * P:(j + 1) * P])
                act.wait_ge(rw_v, RV.at("l0", l))
                nc.scalar.activation(e0, e0, ACT.Exp).then_inc(rw_a, 1)
                nc.scalar.activation(e1, lcum, ACT.Exp).then_inc(rw_a, 1)
                nc.scalar.activation(e2, lcum, ACT.Exp, scale=-1.0).then_inc(rw_a, 1)

                def to_tokens(dst, banks):
                    src = ps[:, banks:banks + 2, :].rearrange("p b (u c) -> p (b u) c", c=P)
                    d = units(dst).rearrange("p (u o) c -> p u o c", o=2)
                    for odd in range(2):
                        for h in range(2):
                            ins = nc.scalar.copy(d[h * 64:h * 64 + 64, :, odd, :],
                                                 src[odd * 64:odd * 64 + 64, :, h * 64:h * 64 + 64])
                    return ins

                act.wait_ge(ml_v, MVS.at("c3", l))
                nc.scalar.activation(nsq[:, :, :], nsq[:, :, :], ACT.Silu).then_inc(ml_a, 1)
                nc.scalar.activation(z[:, MO:MO + QT, 1:T + 1], z[:, MO:MO + QT, 1:T + 1], ACT.Sigmoid)\
                    .then_inc(ml_a, 1)
                act.wait_ge(rw_p, RP.at("vt", l))
                act.wait_ge(rw_v, RV.at("kh", l))
                to_tokens(v_t, 2).then_inc(rw_a, 1)
                act.wait_ge(ml_p, MP.at("if", l))
                nc.scalar.activation(rows4[0:4, 0, :], ps[0:4, 6, T:2 * T], ACT.Abs, bias=vcol(f"fb{l}", 0)[0:4])\
                    .then_inc(ml_a, 1)
                act.wait_ge(ml_a, MA.at("ab", l))
                nc.scalar.activation(rows4[0:4, 1, :], rows4[0:4, 0, :], ACT.Exp, scale=-1.0).then_inc(ml_a, 1)
                act.wait_ge(ml_a, MA.at("ex", l))
                nc.scalar.activation(rows4[0:4, 2, :], rows4[0:4, 1, :], ACT.Ln, bias=const("one")[0:4])\
                    .then_inc(ml_a, 1)
                act.wait_ge(rw_p, RP.at("khct", l))
                to_tokens(khc_t, 0).then_inc(rw_a, 1)
                act.wait_ge(rw_p, RP.at("bhct", l))
                to_tokens(bhc_t, 4).then_inc(rw_a, 1)
                for h in range(4):
                    r = l * 4 + h
                    act.wait_ge(mh_am, r + 1)
                    if r >= 2:
                        act.wait_ge(mh_pm, r - 1)
                    nc.scalar.activation(ee[:, h % 2, :], am[:, h % 2, :], ACT.Exp).then_inc(mh_ee, 1)
                    act.wait_ge(mh_em, r + 1)
                    if r >= 2:
                        act.wait_ge(mh_dn, r - 1)
                    nc.scalar.activation(ems[:, h % 2, :], ps[:, 4 + h % 2, 0:T], ACT.Exp, scale=-1.0)\
                        .then_inc(mh_ems, 1)
                act.wait_ge(ml_v, MVS.at("hc", l))
                nc.scalar.activation(hN, hc, ACT.Square).then_inc(ml_a, 1)
                act.wait_ge(ml_p, MP.at("var", l))
                nc.scalar.activation(yb, ps[:, 2:4, :].rearrange("p a (b t) -> p (a b) t", t=T), ACT.Sqrt,
                                     bias=const("eps_ml"), scale=1.0 / P).then_inc(ml_a, 1)
                nc.scalar.activation(z[:, GA:GA + 2 * KD, 1:T + 1], z[:, GA:GA + 2 * KD, 1:T + 1], ACT.Sigmoid)\
                    .then_inc(ml_a, 1)
                for i in range(len(LEVELS)):
                    step = l * len(LEVELS) + i
                    for half in range(2):
                        act.wait_ge(lev_p, LP.at(f"w{half}", step))
                        nc.scalar.copy(units(ws)[:, half * 8:half * 8 + 8, :],
                                       ps[:, half, :].rearrange("p (u t) -> p u t", t=CHUNK)).then_inc(lev_a, 1)
                for c in range(NC_):
                    step = l * NC_ + c
                    act.wait_ge(ch_p, CP.at("r", step))
                    nc.scalar.copy(rr[:, :, c * CHUNK:(c + 1) * CHUNK],
                                   ps[:, 0, 0:QT * HD].rearrange("p (j v) -> p j v", v=HD)).then_inc(ch_a, 1)
                act.wait_ge(rw_v, RV.at("s2", l))
                nc.scalar.activation(small_y[:, 4, :], small_y[:, 3, :], ACT.Sqrt, bias=const("eps_gn"),
                                     scale=1.0 / HD).then_inc(rw_a, 1)
                act.wait_ge(rw_p, RP.at("yT", l))
                src = ps[0:64, 4:8, :].rearrange("p b (u c) -> p (b u) c", c=P)
                for h in range(2):
                    ins = nc.scalar.copy(units(tmp)[h * 64:h * 64 + 64, :, :], src[:, :, h * 64:h * 64 + 64])
                ins.then_inc(rw_a, 1)

                act.wait_ge(resid, 3 * l + 2)
                norm(("ffn2", l, 0), x[:, :, :], 4 + 2 * l)
                ffn(4 + 2 * l)
            act.wait_ge(resid, 3 * LAYERS)
            norm(("final", 0, 0), x[:, :, :])

        @block.vector
        def _(dve):
            dve.wait_ge(const_loaded, 64)
            for l in range(LAYERS):
                ka0, ka1 = V[f"k_a{l}"]
                ins = nc.vector.tensor_scalar(omka[:, l * QT:(l + 1) * QT], vec[:, ka0:ka1], -1.0, 1.0,
                                              ALU.mult, ALU.add)
            ins.then_inc(kab, 1)
            b0 = V["b_ada"][0]

            def ada(l, n, i=None):
                g, u, at = l * ADA + n, n % 2, (l * ADA + n) * 2
                dve.wait_ge(ada_turned, g + 1 if i is None else i * 2 + (g + 1))
                to = slice(at, at + 2) if i is None else bass.ds(i * 4 + at, 2)
                bias = slice(b0 + at, b0 + at + 2) if i is None else bass.ds(i * 4 + (b0 + at), 2)
                nc.vector.tensor_tensor(
                    mod[:, to, :], ps[:, 4 + u, T:T + 4].rearrange("p (a b) -> p a b", b=2),
                    vec[:, bias][:, :, None].to_broadcast([P, 2, 2]), ALU.add).then_inc(ada_free, 1)

            def gains(l):
                dve.wait_ge(ada_free, (l + 1) * ADA)
                for i, (part, name, plus) in enumerate([(1, "pre_mix", 1.0), (2, "post_mix", 0.0),
                                                        (4, "pre_ffn", 1.0), (5, "post_ffn", 0.0)]):
                    v0, v1 = V[f"{name}{l}"]
                    ins = nc.vector.scalar_tensor_tensor(
                        gain[:, l, i], mod[:, l * NMOD + part * KD:l * NMOD + (part + 1) * KD, :], plus,
                        vec[:, v0:v1][:, :, None].to_broadcast([P, KD, 2]), ALU.add, ALU.mult)
                ins.then_inc(gain_ready, 1)
                dve.wait_ge(gain_ready, l + 1)

            with dve.Fori(0, ADA // 2) as i:
                ada(0, 0, i)
                ada(0, 1, i)
            gains(0)

            def norm(key, src, gains, dst, shift=None, onto=None):
                n = n_id[key]
                dve.wait_ge(norm_rt, n + 1)
                nc.vector.reciprocal(rstd[:, :], nrt[:, :]).then_inc(norm_rstd, 1)
                dve.wait_ge(norm_rstd, n + 1)
                for k in range(KD):
                    ins = nc.vector.scalar_tensor_tensor(dst[:, k, :], src[:, k, :], gains(k), rstd[:, :],
                                                         ALU.mult, ALU.mult)
                if shift is None and onto is None:
                    ins.then_inc(norm_out, 1)
                    return
                ins.then_inc(norm_scaled, 1)
                dve.wait_ge(norm_scaled, n_two[key] + 1)
                if shift is not None:
                    to, add = shift
                    for k in range(KD):
                        ins = nc.vector.tensor_scalar(to[:, k, :], dst[:, k, :], add(k), None, ALU.add)
                    ins.then_inc(norm_out, 1)
                else:
                    nc.vector.tensor_tensor(onto, onto, dst[:, :, :], ALU.add).then_inc(norm_out, 1)

            def rest_a(call, f, i=None):
                c, t = chunk0[f"ffn{call}"] + f, call * FT + f
                for part in range(2):
                    n = 2 * t + part + 1
                    dve.wait_ge(hi_a, n if i is None else i * 4 + n)
                    ins = nc.vector.tensor_tensor(w_lo[:, f % 2, part], ring_a[:, c % 2, part],
                                                  w_hi[:, f % 2, part].bitcast(F32), ALU.subtract)
                ins.then_inc(a_used, 1)

            def rest_d(call, f, i=None):
                d = call * FT + f
                wait(dve, hi_d, d + 1, i)
                nc.vector.tensor_tensor(d_lo[:, f % 2], ring_d[:, d % 2], d_hi[:, f % 2].bitcast(F32), ALU.subtract)\
                    .then_inc(d_used, 1)

            def norm_split(key, src, call, gains=None):
                n = n_id[key]
                rest_a(call, 0)
                dve.wait_ge(norm_rt, n + 1)
                nc.vector.reciprocal(rstd[:, :], nrt[:, :]).then_inc(norm_rstd, 1)
                dve.wait_ge(norm_rstd, n + 1)
                for k in range(KD):
                    if gains is None:
                        ins = nc.vector.tensor_tensor(hn[:, k, :], src[:, k, :], rstd[:, :], ALU.mult)
                    else:
                        ins = nc.vector.scalar_tensor_tensor(hn[:, k, :], src[:, k, :], gains(k), rstd[:, :],
                                                             ALU.mult, ALU.mult)
                    ins.then_inc(v_ready, 1)
                whole = nsq if gains is None else hn
                for k in range(KD):
                    dve.wait_ge(hh_ready, call * KD + k + 1)
                    if gains is not None:
                        dve.wait_ge(v_ready, call * KD + k + 1)
                    nc.vector.tensor_tensor(h_lo[:, k, :], whole[:, k, :], h_hi[:, k, :].bitcast(F32), ALU.subtract)\
                        .then_inc(hl_ready if k < KD - 1 else norm_out, 1)

            def ffn(call):
                rest_a(call, 1)
                rest_d(call, 0)

                def tile(f, i=None):
                    t = call * FT + f
                    wait(dve, sg_ready, t + 1, i)
                    nc.vector.tensor_tensor(hid[:, f % 2, :], sg[:, f % 2, :], ps[:, 4 + f % 2, T:2 * T], ALU.mult)\
                        .then_inc(hid_mul, 1)
                    wait(dve, hid_mul, t + 1, i)
                    wait(dve, dn_done, t - 1, i)
                    nc.vector.tensor_copy(hid_hi[:, f % 2, :], hid[:, f % 2, :]).then_inc(hid_rounded, 1)
                    wait(dve, hid_rounded, t + 1, i)
                    nc.vector.tensor_tensor(hid_lo[:, f % 2, :], hid[:, f % 2, :], hid_hi[:, f % 2, :].bitcast(F32),
                                            ALU.subtract).then_inc(hid_ready, 1)
                    if f + 2 < FT:
                        rest_a(call, f + 2, i)
                    if f + 1 < FT:
                        rest_d(call, f + 1, i)

                tile(0)
                tile(1)
                with dve.Fori(0, FT // 2 - 2) as i:
                    tile(2, i)
                    tile(3, i)
                tile(FT - 2)
                tile(FT - 1)

            def attention(call, l, which):
                n_keys = 2 * T if which == 0 else T

                def scores(u):
                    g, h, blk, r = call * 16 + u, (u % 2) * 4 + (u // 2) % 4, u // 8, u % 2
                    dve.wait_ge(at_sc, g + 1)
                    if g >= 2:
                        dve.wait_ge(at_exp, g - 1)
                    if which == 0:
                        ins = nc.vector.scalar_tensor_tensor(
                            s_sb[:, r, :], ps[:, r, :], HD ** -0.5, const1("win")[:, blk * 2 * T:(blk + 1) * 2 * T],
                            ALU.mult, ALU.add)
                    else:
                        ins = nc.vector.tensor_scalar(s_sb[:, r, 0:T], ps[:, r, 0:T], HD ** -0.5, None, ALU.mult)
                    ins.then_inc(at_s, 1)
                    dve.wait_ge(at_s, g + 1)
                    nc.vector.reduce_max(tiny[:, r, 0:1], s_sb[:, r, 0:n_keys], AX_X).then_inc(at_mx, 1)
                    dve.wait_ge(at_mx, g + 1)
                    nc.vector.tensor_scalar(tiny[:, r, 1:2], tiny[:, r, 0:1], vcol("sink", l * 8 + h), -1.0,
                                            ALU.max, ALU.mult).then_inc(at_nm, 1)

                def normalise(u):
                    g, r = call * 16 + u, u % 2
                    dve.wait_ge(at_exp, g + 1)
                    nc.vector.tensor_tensor(tiny[:, r, 4:5], tiny[:, r, 2:3], tiny[:, r, 3:4], ALU.add)\
                        .then_inc(at_den, 1)
                    dve.wait_ge(at_den, g + 1)
                    nc.vector.reciprocal(tiny[:, r, 5:6], tiny[:, r, 4:5]).then_inc(at_rd, 1)
                    dve.wait_ge(at_rd, g + 1)
                    if g >= 2:
                        dve.wait_ge(at_tr, g - 1)
                    nc.vector.tensor_scalar(pn[:, r, 0:n_keys], probs[:, r, 0:n_keys], tiny[:, r, 5:6], None,
                                            ALU.mult).then_inc(at_pn, 1)

                for u in range(17):
                    if u < 16:
                        scores(u)
                    if u >= 1:
                        normalise(u - 1)
                    if l == 0 and u in ADA_STEPS and ada_chunk(which, u):
                        ada(1, ada_chunk(which, u) - 1)

            acall = 0
            for l in range(LAYERS):
                if l == 0:
                    dve.wait_ge(in_loaded, 32)
                norm(("pre_mix", l, 0), x, gain_of(l, 0, 0), hn, shift=(h2[:, :, 0:T], shift_of(l, 0, 0)))
                norm(("pre_mix", l, 1), xc, gain_of(l, 0, 1), hn, shift=(h2[:, :, T:2 * T], shift_of(l, 0, 1)))
                cos, sin = (const1(n)[:, None, :].to_broadcast([P, 5, T]) for n in ("cos", "sin"))
                dve.wait_ge(rope_rot, l + 1)
                rot = ps[:, 0:3, :].rearrange("p a (b t) -> p (a b) t", t=T)[:, 0:5, :]
                nc.vector.tensor_tensor(rtmp, rot, sin, ALU.mult).then_inc(rope_sin, 1)
                nc.vector.tensor_tensor(raw[:, :, 0:T], raw[:, :, 0:T], cos, ALU.mult).then_inc(rope_cos, 1)
                dve.wait_ge(rope_sin, l + 1)
                dve.wait_ge(rope_cos, l + 1)
                nc.vector.tensor_tensor(kall[:, 0:T], raw[:, 0, 0:T], rtmp[:, 0, :], ALU.add)
                nc.vector.tensor_tensor(qr, raw[:, 1:5, 0:T], rtmp[:, 1:5, :], ALU.add).then_inc(rope_out, 1)
                for which in ([0, 1] if l == 0 else [0]):
                    attention(acall, l, which)
                    acall += 1
                if l == 0:
                    ada(1, ADA - 1)
                    gains(1)
                for which in ([0, 1] if l == 0 else [0]):
                    res = x[:, :, :] if which == 0 else xc
                    mixed = mix[:, :, token_cols(l, which)]
                    norm(("post_mix", l, which), mixed, gain_of(l, 1, which), hn, onto=res)
                    dve.wait_ge(norm_out, n_id[("post_mix", l, which)] + 1)
                    norm_split(("pre_ffn", l, which), res, 2 * l + which)
                    ffn(2 * l + which)
                    norm(("post_ffn", l, which), mixed, gain_of(l, 3, which), hn, onto=res)

            def per_channel(name, l):
                return lambda k: vcol(f"{name}{l}", k)

            def v(name, l):
                dve.wait_ge(rw_v, RV.at(name, l))

            def wide(bank):
                return ps[:, bank:bank + 2, :].rearrange("p a (b t) -> p (a b) t", t=T)

            dve.wait_ge(norm_out, n_id[("post_ffn", 1, 0)] + 1)
            for l in range(LAYERS):
                norm_split(("ffn1", l, 0), x, 3 + 2 * l, per_channel("ffn1", l))
                ffn(3 + 2 * l)
                dve.wait_ge(dn_done, (4 + 2 * l) * FT)
                acc = ps[:, 0:4, :].rearrange("p a (b t) -> p (a b) t", t=T)
                nc.vector.scalar_tensor_tensor(x[:, :, :], acc, 0.5, x[:, :, :], ALU.mult, ALU.add).then_inc(resid, 1)
                dve.wait_ge(resid, 3 * l + 1)
                norm(("mix", l, 0), x, per_channel("mix", l), hn)

                zr, zk, zv = (z[:, a:a + QT, 1:T + 1] for a in (R0, K0, V0))
                p0 = tile0[f"proj2{l}"]
                dve.wait_ge(proj_free, p0 + MIXED)
                nc.vector.tensor_tensor(diff, z[:, 0:MIXED, 0:T], z[:, 0:MIXED, 1:T + 1], ALU.subtract)\
                    .then_inc(rw_v, 1)
                v("diff", l)
                for k in range(MIXED):
                    rows = slice(0, P) if k != MISC else slice(0, 32)
                    zz = z[rows, k, 1:T + 1]
                    ins = nc.vector.scalar_tensor_tensor(zz, diff[rows, k, :], vcol(f"mu{l}", k)[rows], zz,
                                                         ALU.mult, ALU.add)
                ins.then_inc(rw_v, 1)
                dve.wait_ge(proj_free, p0 + MK + QT)
                for tap in range(4):
                    if tap:
                        dve.wait_ge(ml_v, MVS.at(f"c{tap - 1}", l))
                    for k in range(2 * QT):
                        zz = z[:, MQ + k, 1:T + 1 - tap]
                        if tap == 0:
                            ins = nc.vector.tensor_scalar(nsq[:, k, :], zz, vcol(f"tap3{l}", k),
                                                          vcol(f"conv_b{l}", k), ALU.mult, ALU.add)
                        else:
                            ins = nc.vector.scalar_tensor_tensor(nsq[:, k, tap:T], zz, vcol(f"tap{3 - tap}{l}", k),
                                                                 nsq[:, k, tap:T], ALU.mult, ALU.add)
                    ins.then_inc(ml_v, 1)
                dve.wait_ge(rw_a, RA.at("sw", l))
                nc.vector.tensor_scalar(lw, lw, -float(np.exp(-0.5)), None, ALU.mult).then_inc(rw_v, 1)
                v("lw", l)
                for j in range(QT):
                    ins = nc.vector.tensor_tensor_scan(lcum[:, j, :], const("restart"), lw[:, j, :], 0.0,
                                                       ALU.mult, ALU.add)
                ins.then_inc(rw_v, 1)
                v("mix", l)
                for j in range(QT):
                    ins = nc.vector.tensor_scalar(kk[:, j, :], zk[:, j, :], vcol(f"k_k{l}", j), None, ALU.mult)
                ins.then_inc(rw_v, 1)
                v("kk", l)
                nc.vector.tensor_tensor(bon, kk, kk, ALU.mult).then_inc(rw_v, 1)
                if l == 0:
                    nc.vector.tensor_copy(vfirst[:, :, :], zv)
                else:
                    dve.wait_ge(vres_a, 1)
                    nc.vector.tensor_tensor(e1, vfirst[:, :, :], zv, ALU.subtract).then_inc(vres_v, 1)
                    dve.wait_ge(vres_v, VV.at("d", 0))
                    nc.vector.tensor_tensor(e1, e1, vg, ALU.mult).then_inc(vres_v, 1)
                    dve.wait_ge(vres_v, VV.at("m", 0))
                    nc.vector.tensor_tensor(zv, zv, e1, ALU.add).then_inc(vres_v, 1)
                dve.wait_ge(rw_a, RA.at("rsq", l))
                nc.vector.tensor_scalar(tmp[0:8, 3, :], tmp[0:8, 3, :], 1e-12, None, ALU.max).then_inc(rw_v, 1)
                v("rnmax", l)
                nc.vector.reciprocal(inv_norm, tmp[0:8, 3, :]).then_inc(rw_v, 1)
                dve.wait_ge(rw_p, RP.at("rnb", l))
                nc.vector.tensor_tensor(kk, kk, wide(0), ALU.mult).then_inc(rw_v, 1)
                v("kkn", l)
                dve.wait_ge(rw_a, RA.at("aa", l))
                nc.vector.tensor_tensor(bb, kk, aa, ALU.mult).then_inc(rw_v, 1)
                v("b", l)
                dve.wait_ge(kab, 1)
                for j in range(QT):
                    ins = nc.vector.tensor_scalar(aa[:, j, :], aa[:, j, :], vcol(f"k_a{l}", j),
                                                  omka[:, l * QT + j:l * QT + j + 1], ALU.mult, ALU.add)
                ins.then_inc(rw_v, 1)
                v("ka", l)
                nc.vector.tensor_tensor(zk, zk, aa, ALU.mult).then_inc(rw_v, 1)
                v("kp", l)
                dve.wait_ge(rw_p, RP.at("ss", l))
                for j in range(QT):
                    ins = nc.vector.scalar_tensor_tensor(bon[:, j, :], zr[:, j, :], vcol(f"r_k{l}", j), zk[:, j, :],
                                                         ALU.mult, ALU.mult)
                ins.then_inc(rw_v, 1)
                if l:
                    dve.wait_ge(vres_v, VV.at("v", 0))
                dve.wait_ge(rw_p, RP.at("bon", l))
                nc.vector.tensor_tensor(bon, wide(2), zv, ALU.mult).then_inc(rw_v, 1)
                v("scan", l)
                nc.vector.tensor_tensor(e0, lcum, lw, ALU.subtract).then_inc(rw_v, 1)
                dve.wait_ge(rw_a, RA.at("e2", l))
                nc.vector.tensor_tensor(kt, kk, e0, ALU.mult).then_inc(rw_v, 1)
                nc.vector.tensor_tensor(bh, bb, e2, ALU.mult).then_inc(rw_v, 1)
                v("kt", l)
                nc.vector.tensor_tensor(kh, zk, e2, ALU.mult).then_inc(rw_v, 1)
                nc.vector.tensor_tensor(zr, zr, e1, ALU.mult).then_inc(rw_v, 1)
                v("kh", l)
                pc = units(e1)[:, :, CHUNK - 1:CHUNK].to_broadcast([P, UNITS, CHUNK])
                nc.vector.tensor_tensor(units(khc), units(kh), pc, ALU.mult).then_inc(rw_v, 1)
                nc.vector.tensor_tensor(units(bhc), units(bh), pc, ALU.mult).then_inc(rw_v, 1)

                def m(name):
                    dve.wait_ge(ml_v, MVS.at(name, l))
                row = lambda i: rows4[0:4, i, :]
                dve.wait_ge(ml_a, MA.at("ab", l))
                nc.vector.tensor_scalar(row(3), ps[0:4, 6, T:2 * T], vcol(f"fb{l}", 0)[0:4], 0.0, ALU.add, ALU.min)\
                    .then_inc(ml_v, 1)
                m("mn")
                dve.wait_ge(ml_a, MA.at("ln", l))
                nc.vector.tensor_tensor(row(4), row(3), row(2), ALU.subtract).then_inc(ml_v, 1)
                m("lf")
                ones_row = const("one")[0:4].to_broadcast([4, T])
                nc.vector.tensor_tensor_scan(row(5), ones_row, row(4), 0.0, ALU.mult, ALU.add).then_inc(ml_v, 1)
                m("F")
                nc.vector.scalar_tensor_tensor(row(6), ps[0:4, 6, 0:T], vcol(f"ib{l}", 0)[0:4], row(5),
                                               ALU.add, ALU.subtract).then_inc(ml_v, 1)
                m("g")
                nc.vector.tensor_tensor_scan(row(7), ones_row, row(6), 0.0, ALU.mult, ALU.max).then_inc(ml_v, 1)
                m("M")
                nc.vector.tensor_scalar(row(0), row(7), -1.0, None, ALU.mult).then_inc(ml_v, 1)
                nc.vector.tensor_tensor(row(1), row(5), row(7), ALU.add).then_inc(ml_v, 1)
                for h in range(5):
                    r = l * 4 + h
                    if h < 4:
                        dve.wait_ge(mh_arg, r + 1)
                        if r >= 2:
                            dve.wait_ge(mh_ee, r - 1)
                        nc.vector.tensor_tensor(am[:, h % 2, :], ps[:, h % 2, 0:T + P], const("tri"), ALU.add)\
                            .then_inc(mh_am, 1)
                        dve.wait_ge(mh_ee, r + 1)
                        dve.wait_ge(mh_s, r + 1)
                        if r >= 2:
                            dve.wait_ge(mh_nd, r - 1)
                        nc.vector.scalar_tensor_tensor(pm[:, h % 2, :], ps[:, 2 + h % 2, 0:T + P], float(P) ** -0.5,
                                                       ee[:, h % 2, :], ALU.mult, ALU.mult).then_inc(mh_pm, 1)
                    if h >= 1:
                        r, o = r - 1, (h - 1) % 2
                        dve.wait_ge(mh_ems, r + 1)
                        dve.wait_ge(mh_nd, r + 1)
                        nc.vector.scalar_tensor_tensor(dn[:, o, :], ps[:, 6 + o, T:2 * T], -1.0, ems[:, o, :],
                                                       ALU.mult, ALU.max).then_inc(mh_dn, 1)
                        dve.wait_ge(mh_dn, r + 1)
                        nc.vector.tensor_tensor(dn[:, o, :], ps[:, 6 + o, T:2 * T], dn[:, o, :], ALU.max)\
                            .then_inc(mh_abs, 1)
                        dve.wait_ge(mh_abs, r + 1)
                        nc.vector.reciprocal(dn[:, o, :], dn[:, o, :]).then_inc(mh_rc, 1)
                        dve.wait_ge(mh_rc, r + 1)
                        nc.vector.tensor_tensor(hN[:, h - 1, :], ps[:, 6 + o, 0:T], dn[:, o, :], ALU.mult)\
                            .then_inc(mh_h, 1)
                dve.wait_ge(ml_p, MP.at("mu", l))
                nc.vector.scalar_tensor_tensor(hc, wide(0), -1.0 / P, hN, ALU.mult, ALU.add).then_inc(ml_v, 1)
                dve.wait_ge(ml_a, MA.at("hsd", l))
                nc.vector.reciprocal(yb, yb).then_inc(ml_v, 1)
                m("rec")
                nc.vector.tensor_tensor(hc, hc, yb, ALU.mult).then_inc(ml_v, 1)
                m("hs")
                for j in range(QT):
                    ins = nc.vector.scalar_tensor_tensor(yb[:, j, :], hc[:, j, :], vcol(f"ml_w{l}", j),
                                                         z[:, MO + j, 1:T + 1], ALU.mult, ALU.mult)
                ins.then_inc(ml_v, 1)
                m("yb")

                def masked(dst, bank, mask, op=ALU.mult):
                    return nc.vector.tensor_tensor(
                        units(dst), ps[:, bank:bank + 2, :].rearrange("p b (u t) -> p (b u) t", t=CHUNK),
                        const(mask)[:, None, :].to_broadcast([P, UNITS, CHUNK]), op)

                eye = const("eye")[:, None, :].to_broadcast([P, UNITS, CHUNK])
                dve.wait_ge(rw_p, RP.at("at", l))
                masked(at_, 4, "strict").then_inc(rw_v, 1)
                dve.wait_ge(rw_p, RP.at("a", l))
                masked(xs, 0, "low1").then_inc(rw_v, 1)
                v("at", l)
                nc.vector.tensor_tensor(units(xt), units(at_),
                                        const("up1")[:, None, :].to_broadcast([P, UNITS, CHUNK]), ALU.mult)\
                    .then_inc(rw_v, 1)
                dve.wait_ge(rw_p, RP.at("mt", l))
                masked(mt, 6, "strict").then_inc(rw_v, 1)
                v("xt1", l)
                nc.vector.tensor_tensor(units(xs), eye, units(xs), ALU.subtract).then_inc(rw_v, 1)
                nc.vector.tensor_tensor(units(xt), eye, units(xt), ALU.subtract).then_inc(rw_v, 1)
                dve.wait_ge(rw_p, RP.at("mrt", l))
                masked(mrt, 2, "incl").then_inc(rw_v, 1)
                dve.wait_ge(rw_p, RP.at("art", l))
                masked(art, 4, "incl").then_inc(rw_v, 1)
                for i in range(len(LEVELS)):
                    step = l * len(LEVELS) + i
                    for half in range(2):
                        us = slice(half * 8, half * 8 + 8)
                        dve.wait_ge(lev_p, LP.at(f"x{half}", step))
                        for buf, bank in ((xs, 2), (xt, 4)):
                            nc.vector.tensor_tensor(
                                units(buf)[:, us, :], units(buf)[:, us, :],
                                ps[:, bank + half, :].rearrange("p (u t) -> p u t", t=CHUNK), ALU.subtract)\
                                .then_inc(lev_v, 1)
                pcs = units(e1)[:, :, CHUNK - 1:CHUNK]
                for c in range(NC_):
                    step = l * NC_ + c
                    if c == 0:
                        nc.vector.memset(state[:, 0], 0.0).then_inc(ch_v, 1)
                    else:
                        dve.wait_ge(ch_v, CV.at("s", step - 1))
                        nc.vector.tensor_tensor(
                            sdec, state[:, c % 2],
                            e1[:, :, c * CHUNK + CHUNK - 1:c * CHUNK + CHUNK].to_broadcast([P, QT, HD]),
                            ALU.mult).then_inc(ch_v, 1)
                    dve.wait_ge(ch_p, CP.at("u", step))
                    nc.vector.tensor_scalar(nu[:, :, c * CHUNK:(c + 1) * CHUNK],
                                            ps[:, 1, 0:QT * HD].rearrange("p (j v) -> p j v", v=HD), -1.0, None,
                                            ALU.mult).then_inc(ch_v, 1)
                    dve.wait_ge(ch_p, CP.at("s", step))
                    sp_ = ps[:, 4, 0:QT * HD].rearrange("p (j v) -> p j v", v=HD)
                    if c:
                        dve.wait_ge(ch_v, CV.at("nu", step))
                        nc.vector.tensor_tensor(state[:, (c + 1) % 2], sp_, sdec, ALU.add).then_inc(ch_v, 1)
                    else:
                        nc.vector.tensor_copy(state[:, 1], sp_).then_inc(ch_v, 1)
                yps = ps[:, 2:4, :].rearrange("p b (u t) -> p (b u) t", t=HD)
                stat = lambda i: small_y[:, i, :]
                wide_stat = lambda i: small_y[:, i, :][:, :, None].to_broadcast([P, UNITS, HD])
                dve.wait_ge(ch_p, CP.at("y", l * NC_ + NC_ - 1))
                nc.vector.reduce_sum(stat(0), yps, AX_X).then_inc(rw_v, 1)
                v("s1", l)
                nc.vector.tensor_scalar(stat(1), stat(0), -1.0 / HD, None, ALU.mult).then_inc(rw_v, 1)
                v("ym", l)
                nc.vector.tensor_tensor(units(yy), yps, wide_stat(1), ALU.add).then_inc(rw_v, 1)
                v("yc", l)
                nc.vector.tensor_tensor(units(yq), units(yy), units(yy), ALU.mult).then_inc(rw_v, 1)
                v("yq", l)
                nc.vector.reduce_sum(stat(3), units(yq), AX_X).then_inc(rw_v, 1)
                dve.wait_ge(rw_a, RA.at("ysd", l))
                nc.vector.reciprocal(stat(5), stat(4)).then_inc(rw_v, 1)
                v("yr", l)
                nc.vector.tensor_tensor(units(yy), units(yy), wide_stat(5), ALU.mult).then_inc(rw_v, 1)
                dve.wait_ge(rw_a, RA.at("yT", l))
                for j in range(QT):
                    ins = nc.vector.tensor_scalar(tmp[:, j, :], tmp[:, j, :], vcol(f"gn_w{l}", j),
                                                  vcol(f"gn_b{l}", j), ALU.mult, ALU.add)
                ins.then_inc(rw_v, 1)
                v("gn", l)
                nc.vector.tensor_tensor(tmp, tmp, bon, ALU.add).then_inc(rw_v, 1)
                v("gb", l)
                nc.vector.tensor_tensor(ya, tmp, gg, ALU.mult).then_inc(rw_v, 1)

                dve.wait_ge(ml_a, MA.at("gates", l))
                for n in range(KD):
                    r = l * KD + n
                    if n % 2:
                        dve.wait_ge(a_used, chunk0[f"br{l}"] + n // 2 + 1)
                    else:
                        dve.wait_ge(br_ready, r // 2 + 1)
                    nc.vector.tensor_tensor(umix[:, n, :], ps[:, 4 + n % 2, 0:T], z[:, GA + n, 1:T + 1], ALU.mult)\
                        .then_inc(br_part, 1)
                    nc.vector.tensor_tensor(xs[:, n % 2, :], ps[:, 4 + n % 2, T:2 * T], z[:, GB + n, 1:T + 1], ALU.mult)\
                        .then_inc(br_part, 1)
                    dve.wait_ge(br_part, 2 * r + 2)
                    nc.vector.tensor_tensor(umix[:, n, :], umix[:, n, :], xs[:, n % 2, :], ALU.add).then_inc(br_free, 1)
                for n in range(KD // 2):
                    dve.wait_ge(a_used, chunk0[f"out2{l}"] + n + 1)
                    xx = x[:, 2 * n:2 * n + 2, :]
                    ins = nc.vector.tensor_tensor(xx, xx, ps[:, n, :].rearrange("p (a b) -> p a b", b=T), ALU.add)
                ins.then_inc(resid, 1)
                dve.wait_ge(resid, 3 * l + 2)
                norm_split(("ffn2", l, 0), x, 4 + 2 * l, per_channel("ffn2", l))
                ffn(4 + 2 * l)
                dve.wait_ge(dn_done, (5 + 2 * l) * FT)
                nc.vector.scalar_tensor_tensor(x[:, :, :], acc, 0.5, x[:, :, :], ALU.mult, ALU.add).then_inc(resid, 1)
                dve.wait_ge(resid, 3 * l + 3)
            norm(("final", 0, 0), x, lambda k: vcol("final", k), hn)

        @block.tensor
        def _(pe):
            pe.wait_ge(const_loaded, 64)
            ones, ident = const("ones"), const("ident")

            def chunk_here(c, slot, i=None):
                n = 16 * (c // 2 + 1)
                pe.wait_ge(a_loaded[slot], n if i is None else i * 16 + n)

            pe.wait_ge(cs_ready, 1)

            def ada(l, n, i=None):
                c, g, u = chunk0[f"ada{l}"] + n, l * ADA + n, n % 2
                chunk_here(c, c % 2, i)
                if g >= 2:
                    pe.wait_ge(ada_free, g - 1 if i is None else i * 2 + (g - 1))
                for k in range(KD):
                    mm = nc.tensor.matmul(ps[0:2, 4 + u, 0:T].rearrange("p (a b) -> p a b", b=P), cs[:, k, :],
                                          ring_a[:, c % 2, :, k, :], start=(k == 0), stop=(k == KD - 1))
                mm.then_inc(a_used, 1)

            def ada_turn(l, n, i=None):
                g, u = l * ADA + n, n % 2
                pe.wait_ge(ada_row, g + 1 if i is None else i * 2 + (g + 1))
                for h in range(2):
                    mm = nc.tensor.matmul(ps[:, 4 + u, T + 2 * h:T + 2 * h + 2], ada_rows[0:2, u, h * P:(h + 1) * P],
                                          ident[0:2, 0:2], start=True, stop=True)
                mm.then_inc(ada_turned, 1)

            ada(0, 0)
            ada(0, 1)
            ada_turn(0, 0)
            with pe.Fori(0, ADA // 2 - 1) as i:
                for u in range(2):
                    ada(0, 2 + u, i)
                    ada_turn(0, 1 + u, i)
            ada_turn(0, ADA - 1)

            def norm(key):
                n = n_id[key]
                pe.wait_ge(norm_sq, n + 1)
                if n:
                    pe.wait_ge(norm_rt, n)
                for k in range(KD):
                    mm = nc.tensor.matmul(ps[:, 6, 0:T], ones, nsq[:, k, :], start=(k == 0), stop=(k == KD - 1))
                mm.then_inc(norm_sum, 1)

            def split_product(out, parts, start, stop):
                hi, lo, to_hi, to_lo = parts
                nc.tensor.matmul(out, hi, to_hi, start=start, stop=False, skip_group_check=True)
                nc.tensor.matmul(out, hi, to_lo, start=False, stop=False, skip_group_check=True)
                return nc.tensor.matmul(out, lo, to_hi, start=False, stop=stop, skip_group_check=True)

            def ffn(call, key):
                c0, d0 = chunk0[f"ffn{call}"], call * FT

                def gate_up(f, i=None):
                    c, t = c0 + f, d0 + f
                    wait(pe, a_used, c + 1, i)
                    if f >= 2 or call:
                        wait(pe, hid_mul, t - 1, i)
                    for part in range(2):
                        for k in range(KD):
                            if f == 0 and part == 0:
                                if k < KD - 1:
                                    pe.wait_ge(hl_ready, call * (KD - 1) + k + 1)
                                else:
                                    pe.wait_ge(norm_out, n_id[key] + 1)
                            mm = split_product(ps[:, 4 + f % 2, part * T:part * T + T],
                                               (w_hi[:, f % 2, part, k, :], w_lo[:, f % 2, part, k, :],
                                                h_hi[:, k, :], h_lo[:, k, :]), start=(k == 0), stop=(k == KD - 1))
                    mm.then_inc(gu_done, 1)

                def down(f, i=None):
                    d = d0 + f
                    wait(pe, d_used, d + 1, i)
                    wait(pe, hid_ready, d + 1, i)
                    for n in range(KD):
                        mm = split_product(ps[:, n // 2, n % 2 * T:n % 2 * T + T],
                                           (d_hi[:, f % 2, n, :], d_lo[:, f % 2, n, :],
                                            hid_hi[:, f % 2, :], hid_lo[:, f % 2, :]),
                                           start=(f == 0 and n % 2 == 0), stop=(f == FT - 1))
                    mm.then_inc(dn_done, 1)

                gate_up(0)
                gate_up(1)
                down(0)
                with pe.Fori(0, (FT - 2) // 2) as i:
                    for u in range(2):
                        gate_up(2 + u, i)
                        down(1 + u, i)
                down(FT - 1)

            def tile_done(mm, stage, i):
                mm.then_inc(a_used if i % 2 or i == ZT + QT - 1 else proj_ready, 1)

            def project(stage, i, h, cols):
                p, slot = tile0[stage] + i, (chunk0[stage] + i // 2) % 2
                if i % 2 == 0:
                    chunk_here(chunk0[stage] + i // 2, slot)
                if p >= 2:
                    pe.wait_ge(proj_free, p - 1)
                for k in range(KD):
                    mm = nc.tensor.matmul(ps[:, 4 + p % 2, 0:cols.stop - cols.start], ring_a[:, slot, i % 2, k, :],
                                          h[:, k, cols], start=(k == 0), stop=(k == KD - 1))
                tile_done(mm, stage, i)

            def project_tokens(stage, i, h, blocks):
                p, slot = tile0[stage] + i, (chunk0[stage] + i // 2) % 2
                if i % 2 == 0:
                    chunk_here(chunk0[stage] + i // 2, slot)
                if p >= 2:
                    pe.wait_ge(proj_free, p - 1)
                for b in range(blocks):
                    for k in range(KD):
                        mm = nc.tensor.matmul(ps[:, 4 + p % 2, b * P:(b + 1) * P], h[:, k, b * P:(b + 1) * P],
                                              ring_a[:, slot, i % 2, k, :], start=(k == 0), stop=(k == KD - 1))
                tile_done(mm, stage, i)

            def fourier(call, l, which):
                wait_u = tile0[f"proj1{l}"] + 10
                pe.wait_ge(proj_free, wait_u)
                pe.wait_ge(rope_sin, l + 1)
                if call:
                    pe.wait_ge(fo_out, call * QT)
                if which:
                    pe.wait_ge(at_pt, (call) * 16)
                    pe.wait_ge(at_s, (call) * 16)
                for j in range(QT):
                    for b in range(2):
                        mm = nc.tensor.matmul(ps[:, j, :], u_tok[:, 2 * which + b, j * P:(j + 1) * P],
                                              const1("dft")[:, b * 2 * T:(b + 1) * 2 * T], start=(b == 0), stop=(b == 1))
                    mm.then_inc(fo_dft, 1)
                for j in range(QT):
                    pe.wait_ge(fo_fu, call * QT + j + 1)
                    nc.tensor.matmul(ps[:, j, 0:T], const1("chc"), fu[:, j, 0:T], start=True, stop=False)
                    nc.tensor.matmul(ps[:, j, 0:T], const1("chs"), fu[:, j, T:2 * T], start=False, stop=True)\
                        .then_inc(fo_ch, 1)
                for j in range(QT):
                    pe.wait_ge(fo_fm, call * QT + j + 1)
                    nc.tensor.matmul(ps[:, j, T:2 * T], wfour[:, l * QT + j, :], fm[:, j, :], start=True, stop=True)\
                        .then_inc(fo_w, 1)

            def attention(call, l, which):
                n_keys = 2 * T if which == 0 else T
                keys = kall if which == 0 else kall[:, T:2 * T]
                pe.wait_ge(fo_out, (call + 1) * QT)
                pe.wait_ge(rope_out, l + 1)

                def scores(u):
                    g, blk, j, kv = call * 16 + u, u // 8, u // 2 % 4, u % 2
                    half = slice(kv * HD, kv * HD + HD)
                    if g >= 2:
                        pe.wait_ge(at_s, g - 1)
                    q = qr[half, j, blk * P:(blk + 1) * P] if which == 0 else \
                        raw[half, 1 + j, T + blk * P:T + (blk + 1) * P]
                    nc.tensor.matmul(ps[:, u % 2, 0:n_keys], q, keys[half, :], start=True, stop=True).then_inc(at_sc, 1)

                def turn(u):
                    g = call * 16 + u
                    pe.wait_ge(at_pn, g + 1)
                    if g >= 2:
                        pe.wait_ge(at_pt, g - 1)
                    for b in range(n_keys // P):
                        mm = nc.tensor.transpose(ps[:, 2 + u % 2, b * P:(b + 1) * P], pn[:, u % 2, b * P:(b + 1) * P],
                                                 ident)
                    mm.then_inc(at_tr, 1)

                def values(u):
                    g, w, kv = call * 16 + u, u // 2, u % 2
                    half = slice(kv * HD, kv * HD + HD)
                    pe.wait_ge(at_pt, g + 1)
                    if call * 8 + w >= 2:
                        pe.wait_ge(at_o, call * 8 + w - 1)
                    nb = n_keys // P
                    for b in range(nb):
                        mm = nc.tensor.matmul(ps[half, 6 + w % 2, 0:P], v_tok[:, 4 - nb + b, half], pt[:, u % 2, b, :],
                                              start=(b == 0), stop=(b == nb - 1))
                    mm.then_inc(at_pv, 1)

                for u in range(18):
                    if u < 16:
                        scores(u)
                    if 1 <= u <= 16:
                        turn(u - 1)
                    if u >= 2:
                        values(u - 2)
                    if l == 0 and u in ADA_STEPS:
                        n = ada_chunk(which, u)
                        ada(1, n)
                        if n:
                            ada_turn(1, n - 1)

            fcall = 0
            for l in range(LAYERS):
                norm(("pre_mix", l, 0))
                norm(("pre_mix", l, 1))
                pe.wait_ge(norm_out, n_id[("pre_mix", l, 1)] + 1)
                stage, n_q = f"proj1{l}", (2 * T, T)[l]
                for i in range(10):
                    if i == 0:
                        project(stage, i, h2, slice(0, 2 * T))
                    elif i <= QT:
                        project(stage, i, h2, slice(0, n_q))
                    else:
                        project_tokens(stage, i, h2, 4 if i == QT + 1 else n_q // P)
                    if i == 6:
                        pe.wait_ge(proj_free, tile0[stage] + 5)
                        for j in range(5):
                            mm = nc.tensor.matmul(ps[:, j // 2, j % 2 * T:j % 2 * T + T], const1("rot"), raw[:, j, 0:T],
                                                  start=True, stop=True)
                        mm.then_inc(rope_rot, 1)
                for which in ([0, 1] if l == 0 else [0]):
                    fourier(fcall, l, which)
                    attention(fcall, l, which)
                    fcall += 1
                if l == 0:
                    ada_turn(1, ADA - 1)
                    pe.wait_ge(ada_free, LAYERS * ADA)
                pe.wait_ge(at_o, fcall * 8)
                for i in range(KD):
                    project(f"out1{l}", i, mixin, slice(0, n_q))
                for which in ([0, 1] if l == 0 else [0]):
                    norm(("post_mix", l, which))
                    norm(("pre_ffn", l, which))
                    ffn(2 * l + which, ("pre_ffn", l, which))
                    norm(("post_ffn", l, which))

            heads = [(slice(0, 64), 0), (slice(64, 128), 1)]

            for l in range(LAYERS):
                norm(("ffn1", l, 0))
                ffn(3 + 2 * l, ("ffn1", l, 0))
                norm(("mix", l, 0))
                pe.wait_ge(norm_out, n_id[("mix", l, 0)] + 1)
                p0, c0 = tile0[f"proj2{l}"], chunk0[f"proj2{l}"]

                def tiles(first, count):
                    with pe.Fori(0, count // 4) as i:
                        for u in range(4):
                            t, c = first + u, c0 + (first + u) // 2
                            slot = c % 2
                            if u % 2 == 0:
                                chunk_here(c, slot, i)
                            pe.wait_ge(proj_free, i * 4 + (p0 + t - 1))
                            for k in range(KD):
                                mm = nc.tensor.matmul(ps[:, 4 + (p0 + t) % 2, 0:T], ring_a[:, slot, u % 2, k, :],
                                                      hn[:, k, :], start=(k == 0), stop=(k == KD - 1))
                            tile_done(mm, f"proj2{l}", u)

                tiles(0, 28)
                wa_up, g_up, m_up = (small[:, SM[n][0]:SM[n][1]] for n in ("waup", "gup", "mup"))
                pe.wait_ge(rw_a, RA.at("sgx", l))
                pe.wait_ge(small_loaded, 16 * (l + 1))
                half = lambda j: slice(j % 2 * T, j % 2 * T + T)
                cols = lambda j: slice(j * P, j * P + P)
                for j in range(QT):
                    mm = nc.tensor.matmul(ps[:, j // 2, half(j)], wa_up[0:64, cols(j)], tmp[0:64, 0, :],
                                          start=True, stop=True)
                mm.then_inc(rw_p, 1)
                for j in range(QT):
                    mm = nc.tensor.matmul(ps[:, 2 + j // 2, half(j)], wa_up[64:128, cols(j)], z[64:128, XWA, 1:T + 1],
                                          start=True, stop=True)
                mm.then_inc(rw_p, 1)
                for j in range(QT):
                    nc.tensor.matmul(ps[:, 6 + j // 2, half(j)], g_up[:, cols(j)], tmp[:, 1, :], start=True, stop=False)
                    mm = nc.tensor.matmul(ps[:, 6 + j // 2, half(j)], m_up[0:32, cols(j)], tmp[0:32, 2, :],
                                          start=False, stop=True)
                mm.then_inc(rw_p, 1)
                tiles(28, 8)
                if l:
                    pe.wait_ge(rw_a, RA.at("sw", l))
                    for j in range(QT):
                        mm = nc.tensor.matmul(ps[:, j // 2, half(j)], m_up[VROW:P, cols(j)], z[VROW:P, MISC, 1:T + 1],
                                              start=True, stop=True, tile_position=(VROW, 0))
                    mm.then_inc(vres_p, 1)
                pe.wait_ge(rw_v, RV.at("kq", l))
                pe.wait_ge(rw_a, RA.at("aa", l))
                hs = const("headsum")
                for j in range(QT):
                    mm = nc.tensor.matmul(ps[0:8, 2, 0:T], hs[:, j * 8:(j + 1) * 8], bon[:, j, :],
                                          start=(j == 0), stop=(j == QT - 1))
                mm.then_inc(rw_p, 1)
                tiles(36, 4)
                pe.wait_ge(rw_v, RV.at("rn", l))
                if l:
                    pe.wait_ge(vres_a, 1)
                hr = const("headrow")
                for j in range(QT):
                    mm = nc.tensor.matmul(ps[:, j // 2, half(j)], hr[0:8, cols(j)], inv_norm, start=True, stop=True)
                mm.then_inc(rw_p, 1)
                for t in range(40, ZT + QT):
                    if t < ZT:
                        project(f"proj2{l}", t, hn, slice(0, T))
                    else:
                        project_tokens(f"proj2{l}", t, hn, 2)
                pe.wait_ge(rw_v, RV.at("rkr", l))
                for j in range(QT):
                    mm = nc.tensor.matmul(ps[:, 2 + j // 2, half(j)], const("headones"), bon[:, j, :],
                                          start=True, stop=True)
                mm.then_inc(rw_p, 1)

                def to_tokens(src, bank):
                    for j in range(QT):
                        for b in range(2):
                            mm = nc.tensor.transpose(ps[:, bank + j // 2, (j % 2 * 2 + b) * P:(j % 2 * 2 + b + 1) * P],
                                                     src[:, j, b * P:(b + 1) * P], ident)
                    return mm

                pe.wait_ge(rw_v, RV.at("bon", l))
                to_tokens(z[:, V0:V0 + QT, 1:T + 1], 2).then_inc(rw_p, 1)
                pe.wait_ge(rw_a, RA.at("gg", l))
                pe.wait_ge(proj_free, p0 + ZT + QT)
                nc.tensor.matmul(ps[0:4, 6, 0:T], const("seli"), z[:, MISC, 1:T + 1], start=True, stop=True)
                nc.tensor.matmul(ps[0:4, 6, T:2 * T], const("self"), z[:, MISC, 1:T + 1], start=True, stop=True)\
                    .then_inc(ml_p, 1)
                pe.wait_ge(rw_v, RV.at("bhc", l))
                to_tokens(khc, 0).then_inc(rw_p, 1)
                to_tokens(bhc, 4).then_inc(rw_p, 1)

                pe.wait_ge(ml_v, MVS.at("fm", l))
                pe.wait_ge(ml_a, MA.at("silu", l))
                pe.wait_ge(rw_a, RA.at("bhct", l))

                def front(h):
                    r, o = l * 4 + h, h % 2
                    pick = ident[0:4, h:h + 1]
                    g, neg_m, f_m = (rows4[0:4, i, :] for i in (6, 0, 1))
                    if h >= 2:
                        pe.wait_ge(mh_am, r - 1)
                    for b in range(2):
                        c = slice(0, T) if b == 0 else slice(T, T + P)
                        w = c.stop - c.start
                        nc.tensor.matmul(ps[:, o, c], g[:, b * P:(b + 1) * P], pick.to_broadcast([4, w]),
                                         start=True, stop=False)
                        mm = nc.tensor.matmul(ps[:, o, c], pick.to_broadcast([4, P]), neg_m[:, b * P:T],
                                              start=False, stop=True)
                    mm.then_inc(mh_arg, 1)
                    if h >= 2:
                        pe.wait_ge(mh_pm, r - 1)
                    for b in range(2):
                        c = slice(0, T) if b == 0 else slice(T, T + P)
                        mm = nc.tensor.matmul(ps[:, 2 + o, c], nsq[:, QT + h, b * P:(b + 1) * P], nsq[:, h, b * P:T],
                                              start=True, stop=True)
                    mm.then_inc(mh_s, 1)
                    if h >= 2:
                        pe.wait_ge(mh_ems, r - 1)
                    nc.tensor.matmul(ps[:, 4 + o, 0:T], pick.to_broadcast([4, P]), f_m, start=True, stop=True)\
                        .then_inc(mh_em, 1)

                front(0)
                for h in range(4):
                    r, o = l * 4 + h, h % 2
                    if h < 3:
                        front(h + 1)
                    pe.wait_ge(mh_pm, r + 1)
                    if h >= 2:
                        pe.wait_ge(mh_h, r - 1)
                    for c0_, left in ((0, lambda b: mv[:, b, h * P:(h + 1) * P]), (T, lambda b: ones)):
                        nc.tensor.matmul(ps[:, 6 + o, c0_:c0_ + T], left(0), pm[:, o, 0:T], start=True, stop=False)
                        mm = nc.tensor.matmul(ps[:, 6 + o, c0_ + P:c0_ + T], left(1), pm[:, o, T:T + P],
                                              start=False, stop=True)
                    mm.then_inc(mh_nd, 1)
                pe.wait_ge(mh_h, l * 4 + 4)
                for j in range(QT):
                    mm = nc.tensor.matmul(ps[:, j // 2, half(j)], ones, hN[:, j, :], start=True, stop=True)
                mm.then_inc(ml_p, 1)
                pe.wait_ge(ml_a, MA.at("hq", l))
                for j in range(QT):
                    mm = nc.tensor.matmul(ps[:, 2 + j // 2, half(j)], ones, hN[:, j, :], start=True, stop=True)
                mm.then_inc(ml_p, 1)

                pe.wait_ge(rw_v, RV.at("bhc", l))

                def unit(v, u, h):
                    j, c = u // NC_, u % NC_
                    return v[h * HD:h * HD + HD, j, c * CHUNK:(c + 1) * CHUNK]

                def out_unit(bank, u, h):
                    return ps[h * HD:h * HD + HD, bank + u // 8, u % 8 * CHUNK:(u % 8 + 1) * CHUNK]

                def per_unit(bank, left, right, us=range(UNITS)):
                    for u in us:
                        for h in range(2):
                            mm = nc.tensor.matmul(out_unit(bank, u, h), unit(left, u, h), unit(right, u, h),
                                                  start=True, stop=True)
                    return mm

                rt = z[:, R0:R0 + QT, 1:T + 1]
                per_unit(4, bh, kt).then_inc(rw_p, 1)
                pe.wait_ge(ml_v, MVS.at("hc", l))
                per_unit(0, kt, bh).then_inc(rw_p, 1)
                per_unit(6, kh, kt).then_inc(rw_p, 1)
                pe.wait_ge(ml_a, MA.at("hsd", l))
                per_unit(2, kh, rt).then_inc(rw_p, 1)
                pe.wait_ge(rw_v, RV.at("at", l))
                per_unit(4, bh, rt).then_inc(rw_p, 1)

                pe.wait_ge(rw_v, RV.at("art", l))
                for i in range(len(LEVELS)):
                    step = l * len(LEVELS) + i
                    pe.wait_ge(lev_g, step + 1)
                    for b in range(2):
                        if i:
                            pe.wait_ge(lev_v, LV.at(f"xt{b}", step - 1))
                        per_unit(0, aoff, xs, range(b * 8, b * 8 + 8)).then_inc(lev_p, 1)
                    for b in range(2):
                        us = range(b * 8, b * 8 + 8)
                        pe.wait_ge(lev_a, LA.at(f"w{b}", step))
                        per_unit(2, xt, ws, us)
                        per_unit(4, ws, xt, us).then_inc(lev_p, 1)

                pe.wait_ge(lev_v, LV.at("xt1", l * len(LEVELS) + len(LEVELS) - 1))
                pe.wait_ge(rw_a, RA.at("bhct", l))
                for c in range(NC_):
                    step = l * NC_ + c

                    def sums(out, pairs):
                        for j in range(QT):
                            for h in range(2):
                                rows = slice(h * HD, h * HD + HD)
                                for i, (left, right) in enumerate(pairs):
                                    mm = nc.tensor.matmul(out(j, rows), left(j, rows), right(j, rows), start=(i == 0),
                                                          stop=(i == len(pairs) - 1))
                        return mm

                    def here(v):
                        return lambda j, rows: v[rows, j, c * CHUNK:(c + 1) * CHUNK]

                    old = lambda j, rows: state[rows, c % 2, j, :]
                    narrow = lambda bank: lambda j, rows: ps[rows, bank, j * HD:(j + 1) * HD]
                    if c:
                        pe.wait_ge(ch_v, CV.at("s", step - 1))
                    carried = [(here(kt), old)] if c else []
                    sums(narrow(0), [(here(mt), here(v_t))] + carried).then_inc(ch_p, 1)
                    pe.wait_ge(ch_a, step + 1)
                    sums(narrow(1), [(here(xt), here(rr))]).then_inc(ch_p, 1)
                    pe.wait_ge(ch_v, CV.at("nu", step))
                    sums(narrow(4), [(here(khc_t), here(v_t)), (here(bhc_t), here(nu))]).then_inc(ch_p, 1)
                    carried = [(here(rt), old)] if c else []
                    sums(lambda j, rows: ps[rows, 2 + j // 2, j % 2 * T + c * CHUNK:j % 2 * T + (c + 1) * CHUNK],
                         carried + [(here(mrt), here(v_t)), (here(art), here(nu))]).then_inc(ch_p, 1)
                pe.wait_ge(rw_v, RV.at("yn", l))
                for u in range(UNITS):
                    j, c = u // NC_, u % NC_
                    mm = nc.tensor.transpose(ps[0:64, 4 + u // 4, u % 4 * P:(u % 4 + 1) * P],
                                             yy[:, j, c * CHUNK:(c + 1) * CHUNK], ident)
                mm.then_inc(rw_p, 1)

                pe.wait_ge(rw_v, RV.at("ya", l))
                pe.wait_ge(ml_v, MVS.at("yb", l))
                for n in range(KD):
                    c = chunk0[f"br{l}"] + n // 2
                    if n % 2 == 0:
                        chunk_here(c, c % 2)
                    if n >= 2:
                        pe.wait_ge(br_free, l * KD + n - 1)
                    for part, y in enumerate((ya, yb)):
                        for k in range(QT):
                            mm = nc.tensor.matmul(ps[:, 4 + n % 2, part * T:(part + 1) * T],
                                                  ring_a[:, c % 2, n % 2, part * QT + k, :], y[:, k, :],
                                                  start=(k == 0), stop=(k == QT - 1))
                    mm.then_inc(a_used if n % 2 else br_ready, 1)
                pe.wait_ge(br_free, (l + 1) * KD)
                for n in range(KD // 2):
                    c = chunk0[f"out2{l}"] + n
                    chunk_here(c, c % 2)
                    for i in range(2):
                        for k in range(KD):
                            mm = nc.tensor.matmul(ps[:, n, i * T:(i + 1) * T], ring_a[:, c % 2, i, k, :], umix[:, k, :],
                                                  start=(k == 0), stop=(k == KD - 1))
                    mm.then_inc(a_used, 1)
                norm(("ffn2", l, 0))
                ffn(4 + 2 * l, ("ffn2", l, 0))
            norm(("final", 0, 0))


def tiles_of(w):
    k, n = w.shape
    return w.reshape(k // P, P, n // P, P).transpose(2, 1, 0, 3)


def chunks_of(tiles):
    if len(tiles) % 2:
        tiles = np.concatenate([tiles, np.zeros_like(tiles[:1])])
    n, p, k, c = tiles.shape
    return tiles.reshape(n // 2, 2, p, k, c).transpose(0, 2, 1, 3, 4).reshape(n // 2, p, -1)


def columns(v):
    return np.asarray(v).reshape(-1, P).T


def lay_out(a):
    zeros = lambda *s: np.zeros(s, np.float32)
    ffn_chunks = lambda g, u: np.stack([tiles_of(g), tiles_of(u)], 1).reshape(-1, P, KD, P)
    wa = [chunks_of(tiles_of(a["w_ada"][l])) for l in range(LAYERS)]
    q_heads = [h for j in range(4) for h in (j, j + 4)]
    q_cols = np.concatenate([np.arange(h * HD, h * HD + HD) for h in q_heads])
    for l in range(LAYERS):
        w = a["w_in"][l]
        w = np.concatenate([w[:, 512:640], w[:, q_cols], w[:, 640:768], w[:, 768:1280]], 1)
        w_out = np.concatenate([a["w_out"][l][q_cols], a["w_out"][l][512:]], 0)
        wa += [chunks_of(tiles_of(w)), chunks_of(tiles_of(w_out)),
               chunks_of(ffn_chunks(a["w_gate"][l], a["w_up"][l]))]
    small, mus = [], []
    for l in range(LAYERS):
        w = a["w_in_2"][l]
        at = 0
        part = {}
        for name, n in (("r", 512), ("k", 512), ("v", 512), ("xw", 64), ("xa", 64), ("xg", 160), ("mq", 512),
                        ("mk", 512), ("mv", 512), ("mo", 512), ("mi", 4), ("mf", 4), ("g", 2048)):
            part[name] = w[:, at:at + n]
            at += n
        down = a["vres_down_2"][l - 1] if l else zeros(D, 32)
        misc = np.concatenate([part["xg"][:, P:], part["mi"], zeros(D, 28), part["mf"], zeros(D, 28), down], 1)
        w = np.concatenate([part["r"], part["k"], part["v"], part["xw"], part["xa"], part["xg"][:, :P], misc,
                            part["mq"], part["mk"], part["mo"], part["g"], part["mv"]], 1)
        br = np.concatenate([tiles_of(a["br_a_2"][l]), tiles_of(a["br_b_2"][l])], 2)
        f1, f2 = a["ffn1_w_in_2"][l], a["ffn2_w_in_2"][l]
        wa += [chunks_of(ffn_chunks(f1[:, :FFN], f1[:, FFN:])), chunks_of(tiles_of(w)), chunks_of(br),
               chunks_of(tiles_of(a["w_out_2"][l])), chunks_of(ffn_chunks(f2[:, :FFN], f2[:, FFN:]))]
        up = a["vres_up_2"][l - 1] if l else zeros(32, 512)
        g_up = a["rw_g_up_2"][l]
        small.append(np.concatenate([np.concatenate([a["rw_w_up_2"][l], a["rw_a_up_2"][l]], 0), g_up[:P],
                                     np.concatenate([g_up[P:], zeros(64, 512), up], 0)], 1))
        mu = a["shift_mu_2"][l]
        mus.append(np.concatenate([mu, zeros(96)]))
    wd = np.concatenate([a["w_down"], np.stack([a[f"ffn{i}_w_out_2"][l] for l in range(LAYERS) for i in (1, 2)])])
    wd = wd.reshape(-1, P, D)

    vec = {"c": np.stack([a["c"][0].reshape(KD, P), a["c_ctx"].reshape(KD, P)], 1).reshape(-1, P).T,
           "b_ada": columns(a["b_ada"].reshape(-1)), "final": columns(a["final_norm_2"]),
           "vbias1": columns(a["vres_bias_2"][0]),
           "sink": np.broadcast_to(a["sink"].reshape(1, -1), (P, LAYERS * 8))}
    for l in range(LAYERS):
        for name, src in (("pre_mix", "norm_pre_mix"), ("post_mix", "norm_post_mix"), ("pre_ffn", "norm_pre_ffn"),
                          ("post_ffn", "norm_post_ffn"), ("ffn1", "ffn1_norm_2"), ("mix", "mix_norm_2"),
                          ("ffn2", "ffn2_norm_2"), ("conv_b", "ml_conv_b_2"), ("w0", "rw_w0_2"), ("a0", "rw_a0_2"),
                          ("k_k", "rw_k_k_2"), ("k_a", "rw_k_a_2"), ("r_k", "rw_r_k_2"), ("gn_w", "rw_gn_w_2"),
                          ("gn_b", "rw_gn_b_2"), ("ml_w", "ml_norm_w_2")):
            vec[f"{name}{l}"] = columns(a[src][l].reshape(-1))
        for t in range(4):
            vec[f"tap{t}{l}"] = columns(a["ml_conv_w_2"][l, t])
        vec[f"mu{l}"] = columns(mus[l])
        for name, src in (("ib", "ml_i_bias_2"), ("fb", "ml_f_bias_2")):
            vec[f"{name}{l}"] = np.concatenate([a[src][l], zeros(P - 4)])[:, None]
    vec = np.concatenate([vec[n] for n in V], 1)
    four = np.zeros((LAYERS, QT, 2, HD, 2, HD), np.float32)
    w4 = a["w_fourier"].reshape(LAYERS, QT, 2, HD, HD)
    for h in range(2):
        four[:, :, h, :, h, :] = w4[:, :, h]
    four = four.reshape(LAYERS * QT, P, P).transpose(1, 0, 2).reshape(P, -1)
    c1, c2 = constants()
    rows = lambda v: np.asarray(v[0]).T.reshape(KD, P, T).transpose(1, 0, 2)
    full = np.ascontiguousarray
    return {"wa": full(np.concatenate(wa)), "wd": full(wd), "c1": full(c1), "c2": full(c2), "vec": full(vec),
            "small": full(np.stack(small)), "four": full(four), "x": full(rows(a["x"])), "ctx": full(rows(a["ctx"]))}


def kernel(**inputs):
    import concourse.bacc as bacc
    from concourse.bass_utils import run_bass_kernel_spmd

    arrays = lay_out({n: np.asarray(v) for n, v in inputs.items()})
    nc = bacc.Bacc("TRN2", target_bir_lowering=False, num_devices=1)
    args = [nc.dram_tensor(f"in_{n}", v.shape, F32, kind="ExternalInput").ap() for n, v in arrays.items()]
    out = nc.dram_tensor("out", (P, KD, T), F32, kind="ExternalOutput").ap()
    program(nc, *args, out)
    got = run_bass_kernel_spmd(nc, [{f"in_{n}": v for n, v in arrays.items()}], core_ids=[0])
    return np.ascontiguousarray(got.results[0]["out"].transpose(2, 1, 0).reshape(1, T, D))
```

```python
from contextlib import ExitStack

import numpy as np

import concourse.bass as bass
from concourse import mybir

F32 = mybir.dt.float32
F32R = mybir.dt.float32r
ALU = mybir.AluOpType
ACT = mybir.ActivationFunctionType
AX_X = mybir.AxisListType.X

P = 128
D = 1024
T = 256
KD = D // P
LAYERS = 2
FFN = 2816
FT = FFN // P
NMOD = 6 * KD
HD = 64
QT = 4
CHUNK = 64
NC_ = T // CHUNK
UNITS = QT * NC_
RMS_EPS, GN_EPS, ML_EPS = 1e-6, 64e-5, 1e-5

R0, K0, V0, XWA, XG, MISC, MQ, MK, MO, MV, GATES = 0, 4, 8, 12, 13, 14, 15, 19, 23, 27, 31
ZT = MV
NT2 = GATES + 2 * KD
MIXED = MISC + 1
XG2, IROW, FROW, VROW = 0, 32, 64, 96

A_ADA = 0
ADA_FIRST = KD
ADA_EARLY = ADA_FIRST - 2
ADA_FILL = 2
ADA_STEP0, ADA_STEP1 = 9, 12
A_B1 = [LAYERS * NMOD // 2]
PROJ1, OUT1 = 5, 4
B1_LAYER = PROJ1 + OUT1 + FT
A_B1.append(A_B1[0] + B1_LAYER)
PROJ2, BR2, OUT2 = 24, 4, 4
B2_LAYER = FT + PROJ2 + BR2 + OUT2 + FT
A_B2 = [A_B1[1] + B1_LAYER, A_B1[1] + B1_LAYER + B2_LAYER]
N_A = A_B2[1] + B2_LAYER


WORK = 27000
PIECES = 4


def spans(widths):
    at, out = 0, {}
    for name, w in widths:
        out[name] = (at, at + w)
        at += w
    return out, at


C1, C1_N = spans([("cos", T), ("sin", T), ("rot", P), ("dft", 2 * 2 * T), ("chc", P), ("chs", P),
                  ("win", 2 * 2 * T)])
LEVELS = [2, 4, 8, 16, 32]
C2, C2_N = spans([("ident", P), ("ones", P), ("headones", P), ("headsum", QT * 8), ("headrow", QT * P),
                  ("restart", T), ("strict", CHUNK), ("incl", CHUNK), ("low1", CHUNK), ("up1", CHUNK),
                  ("eye", CHUNK)] + [(f"lev{m}", CHUNK) for m in LEVELS]
                 + [("tri", T + P), ("seli", 4), ("self", 4),
                    ("eps_rms", 1), ("eps_gn", 1), ("eps_ml", 1), ("one", 1)])
V, V_N = spans([("c", 2 * KD), ("b_ada", LAYERS * NMOD)]
               + [(f"{n}{l}", KD) for n in ("pre_mix", "post_mix", "pre_ffn", "post_ffn", "ffn1", "mix", "ffn2",
                                            "conv_b", "tap0", "tap1", "tap2", "tap3") for l in range(LAYERS)]
               + [("final", KD)]
               + [(f"mu{l}", MIXED) for l in range(LAYERS)]
               + [(f"{n}{l}", QT) for n in ("w0", "a0", "k_k", "k_a", "r_k", "gn_w", "gn_b", "ml_w")
                  for l in range(LAYERS)]
               + [("vbias1", QT)] + [(f"{n}{l}", 1) for n in ("ib", "fb") for l in range(LAYERS)]
               + [("sink", LAYERS * 8)])
SM, SM_N = spans([("waup", 512), ("gup", 512), ("mup", 512)])


def constants():
    pos = np.arange(T)
    rows = T // 64
    row = np.repeat(np.arange(rows), 64).astype(np.float32)
    col = np.tile(np.arange(64), rows).astype(np.float32)
    freqs = (np.float32(10000.0) ** (-np.arange(16, dtype=np.float32) / np.float32(16))).astype(np.float32)
    ang = np.concatenate([row[:, None] * freqs, col[:, None] * freqs], axis=-1)
    pair = (np.arange(P) % HD) // 2
    rot = np.zeros((P, P))
    even = np.arange(0, P, 2)
    rot[even + 1, even] = -1.0
    rot[even, even + 1] = 1.0
    turn = 2 * np.pi * np.outer(pos, pos) % (2 * np.pi * T) / T
    dft = np.concatenate([np.cos(turn), np.sin(turn)], 1).reshape(2, P, 2 * T).transpose(1, 0, 2).reshape(P, -1)
    ch = 2 * np.pi * (np.outer(np.arange(HD), np.arange(HD)) % HD) / HD
    norm = 1.0 / np.sqrt(T * HD)
    two = np.kron(np.eye(2), np.ones((HD, HD)))
    chc, chs = (np.kron(np.eye(2), f(ch) * norm) for f in (np.cos, np.sin))
    win = np.zeros((P, 2, 2 * T))
    for b in range(2):
        q = b * P + np.arange(P)
        win[:, b, :T] = np.where(np.abs(q[:, None] - pos[None]) <= 128, 0.0, -1e30)
    c1 = dict(cos=np.cos(ang).T[pair], sin=np.sin(ang).T[pair], rot=rot, dft=dft, chc=chc, chs=-chs,
              win=win.reshape(P, -1))
    s = (np.arange(P) % CHUNK)[:, None]
    t = np.arange(CHUNK)[None]
    tall = lambda m: np.broadcast_to(m, (P, CHUNK)).astype(np.float32)
    block = lambda m: tall((s // (2 * m) == t // (2 * m)) & (s // m % 2 == 0) & (t // m % 2 == 1))
    headsum = np.zeros((P, QT, 8))
    headrow = np.zeros((P, QT, P))
    for j in range(QT):
        for h in range(2):
            headsum[h * HD:(h + 1) * HD, j, 2 * j + h] = 1.0
            headrow[2 * j + h, j, h * HD:(h + 1) * HD] = 1.0
    tri = np.zeros((P, T + P))
    later = np.where(np.arange(P)[:, None] <= np.arange(P)[None], 0.0, -1e30)
    tri[:, :P] = later
    tri[:, T:] = later
    seli, self_ = np.zeros((P, 4)), np.zeros((P, 4))
    for h in range(4):
        seli[IROW + h, h] = 1.0
        self_[FROW + h, h] = 1.0
    c2 = dict(ident=np.eye(P), ones=np.ones((P, P)), headones=two, headsum=headsum.reshape(P, -1),
              headrow=headrow.reshape(P, -1),
              restart=np.broadcast_to((pos % CHUNK != 0).astype(np.float32), (P, T)),
              strict=tall(s < t), incl=tall(s <= t), low1=tall((s == t + 1) & (t % 2 == 0)), up1=block(1),
              eye=tall(s == t), tri=tri, seli=seli,
              eps_rms=np.full((P, 1), RMS_EPS), eps_gn=np.full((P, 1), GN_EPS), eps_ml=np.full((P, 1), ML_EPS),
              one=np.ones((P, 1)), **{f"lev{m}": block(m) for m in LEVELS}, **{"self": self_})
    side = lambda part, where: np.concatenate([part[n] for n in where], 1).astype(np.float32)
    return side(c1, C1), side(c2, C2)


class Steps:

    def __init__(self, names):
        self.place = {n: i + 1 for i, n in enumerate(names)}
        self.count = len(names)

    def at(self, name, rnd):
        return rnd * self.count + self.place[name]


def program(nc, wa, wd, c1_in, c2_in, vec_in, small_in, four_in, x_in, ctx_in, out):
    with ExitStack() as ctx:
        def sb(name, *shape, dtype=F32):
            return ctx.enter_context(nc.sbuf_tensor(name, [P, *shape], dtype))

        def sem(name):
            return ctx.enter_context(nc.semaphore(name))

        ring_a = sb("ring_a", 2, 2, KD, P)
        ring_d = sb("ring_d", 2, KD, P)
        x = sb("x", KD, T)
        nsq = sb("nsq", KD, T)
        nrt = sb("nrt", T)
        rstd = sb("rstd", T)
        warm = sb("warm", 32)
        sg = sb("sg", 2, T)
        hid = sb("hid", 2, T)
        c2 = sb("c2", C2_N)
        vec = sb("vec", V_N)
        mod = sb("mod", LAYERS * NMOD, 2)
        gain = sb("gain", LAYERS, 4, KD, 2)
        cs = sb("cs", KD, 2)
        omka = sb("omka", LAYERS * QT)
        ada_rows = sb("ada_rows", 2, 2 * P)
        vfirst = sb("vfirst", QT, T)
        h_hi, h_lo = (sb(n, KD, T, dtype=F32R) for n in ("h_hi", "h_lo"))
        t_hi, t_lo = (sb(n, 2, KD, P, dtype=F32R) for n in ("t_hi", "t_lo"))
        with nc.sbuf_tensor("work", [P, WORK], F32) as work:
            pass
        w_hi, w_lo = (sb(n, 2, 2, KD, P, dtype=F32R) for n in ("w_hi", "w_lo"))
        d_hi, d_lo = (sb(n, 2, KD, P, dtype=F32R) for n in ("d_hi", "d_lo"))
        hid_hi, hid_lo = (sb(n, 2, T, dtype=F32R) for n in ("hid_hi", "hid_lo"))
        SPLIT = 3 * 2 * 2 * KD * P + 2 * 2 * T
        ps = ctx.enter_context(nc.psum_tensor("ps", [P, 8, 512], F32))

        def const(name):
            return c2[:, C2[name][0]:C2[name][1]]

        def vcol(name, k):
            return vec[:, V[name][0] + k:V[name][0] + k + 1]

        top = [0]

        def place(*shape):
            n = int(np.prod(shape))
            v = work[:, top[0]:top[0] + n]
            top[0] += n
            assert top[0] <= WORK, top[0]
            if len(shape) == 1:
                return v
            if len(shape) == 2:
                return v.rearrange("p (a b) -> p a b", b=shape[1])
            return v.rearrange("p (a b c) -> p a b c", b=shape[1], c=shape[2])

        def units(v):
            return v.rearrange("p j (c t) -> p (j c) t", t=CHUNK)

        h2 = place(KD, 2 * T)
        mixin = h2
        rtmp = place(5, T)
        qr = place(QT, T)
        kall = place(2 * T)
        v_tok = place(4, P)
        s_sb = place(2, 2 * T)
        probs = place(2, 2 * T)
        pn = place(2, 2 * T)
        pt = place(2, 4, P)
        tiny = place(2, 8)
        fm = place(QT, T)
        top[0] = max(top[0], SPLIT)
        early = work[:, 0:ADA_EARLY * 2 * KD * P].rearrange("p (g a b c) -> p g a b c", a=2, b=KD, c=P)
        fu = place(QT, 2 * T)
        hn = work[:, top[0] - KD * T:top[0]].rearrange("p (a b) -> p a b", b=T)
        xc = place(KD, T)
        shared = top[0]
        raw = place(5, 2 * T)
        u_tok = place(4, 512)
        top[0] = max(top[0], shared + KD * 2 * T)
        mix = work[:, shared:shared + KD * 2 * T].rearrange("p (a b) -> p a b", b=2 * T)
        c1 = place(C1_N)
        wfour = place(LAYERS * QT, P)

        def const1(name):
            return c1[:, C1[name][0]:C1[name][1]]

        top[0] = 0
        S_ = [place(QT, T) for _ in range(12)]
        lw, aa, vg, gg, bon, lcum, e1, e2, e0, kk, bb, tmp = S_
        slot0 = top[0]
        diff = work[:, slot0:slot0 + 15 * T].rearrange("p (a b) -> p a b", b=T)
        at_, art, ws, aoff = (place(QT, T) for _ in range(4))
        assert top[0] >= SPLIT
        z = place(ZT, T + 1)
        mt, mrt = (z[:, a:a + QT, 1:T + 1] for a in (K0, V0))
        gate_a, gate_b = nsq, z[:, MQ:MQ + KD, 1:T + 1]
        mv = place(2, 512)
        small = place(SM_N)
        rows_at = top[0]
        state = place(2, QT, HD)
        sdec = place(QT, HD)
        kt, bh, kh, khc, bhc = kk, bb, e0, lw, aa
        khc_t, bhc_t, v_t = vg, lcum, e2
        xs, xt = tmp, khc
        rr, nu, yy, yq = ws, aoff, at_, xs
        small_y = place(8, UNITS)
        am, ee, pm = (v.rearrange("p a b -> p (a b)")[:, 0:2 * (T + P)].rearrange("p (a b) -> p a b", b=T + P)
                      for v in (bh, kh, ws))
        dn, ems = aoff[:, 0:2, :], aoff[:, 2:4, :]
        hN = aa
        hc = mv.rearrange("p a b -> p (a b)").rearrange("p (a b) -> p a b", b=T)
        rows4 = work[0:4, rows_at:rows_at + 3 * T].rearrange("p (a b) -> p a b", b=T)
        row_m, row_f, row_g = (rows4[:, i, :] for i in range(3))
        ya, yb = gg, bhc
        inv_norm = tmp[0:8, 3, :]
        umix = work[:, 6 * QT * T:8 * QT * T].rearrange("p (a b) -> p a b", b=T)

        a_loaded = [sem("a_loaded0"), sem("a_loaded1")]
        d_loaded = [sem("d_loaded0"), sem("d_loaded1")]
        a_used, d_used = sem("a_used"), sem("d_used")
        early_loaded = [sem(f"early_loaded{i}") for i in range(ADA_EARLY)]
        in_loaded, vec_loaded, c2_loaded, const_loaded, small_loaded, out_stored = (
            sem(n) for n in ("in_loaded", "vec_loaded", "c2_loaded", "const_loaded", "small_loaded", "out_stored"))
        cs_ready, ada_early, ada_row, ada_turned, ada_free, gain_ready = (
            sem(n) for n in ("cs_ready", "ada_early", "ada_row", "ada_turned", "ada_free", "gain_ready"))
        onto_scaled, onto_part = sem("onto_scaled"), sem("onto_part")
        norm_sq, norm_sum, norm_rt, norm_rstd, norm_scaled, norm_out = (
            sem(n) for n in ("norm_sq", "norm_sum", "norm_rt", "norm_rstd", "norm_scaled", "norm_out"))
        proj_ready, proj_free = sem("proj_ready"), sem("proj_free")
        hi_a, hi_d, v_ready, hh_ready, hl_ready = (
            sem(n) for n in ("hi_a", "hi_d", "v_ready", "hh_ready", "hl_ready"))
        gu_done, dn_done, sg_ready, hid_mul, hid_rounded, hid_ready, ffn_out = (
            sem(n) for n in ("gu_done", "dn_done", "sg_ready", "hid_mul", "hid_rounded", "hid_ready", "ffn_out"))
        resid = sem("resid")
        rope_rot, rope_sin, rope_cos, rope_out = (sem(n) for n in ("rope_rot", "rope_sin", "rope_cos", "rope_out"))
        fo_dft, fo_fu, fo_ch, fo_fm, fo_w, fo_out = (
            sem(n) for n in ("fo_dft", "fo_fu", "fo_ch", "fo_fm", "fo_w", "fo_out"))
        at_sc, at_s, at_mx, at_nm, at_exp, at_den, at_rd, at_pn, at_tr, at_pt, at_pv, at_o = (
            sem(f"at_{n}") for n in ("sc", "s", "mx", "nm", "exp", "den", "rd", "pn", "tr", "pt", "pv", "o"))
        z_zero, kab = sem("z_zero"), sem("kab")
        rw_v, rw_a, rw_p, vres_v, vres_a, vres_p, lev_v, lev_a, lev_p, lev_g, ch_v, ch_a, ch_p = (
            sem(n) for n in ("rw_v", "rw_a", "rw_p", "vres_v", "vres_a", "vres_p", "lev_v", "lev_a", "lev_p", "lev_g",
                             "ch_v", "ch_a", "ch_p"))
        ml_v, ml_a, ml_p = (sem(n) for n in ("ml_v", "ml_a", "ml_p"))
        mh_arg, mh_s, mh_em, mh_nd, mh_am, mh_pm, mh_ee, mh_ems, mh_dn, mh_abs, mh_rc, mh_h = (
            sem(f"mh_{n}") for n in ("arg", "s", "em", "nd", "am", "pm", "ee", "ems", "dn", "abs", "rc", "h"))
        t_hi_ready, t_half, t_even, t_done, t_free = (
            sem(n) for n in ("t_hi_ready", "t_half", "t_even", "t_done", "t_free"))
        br_ready, br_part, br_free = (sem(n) for n in ("br_ready", "br_part", "br_free"))

        RV = Steps(["diff", "mix", "kk", "kq", "lw", "scan", "ka", "kp", "rkr", "rnmax", "rn", "l0", "kkn", "b", "bon",
                    "kt", "bh", "kh", "rt", "khc", "bhc", "at", "x1", "xt1", "x", "xt", "mrt", "mt", "art",
                    "s1", "ym", "yc", "yq", "s2", "yr", "yn", "gn", "gb", "ya"])
        RA = Steps(["tanh", "sgx", "sw", "aa", "gg", "rsq", "e0", "e1", "e2", "vt", "khct", "bhct", "ysd", "yT"])
        RP = Steps(["lw", "la", "lg", "ss", "rnb", "bon", "vt", "khct", "bhct", "at", "a", "mrt", "mt", "art", "yT"])
        VV = Steps(["d", "m", "v"])
        LP = Steps(["w0", "w1", "x0", "x1"])
        LV = Steps(["x0", "x1"])
        LA = Steps(["w0", "w1"])
        CP = Steps(["r", "u", "s", "y"])
        CV = Steps(["dec", "nu", "s"])
        MVS = Steps(["c0", "c1", "c2", "c3", "mn", "lf", "F", "g", "M", "fm", "nm", "hc"]
                    + [f"{n}{j}" for j in range(QT) for n in ("rec", "hs", "yb")])
        MA = Steps(["ab", "ex", "ln", "silu", "hq", "hsd", "so"])
        MP = Steps(["if", "mu", "var"])

        n_id = {}
        order = []
        for l in range(LAYERS):
            order += [("pre_mix", l, 0), ("pre_mix", l, 1)]
            order += [("post_mix", l, 0), ("pre_ffn", l, 0), ("post_ffn", l, 0)]
            if l == 0:
                order += [("post_mix", l, 1), ("pre_ffn", l, 1), ("post_ffn", l, 1)]
        for l in range(LAYERS):
            order += [("ffn1", l, 0), ("mix", l, 0), ("ffn2", l, 0)]
        order.append(("final", 0, 0))
        split_id = {key: i for i, key in enumerate(k for k in order if k[0] in ("pre_ffn", "ffn1", "mix", "ffn2"))}
        n_two, onto_id = {}, {}
        for i, key in enumerate(order):
            n_id[key] = i
            if key[0] == "pre_mix":
                n_two[key] = len(n_two)
            if key[0] in ("post_mix", "post_ffn"):
                onto_id[key] = len(onto_id)
        ffns = [(0, 0), (0, 1), (1, 0)] + [(2, 0), (3, 0), (4, 0), (5, 0)]
        a_dram_ffn = [A_B1[0] + PROJ1 + OUT1, A_B1[1] + PROJ1 + OUT1,
                      A_B2[0], A_B2[0] + FT + PROJ2 + BR2 + OUT2, A_B2[1], A_B2[1] + FT + PROJ2 + BR2 + OUT2]
        ada_parts = [("0", ADA_FIRST - ADA_EARLY), ("early", ADA_EARLY), ("B0", ADA_FILL), ("L0", 2 * ADA_STEP0), ("M00", ADA_FILL), ("M01", ADA_FILL),
                     ("B1", ADA_FILL), ("L1", ADA_STEP1), ("M10", ADA_FILL)]
        ada_from, n = {}, 0
        for name, count in ada_parts:
            ada_from[name] = n
            n += count
        assert n == LAYERS * NMOD // 2 and ada_from["M00"] >= NMOD // 2 and ada_from["B1"] >= NMOD // 2 + ADA_FIRST

        def ada_stage(name):
            return (f"ada{name}", A_ADA + ada_from[name], dict(ada_parts)[name], None)

        stages = [ada_stage("0")]
        for l in range(LAYERS):
            stages += [ada_stage(f"B{l}"), (f"proj1{l}", A_B1[l], PROJ1, None), ada_stage(f"L{l}")]
            stages.append((f"out1{l}", A_B1[l] + PROJ1, OUT1, None))
            for call in ([0, 1] if l == 0 else [2]):
                stages += [ada_stage(f"M{l}{call % 2}"), (f"ffn{call}", a_dram_ffn[ffns[call][0]], FT, call)]
        for l in range(LAYERS):
            base = A_B2[l] + FT
            stages += [(f"ffn{3 + 2 * l}", A_B2[l], FT, 3 + 2 * l),
                       (f"proj2{l}", base, PROJ2, None), (f"br{l}", base + PROJ2, BR2, None),
                       (f"out2{l}", base + PROJ2 + BR2, OUT2, None),
                       (f"ffn{4 + 2 * l}", base + PROJ2 + BR2 + OUT2, FT, 4 + 2 * l)]
        chunk0, n = {}, 0
        for name, _, count, _ in stages:
            chunk0[name] = n
            n += count
        tile0, first0, n, m = {}, {}, 0, 0
        for name, count in [(f"{s}1{l}", t) for l in range(LAYERS) for s, t in (("proj", 10), ("out", KD))]:
            tile0[name], first0[name] = n, m
            n += count
            m += count // 2

        def ada_step(l, which, u):
            steps = (ADA_STEP0, ADA_STEP1)[l]
            return ada_from[f"L{l}"] + which * steps + u - 2 if 2 <= u < 2 + steps else None

        def ada_chunk(g):
            name = [m for m, _ in ada_parts if ada_from[m] <= g][-1]
            return chunk0[f"ada{name}"] + g - ada_from[name]

        def early_chunk(g):
            n = g - ada_from["early"]
            return n if 0 <= n < ADA_EARLY else None

        def fill(name):
            return range(ada_from[name], ada_from[name] + ADA_FILL)

        def wait(eng, semaphore, value, i=None, step=2):
            if i is not None:
                eng.wait_ge(semaphore, i * step + value)
            elif value > 0:
                eng.wait_ge(semaphore, value)

        def gates_at(what, i):
            if what == "mean":
                return [GATES + i]
            if what == "level":
                return [GATES + 2 + 2 * i, GATES + 3 + 2 * i] if i < len(LEVELS) - 1 else []
            return [GATES + 2 * len(LEVELS) + (i if what == "chunk" else NC_ + i)]

        def gate_bank(t):
            return (4 if t < GATES + 2 else 6) + t % 2

        def last_of_chunk(t):
            return t % 2 == 1 or t == NT2 - 1

        def shift_of(l, part, which):
            return lambda k: mod[:, l * NMOD + part * KD + k, which:which + 1]

        def gain_of(l, i, which):
            return lambda k: gain[:, l, i, k, which:which + 1]

        def token_cols(l, which):
            return slice(which * T, which * T + T)

        block = ctx.enter_context(nc.Block())

        @block.sync
        def _(sp):
            def load_a(c, slot, src, wait=True):
                if wait:
                    sp.wait_ge(a_used, c - 1)
                sp.dma_start(ring_a[:, slot].rearrange("p a b c -> p (a b c)"), src).then_inc(a_loaded[slot], 16)

            def load_d(d, slot, src, wait=True):
                if wait:
                    sp.wait_ge(d_used, d - 1)
                sp.dma_start(ring_d[:, slot].rearrange("p a b -> p (a b)"), src).then_inc(d_loaded[slot], 16)

            for name, first, count, call in stages:
                c0 = chunk0[name]
                if call is None:
                    i = 0
                    if c0 == 0:
                        load_a(0, 0, wa[first], wait=False)
                        load_a(1, 1, wa[first + 1], wait=False)
                        for g in range(ADA_EARLY):
                            sp.dma_start(early[:, g].rearrange("p a b c -> p (a b c)"),
                                         wa[A_ADA + ada_from["early"] + g]).then_inc(early_loaded[g], 16)
                        i = 2
                    pairs = (count - i) // 2
                    if pairs:
                        with sp.Fori(0, pairs) as n:
                            for u in range(2):
                                load_a(n * 2 + (c0 + i + u), (c0 + i + u) % 2,
                                       wa[bass.ds(n * 2 + (first + i + u), 1)].rearrange("a p n -> (a p) n"))
                    if (count - i) % 2:
                        load_a(c0 + count - 1, (c0 + count - 1) % 2, wa[first + count - 1])
                    continue
                d0, dd = call * FT, ffns[call][0] * FT
                load_a(c0, c0 % 2, wa[first])
                load_a(c0 + 1, (c0 + 1) % 2, wa[first + 1])
                load_d(d0, d0 % 2, wd[dd], wait=call > 0)
                load_a(c0 + 2, c0 % 2, wa[first + 2])
                load_d(d0 + 1, (d0 + 1) % 2, wd[dd + 1], wait=call > 0)
                with sp.Fori(0, (FT - 4) // 2) as n:
                    for u in range(2):
                        load_a(n * 2 + (c0 + 3 + u), (c0 + 3 + u) % 2,
                               wa[bass.ds(n * 2 + (first + 3 + u), 1)].rearrange("a p n -> (a p) n"))
                        load_d(n * 2 + (d0 + 2 + u), (d0 + 2 + u) % 2,
                               wd[bass.ds(n * 2 + (dd + 2 + u), 1)].rearrange("a p n -> (a p) n"))
                load_a(c0 + FT - 1, (c0 + FT - 1) % 2, wa[first + FT - 1])
                for f in (FT - 2, FT - 1):
                    load_d(d0 + f, (d0 + f) % 2, wd[dd + f])
            sp.wait_ge(norm_out, n_id[("final", 0, 0)] + 1)
            sp.dma_start(out, nsq[:, :, :]).then_inc(out_stored, 16)
            sp.wait_ge(out_stored, 16)

        @block.gpsimd
        def _(pool):
            def rest_h(key):
                sid = split_id[key]
                for k in range(KD):
                    pool.wait_ge(hh_ready, sid * KD + k + 1)
                    nc.gpsimd.tensor_tensor(h_lo[:, k, :], nsq[:, k, :], h_hi[:, k, :].bitcast(F32), ALU.subtract)\
                        .then_inc(hl_ready if k < KD - 1 else norm_out, 1)

            for l, which in ((0, 0), (0, 1), (1, 0)):
                rest_h(("pre_ffn", l, which))
            pool.wait_ge(norm_out, n_id[("post_ffn", 1, 0)] + 1)
            pool.wait_ge(fo_out, 3 * QT)
            nc.gpsimd.memset(z[:, :, 0:1], 0.0).then_inc(z_zero, 1)
            for l in range(LAYERS):
                if l:
                    pool.wait_ge(rw_p, RP.at("lg", l - 1))
                pool.dma_start(small, small_in[l]).then_inc(small_loaded, 16)

                def rest_t(t, i=None):
                    n, c = l * NT2 + t, chunk0[f"proj2{l}"] + t // 2
                    wait(pool, t_hi_ready, n + 1, i, 4)
                    for part in range(2):
                        k = slice(part * KD // 2, (part + 1) * KD // 2)
                        done = t_half if part == 0 else a_used if last_of_chunk(t) else t_even
                        nc.gpsimd.tensor_tensor(t_lo[:, t % 2, k], ring_a[:, c % 2, t % 2, k],
                                                t_hi[:, t % 2, k].bitcast(F32), ALU.subtract).then_inc(done, 1)

                rest_h(("ffn1", l, 0))
                rest_t(0)
                rest_h(("mix", l, 0))
                rest_t(1)
                rest_t(2)
                with pool.Fori(0, NT2 // 4 - 1) as i:
                    for u in range(4):
                        rest_t(3 + u, i)
                for t in range(NT2 - 4, NT2):
                    rest_t(t)
                rest_h(("ffn2", l, 0))

        @block.scalar
        def _(act):
            act.dma_start(vec[:, :], vec_in).then_inc(vec_loaded, 16)
            act.dma_start(c2[:, :], c2_in).then_inc(c2_loaded, 16)
            act.dma_start(x[:, :, :], x_in).then_inc(in_loaded, 16)
            act.dma_start(xc, ctx_in).then_inc(in_loaded, 16)
            act.wait_ge(vec_loaded, 16)
            nc.scalar.activation(cs[:, :, :].rearrange("p k w -> p (k w)"),
                                 vec[:, V["c"][0]:V["c"][1]], ACT.Silu).then_inc(cs_ready, 1)

            def norm(key, src, call=None, ready=None, onto=None, first=None, also=None):
                n = n_id[key]
                if call is not None:
                    round_a(call, 0)
                if first is not None:
                    first()
                for i in range(PIECES):
                    k = slice(i * KD // PIECES, (i + 1) * KD // PIECES)
                    if ready is not None:
                        act.wait_ge(resid, PIECES * ready + i + 1)
                    if onto is not None and i < PIECES - 1:
                        act.wait_ge(onto_part, (PIECES - 1) * onto_id[onto] + i + 1)
                    elif onto is not None:
                        act.wait_ge(norm_out, n_id[onto] + 1)
                    nc.scalar.activation(nsq[:, k, :], src[:, k, :], ACT.Square).then_inc(norm_sq, 1)
                nc.scalar.activation(warm[:, n:n + 1], const("one"), ACT.Sqrt)
                if also is not None:
                    also()
                act.wait_ge(norm_sum, n + 1)
                if n:
                    act.wait_ge(norm_rstd, n)
                nc.scalar.activation(nrt[:, :], ps[:, 6, 0:T], ACT.Sqrt, bias=const("eps_rms"),
                                     scale=1.0 / D).then_inc(norm_rt, 1)

            def round_a(call, f, i=None):
                c, t = chunk0[f"ffn{call}"] + f, call * FT + f
                n = 16 * (c // 2 + 1)
                act.wait_ge(a_loaded[c % 2], n if i is None else i * 16 + n)
                wait(act, gu_done, t - 1, i)
                for part in range(2):
                    nc.scalar.copy(w_hi[:, f % 2, part], ring_a[:, c % 2, part]).then_inc(hi_a, 1)

            def round_d(call, f, i=None):
                d = call * FT + f
                n = 16 * (d // 2 + 1)
                act.wait_ge(d_loaded[d % 2], n if i is None else i * 16 + n)
                wait(act, dn_done, d - 1, i)
                nc.scalar.copy(d_hi[:, f % 2], ring_d[:, d % 2]).then_inc(hi_d, 1)

            def round_h(sid, modulated=None):
                for k in range(KD):
                    act.wait_ge(v_ready, sid * KD + k + 1)
                    if modulated is None:
                        nc.scalar.copy(h_hi[:, k, :], nsq[:, k, :]).then_inc(hh_ready, 1)
                    else:
                        gains, shift = modulated
                        nc.scalar.activation(nsq[:, k, :], hn[:, k, :], ACT.Identity, scale=gains(k), bias=shift(k))
                        nc.scalar.activation(h_hi[:, k, :], hn[:, k, :], ACT.Identity, scale=gains(k), bias=shift(k))\
                            .then_inc(hh_ready, 1)

            def ffn(call):
                round_a(call, 1)
                round_d(call, 0)

                def tile(f, i=None):
                    t = call * FT + f
                    wait(act, gu_done, t + 1, i)
                    wait(act, hid_mul, t - 1, i)
                    nc.scalar.activation(sg[:, f % 2, :], ps[:, 4 + f % 2, 0:T], ACT.Silu).then_inc(sg_ready, 1)
                    if f + 2 < FT:
                        round_a(call, f + 2, i)
                    if f + 1 < FT:
                        round_d(call, f + 1, i)

                tile(0)
                tile(1)
                with act.Fori(0, FT // 2 - 2) as i:
                    tile(2, i)
                    tile(3, i)
                tile(FT - 2)
                tile(FT - 1)

            def tile_ready(stage, i):
                if i % 2:
                    act.wait_ge(a_used, chunk0[stage] + i // 2 + 1)
                else:
                    act.wait_ge(proj_ready, first0[stage] + i // 2 + 1)

            def empty(stage, i, dst, cols=slice(0, T)):
                tile_ready(stage, i)
                src = ps[:, 4 + (tile0[stage] + i) % 2, cols]
                if len(dst.shape) == 3:
                    src = src.rearrange("p (a b) -> p a b", b=P)
                nc.scalar.copy(dst, src).then_inc(proj_free, 1)

            def fourier(call, l, which):
                for j in range(QT):
                    act.wait_ge(fo_dft, call * QT + j + 1)
                    nc.scalar.copy(fu[:, j, :], ps[:, j, :]).then_inc(fo_fu, 1)
                for j in range(QT):
                    act.wait_ge(fo_ch, call * QT + j + 1)
                    nc.scalar.copy(fm[:, j, :], ps[:, j, 0:T]).then_inc(fo_fm, 1)
                for j in range(QT):
                    act.wait_ge(fo_w, call * QT + j + 1)
                    nc.scalar.copy(mixin[:, QT + j, token_cols(l, which)], ps[:, j, T:2 * T]).then_inc(fo_out, 1)

            def attention(call, l, which):
                n_keys = 2 * T if which == 0 else T

                def exps(u):
                    g, h = call * 16 + u, (u % 2) * 4 + (u // 2) % 4
                    act.wait_ge(at_nm, g + 1)
                    if g >= 2:
                        act.wait_ge(at_pn, g - 1)
                    nc.scalar.activation(probs[:, u % 2, 0:n_keys], s_sb[:, u % 2, 0:n_keys], ACT.Exp,
                                         bias=tiny[:, u % 2, 1:2], accum_out=tiny[:, u % 2, 2:3])
                    nc.scalar.activation(tiny[:, u % 2, 3:4], vcol("sink", l * 8 + h), ACT.Exp,
                                         bias=tiny[:, u % 2, 1:2]).then_inc(at_exp, 1)

                def turned(u):
                    g = call * 16 + u
                    act.wait_ge(at_tr, g + 1)
                    if g >= 2:
                        act.wait_ge(at_pv, g - 1)
                    nc.scalar.copy(pt[:, u % 2, 0:n_keys // P, :],
                                   ps[:, 2 + u % 2, 0:n_keys].rearrange("p (a b) -> p a b", b=P)).then_inc(at_pt, 1)

                def out_pair(w):
                    blk, j = w // 4, w % 4
                    act.wait_ge(at_pv, call * 16 + 2 * w + 2)
                    nc.scalar.copy(mixin[:, j, which * T + blk * P:which * T + (blk + 1) * P],
                                   ps[:, 6 + w % 2, 0:P]).then_inc(at_o, 1)

                for u in range(16 + 4):
                    if u < 16:
                        exps(u)
                    if 1 <= u <= 16:
                        turned(u - 1)
                    if u >= 4 and (u - 3) % 2:
                        out_pair((u - 4) // 2)
                    if ada_step(l, which, u) is not None:
                        ada(ada_step(l, which, u))

            def ada(g):
                u = g % 2
                if early_chunk(g) is not None:
                    act.wait_ge(ada_early, early_chunk(g) + 1)
                else:
                    act.wait_ge(a_used, ada_chunk(g) + 1)
                nc.scalar.copy(ada_rows[0:2, u, :], ps[0:2, 4 + u, 0:T]).then_inc(ada_row, 1)

            for g in range(ADA_FIRST):
                ada(g)
                if g == ADA_FIRST - 4:
                    act.wait_ge(in_loaded, 32)
                    act.wait_ge(c2_loaded, 16)
                    norm(("pre_mix", 0, 0), x[:, :, :])
                if g == ADA_FIRST - 3:
                    norm(("pre_mix", 0, 1), xc)
            act.dma_start(c1, c1_in).then_inc(const_loaded, 16)
            act.dma_start(wfour.rearrange("p a b -> p (a b)"), four_in).then_inc(const_loaded, 16)
            fcall = acall = 0
            for l in range(LAYERS):
                if l:
                    norm(("pre_mix", l, 0), x[:, :, :], onto=("post_ffn", 0, 0))
                    norm(("pre_mix", l, 1), xc, onto=("post_ffn", 0, 1))
                for which in range(2):
                    for k in range(KD):
                        act.wait_ge(norm_scaled, n_two[("pre_mix", l, which)] * KD + k + 1)
                        to = h2[:, k, token_cols(l, which)]
                        ins = nc.scalar.activation(to, to, ACT.Identity, bias=shift_of(l, 0, which)(k))
                    ins.then_inc(norm_out, 1)
                for g in fill(f"B{l}"):
                    ada(g)
                stage, n_q, n_blk = f"proj1{l}", (2 * T, T)[l], (4, 2)[l]
                tile_ready(stage, 0)
                bank = 4 + tile0[stage] % 2
                nc.scalar.copy(raw[:, 0, 0:T], ps[:, bank, 0:T])
                nc.scalar.copy(kall[:, T:2 * T], ps[:, bank, T:2 * T]).then_inc(proj_free, 1)
                for j in range(QT):
                    empty(stage, 1 + j, raw[:, 1 + j, 0:n_q], slice(0, n_q))
                empty(stage, 1 + QT, v_tok, slice(0, 2 * T))
                for j in range(QT):
                    empty(stage, 2 + QT + j, u_tok[:, 0:n_blk, j * P:(j + 1) * P], slice(0, n_blk * P))
                for which in ([0, 1] if l == 0 else [0]):
                    fourier(fcall, l, which)
                    attention(acall, l, which)
                    fcall += 1
                    acall += 1
                for j in range(KD):
                    empty(f"out1{l}", j, mix[:, j, 0:n_q], slice(0, n_q))
                for which in ([0, 1] if l == 0 else [0]):
                    act.wait_ge(proj_free, tile0[f"out1{l}"] + KD)
                    norm(("post_mix", l, which), mix[:, :, token_cols(l, which)])
                    call = 2 * l + which
                    g0, g1 = fill(f"M{l}{which}")
                    ada(g0)
                    norm(("pre_ffn", l, which), x[:, :, :] if which == 0 else xc, call, onto=("post_mix", l, which),
                         also=lambda: ada(g1))
                    round_h(split_id[("pre_ffn", l, which)], (gain_of(l, 2, which), shift_of(l, 3, which)))
                    ffn(call)
                    act.wait_ge(dn_done, (call + 1) * FT)
                    acc = ps[:, 0:4, :].rearrange("p a (b t) -> p (a b) t", t=T)
                    norm(("post_ffn", l, which), acc, also=lambda: nc.scalar.copy(
                        mix[:, :, token_cols(l, which)], acc).then_inc(ffn_out, 1))

            for l in range(LAYERS):
                norm(("ffn1", l, 0), x[:, :, :], 3 + 2 * l, ready=3 * l - 1 if l else None,
                     onto=None if l else ("post_ffn", 1, 0))
                round_h(split_id[("ffn1", l, 0)])
                ffn(3 + 2 * l)
                c0 = chunk0[f"proj2{l}"]

                def round_t(t, i=None):
                    n, c = l * NT2 + t, c0 + t // 2
                    if t % 2 == 0:
                        wait(act, a_loaded[c % 2], 16 * (c // 2 + 1), i, 16)
                    wait(act, t_done, n - 1, i, 4)
                    nc.scalar.copy(t_hi[:, t % 2], ring_a[:, c % 2, t % 2]).then_inc(t_hi_ready, 1)

                norm(("mix", l, 0), x[:, :, :], ready=3 * l, first=lambda: round_t(0))
                round_h(split_id[("mix", l, 0)])
                round_t(1)
                if l == 0:
                    act.wait_ge(z_zero, 1)
                else:
                    act.wait_ge(br_free, KD * l)

                def empty_t(t, i=None):
                    wait(act, t_done, l * NT2 + t + 1, i, 4)
                    to = z[:, t, 1:T + 1] if i is None else z[:, bass.ds(i * 4 + t, 1), 1:T + 1]
                    src = ps[:, 4 + t % 2, 0:T]
                    nc.scalar.activation(to, src if i is None else src.rearrange("p (a b) -> p a b", a=1), ACT.Copy)\
                        .then_inc(t_free, 1)
                    round_t(t + 2, i)

                def empty_values(t):
                    act.wait_ge(t_done, l * NT2 + t + 2)
                    both = ps[:, 5 if t == MV else 7, :].rearrange("p (b s n) -> p s b n", b=2, s=2)
                    for u in range(2):
                        j = t + u - MV
                        nc.scalar.copy(mv[:, :, j * P:(j + 1) * P], both[:, (t + u) % 2]).then_inc(t_free, 1)
                    round_t(t + 2)
                    round_t(t + 3)

                def empty_gate(t):
                    g = t - GATES
                    act.wait_ge(t_done, l * NT2 + t + 1)
                    nc.scalar.activation((gate_a if g < KD else gate_b)[:, g % KD, :], ps[:, gate_bank(t), 0:T], ACT.Sigmoid)\
                        .then_inc(t_free, 1)
                    if t + 2 < NT2:
                        round_t(t + 2)

                for t in range(3):
                    empty_t(t)
                with act.Fori(0, 4) as i:
                    for u in range(4):
                        empty_t(3 + u, i)
                act.wait_ge(rw_v, RV.at("mix", l))
                nc.scalar.activation(tmp[0:64, 0, :], z[0:64, XWA, 1:T + 1], ACT.Tanh).then_inc(rw_a, 1)
                nc.scalar.activation(tmp[:, 1, :], z[:, XG, 1:T + 1], ACT.Sigmoid)
                nc.scalar.activation(tmp[0:32, 2, :], z[0:32, MISC, 1:T + 1], ACT.Sigmoid).then_inc(rw_a, 1)
                empty_t(19)
                act.wait_ge(rw_p, RP.at("lw", l))
                for j in range(QT):
                    ins = nc.scalar.activation(lw[:, j, :], ps[:, j // 2, j % 2 * T:j % 2 * T + T], ACT.Sigmoid,
                                               bias=vcol(f"w0{l}", j))
                ins.then_inc(rw_a, 1)
                act.wait_ge(rw_p, RP.at("la", l))
                for j in range(QT):
                    ins = nc.scalar.activation(aa[:, j, :], ps[:, 2 + j // 2, j % 2 * T:j % 2 * T + T], ACT.Sigmoid,
                                               bias=vcol(f"a0{l}", j))
                ins.then_inc(rw_a, 1)
                empty_t(20)
                act.wait_ge(rw_p, RP.at("lg", l))
                nc.scalar.copy(gg, ps[:, 6:8, :].rearrange("p a (b t) -> p (a b) t", t=T)).then_inc(rw_a, 1)
                for t in range(21, 24):
                    empty_t(t)
                if l:
                    act.wait_ge(vres_p, 1)
                    for j in range(QT):
                        ins = nc.scalar.activation(vg[:, j, :], ps[:, j // 2, j % 2 * T:j % 2 * T + T], ACT.Sigmoid,
                                                   bias=vcol("vbias1", j))
                    ins.then_inc(vres_a, 1)
                for t in range(24, MV):
                    empty_t(t)
                act.wait_ge(rw_p, RP.at("ss", l))
                nc.scalar.activation(tmp[0:8, 3, :], ps[0:8, 2, 0:T], ACT.Sqrt).then_inc(rw_a, 1)
                act.wait_ge(rw_v, RV.at("l0", l))
                nc.scalar.activation(e0, e0, ACT.Exp).then_inc(rw_a, 1)
                nc.scalar.activation(e1, lcum, ACT.Exp).then_inc(rw_a, 1)
                nc.scalar.activation(e2, lcum, ACT.Exp, scale=-1.0).then_inc(rw_a, 1)

                def to_tokens(dst, banks):
                    src = ps[:, banks:banks + 2, :].rearrange("p b (u c) -> p (b u) c", c=P)
                    d = units(dst).rearrange("p (u o) c -> p u o c", o=2)
                    for odd in range(2):
                        for h in range(2):
                            ins = nc.scalar.copy(d[h * 64:h * 64 + 64, :, odd, :],
                                                 src[odd * 64:odd * 64 + 64, :, h * 64:h * 64 + 64])
                    return ins

                empty_values(MV)
                act.wait_ge(rw_p, RP.at("vt", l))
                act.wait_ge(rw_v, RV.at("kh", l))
                to_tokens(v_t, 2).then_inc(rw_a, 1)
                act.wait_ge(rw_p, RP.at("khct", l))
                to_tokens(khc_t, 0).then_inc(rw_a, 1)
                act.wait_ge(rw_p, RP.at("bhct", l))
                to_tokens(bhc_t, 4).then_inc(rw_a, 1)
                act.wait_ge(ml_p, MP.at("if", l))
                nc.scalar.activation(row_m, ps[0:4, 6, T:2 * T], ACT.Abs, bias=vcol(f"fb{l}", 0)[0:4]).then_inc(ml_a, 1)
                act.wait_ge(ml_a, MA.at("ab", l))
                nc.scalar.activation(row_m, row_m, ACT.Exp, scale=-1.0).then_inc(ml_a, 1)
                act.wait_ge(ml_a, MA.at("ex", l))
                nc.scalar.activation(row_m, row_m, ACT.Ln, bias=const("one")[0:4]).then_inc(ml_a, 1)
                empty_values(MV + 2)
                act.wait_ge(ml_v, MVS.at("c3", l))
                nc.scalar.activation(nsq[:, :, :], nsq[:, :, :], ACT.Silu).then_inc(ml_a, 1)
                for h in range(4):
                    r = l * 4 + h
                    act.wait_ge(mh_am, r + 1)
                    if r >= 2:
                        act.wait_ge(mh_pm, r - 1)
                    nc.scalar.activation(ee[:, h % 2, :], am[:, h % 2, :], ACT.Exp).then_inc(mh_ee, 1)
                    act.wait_ge(mh_em, r + 1)
                    if r >= 2:
                        act.wait_ge(mh_dn, r - 1)
                    nc.scalar.activation(ems[:, h % 2, :], ps[:, 4 + h % 2, 0:T], ACT.Exp, scale=-1.0)\
                        .then_inc(mh_ems, 1)
                empty_gate(gates_at("mean", 0)[0])
                act.wait_ge(ml_v, MVS.at("hc", l))
                nc.scalar.activation(hN, hc, ACT.Square).then_inc(ml_a, 1)
                empty_gate(gates_at("mean", 1)[0])
                act.wait_ge(ml_p, MP.at("var", l))
                nc.scalar.activation(yb, ps[:, 2:4, :].rearrange("p a (b t) -> p (a b) t", t=T), ACT.Sqrt,
                                     bias=const("eps_ml"), scale=1.0 / P).then_inc(ml_a, 1)
                nc.scalar.activation(z[:, MO:MO + QT, 1:T + 1], z[:, MO:MO + QT, 1:T + 1], ACT.Sigmoid)\
                    .then_inc(ml_a, 1)
                for i in range(len(LEVELS)):
                    step = l * len(LEVELS) + i
                    for half in range(2):
                        act.wait_ge(lev_p, LP.at(f"w{half}", step))
                        nc.scalar.copy(units(ws)[:, half * 8:half * 8 + 8, :],
                                       ps[:, half, :].rearrange("p (u t) -> p u t", t=CHUNK)).then_inc(lev_a, 1)
                    for t in gates_at("level", i):
                        empty_gate(t)
                for c in range(NC_):
                    step = l * NC_ + c
                    act.wait_ge(ch_p, CP.at("r", step))
                    nc.scalar.copy(rr[:, :, c * CHUNK:(c + 1) * CHUNK],
                                   ps[:, 0, 0:QT * HD].rearrange("p (j v) -> p j v", v=HD)).then_inc(ch_a, 1)
                    for t in gates_at("chunk", c):
                        empty_gate(t)
                empty_gate(gates_at("y", 0)[0])
                act.wait_ge(rw_v, RV.at("s2", l))
                nc.scalar.activation(small_y[:, 4, :], small_y[:, 3, :], ACT.Sqrt, bias=const("eps_gn"),
                                     scale=1.0 / HD).then_inc(rw_a, 1)
                act.wait_ge(rw_p, RP.at("yT", l))
                src = ps[0:64, 0:4, :].rearrange("p b (u c) -> p (b u) c", c=P)
                for h in range(2):
                    ins = nc.scalar.copy(units(tmp)[h * 64:h * 64 + 64, :, :], src[:, :, h * 64:h * 64 + 64])
                ins.then_inc(rw_a, 1)
                empty_gate(gates_at("y", 1)[0])

                act.wait_ge(br_free, (l + 1) * KD)
                norm(("ffn2", l, 0), x[:, :, :], 4 + 2 * l, ready=3 * l + 1)
                round_h(split_id[("ffn2", l, 0)])
                ffn(4 + 2 * l)
            norm(("final", 0, 0), x[:, :, :], ready=3 * LAYERS - 1)

        @block.vector
        def _(dve):
            dve.wait_ge(vec_loaded, 16)
            for l in range(LAYERS):
                ka0, ka1 = V[f"k_a{l}"]
                ins = nc.vector.tensor_scalar(omka[:, l * QT:(l + 1) * QT], vec[:, ka0:ka1], -1.0, 1.0,
                                              ALU.mult, ALU.add)
            ins.then_inc(kab, 1)
            b0 = V["b_ada"][0]

            def ada(g, i=None):
                u, at = g % 2, g * 2
                dve.wait_ge(ada_turned, g + 1 if i is None else i * 2 + (g + 1))
                to = slice(at, at + 2) if i is None else bass.ds(i * 4 + at, 2)
                bias = slice(b0 + at, b0 + at + 2) if i is None else bass.ds(i * 4 + (b0 + at), 2)
                nc.vector.tensor_tensor(
                    mod[:, to, :], ps[:, 4 + u, T:T + 4].rearrange("p (a b) -> p a b", b=2),
                    vec[:, bias][:, :, None].to_broadcast([P, 2, 2]), ALU.add).then_inc(ada_free, 1)

            def gains(done, chunks, which):
                dve.wait_ge(ada_free, chunks)
                parts = [(1, "pre_mix", 1.0), (2, "post_mix", 0.0), (4, "pre_ffn", 1.0), (5, "post_ffn", 0.0)]
                for l, i in which:
                    part, name, plus = parts[i]
                    v0, v1 = V[f"{name}{l}"]
                    ins = nc.vector.scalar_tensor_tensor(
                        gain[:, l, i], mod[:, l * NMOD + part * KD:l * NMOD + (part + 1) * KD, :], plus,
                        vec[:, v0:v1][:, :, None].to_broadcast([P, KD, 2]), ALU.add, ALU.mult)
                ins.then_inc(gain_ready, 1)
                dve.wait_ge(gain_ready, done)

            def norm(key, src, gains, dst, shifted=False, onto=None, also=None):
                n = n_id[key]
                if n_two.get(key):
                    dve.wait_ge(norm_scaled, n_two[key] * KD)
                dve.wait_ge(norm_rt, n + 1)
                nc.vector.reciprocal(rstd[:, :], nrt[:, :]).then_inc(norm_rstd, 1)
                if also is not None:
                    also()
                dve.wait_ge(norm_rstd, n + 1)

                def scale(k):
                    return nc.vector.scalar_tensor_tensor(dst[:, k, :], src[:, k, :], gains(k), rstd[:, :],
                                                          ALU.mult, ALU.mult)

                if onto is not None:
                    m, step = onto_id[key], KD // PIECES
                    for i in range(PIECES + 1):
                        if i < PIECES:
                            for k in range(i * step, (i + 1) * step):
                                ins = scale(k)
                            ins.then_inc(onto_scaled, 1)
                        if i:
                            ks = slice((i - 1) * step, i * step)
                            dve.wait_ge(onto_scaled, PIECES * m + i)
                            nc.vector.tensor_tensor(onto[:, ks, :], onto[:, ks, :], dst[:, ks, :], ALU.add)\
                                .then_inc(onto_part if i < PIECES else norm_out, 1)
                    return
                for k in range(KD):
                    ins = scale(k)
                    if shifted:
                        ins.then_inc(norm_scaled, 1)
                if not shifted:
                    ins.then_inc(norm_out, 1)

            def rest_a(call, f, i=None):
                c, t = chunk0[f"ffn{call}"] + f, call * FT + f
                for part in range(2):
                    n = 2 * t + part + 1
                    dve.wait_ge(hi_a, n if i is None else i * 4 + n)
                    ins = nc.vector.tensor_tensor(w_lo[:, f % 2, part], ring_a[:, c % 2, part],
                                                  w_hi[:, f % 2, part].bitcast(F32), ALU.subtract)
                ins.then_inc(a_used, 1)

            def rest_d(call, f, i=None):
                d = call * FT + f
                wait(dve, hi_d, d + 1, i)
                nc.vector.tensor_tensor(d_lo[:, f % 2], ring_d[:, d % 2], d_hi[:, f % 2].bitcast(F32), ALU.subtract)\
                    .then_inc(d_used, 1)

            def norm_split(key, src, call=None, gains=None):
                n, sid = n_id[key], split_id[key]
                if call is not None:
                    rest_a(call, 0)
                dve.wait_ge(norm_rt, n + 1)
                nc.vector.reciprocal(rstd[:, :], nrt[:, :]).then_inc(norm_rstd, 1)
                dve.wait_ge(norm_rstd, n + 1)
                for k in range(KD):
                    if gains is None:
                        ins = nc.vector.tensor_tensor(hn[:, k, :], src[:, k, :], rstd[:, :], ALU.mult)
                    else:
                        ins = nc.vector.scalar_tensor_tensor(nsq[:, k, :], src[:, k, :], gains(k), rstd[:, :],
                                                             ALU.mult, ALU.mult)
                    ins.then_inc(v_ready, 1)

            def ffn(call):
                rest_a(call, 1)
                rest_d(call, 0)

                def tile(f, i=None):
                    t = call * FT + f
                    wait(dve, sg_ready, t + 1, i)
                    nc.vector.tensor_tensor(hid[:, f % 2, :], sg[:, f % 2, :], ps[:, 4 + f % 2, T:2 * T], ALU.mult)\
                        .then_inc(hid_mul, 1)
                    wait(dve, hid_mul, t + 1, i)
                    wait(dve, dn_done, t - 1, i)
                    nc.vector.tensor_copy(hid_hi[:, f % 2, :], hid[:, f % 2, :]).then_inc(hid_rounded, 1)
                    wait(dve, hid_rounded, t + 1, i)
                    nc.vector.tensor_tensor(hid_lo[:, f % 2, :], hid[:, f % 2, :], hid_hi[:, f % 2, :].bitcast(F32),
                                            ALU.subtract).then_inc(hid_ready, 1)
                    if f + 2 < FT:
                        rest_a(call, f + 2, i)
                    if f + 1 < FT:
                        rest_d(call, f + 1, i)

                tile(0)
                tile(1)
                with dve.Fori(0, FT // 2 - 2) as i:
                    tile(2, i)
                    tile(3, i)
                tile(FT - 2)
                tile(FT - 1)

            def attention(call, l, which):
                n_keys = 2 * T if which == 0 else T

                def scores(u):
                    g, h, blk, r = call * 16 + u, (u % 2) * 4 + (u // 2) % 4, u // 8, u % 2
                    dve.wait_ge(at_sc, g + 1)
                    if g >= 2:
                        dve.wait_ge(at_exp, g - 1)
                    if which == 0:
                        ins = nc.vector.scalar_tensor_tensor(
                            s_sb[:, r, :], ps[:, r, :], HD ** -0.5, const1("win")[:, blk * 2 * T:(blk + 1) * 2 * T],
                            ALU.mult, ALU.add)
                    else:
                        ins = nc.vector.tensor_scalar(s_sb[:, r, 0:T], ps[:, r, 0:T], HD ** -0.5, None, ALU.mult)
                    ins.then_inc(at_s, 1)
                    dve.wait_ge(at_s, g + 1)
                    nc.vector.reduce_max(tiny[:, r, 0:1], s_sb[:, r, 0:n_keys], AX_X).then_inc(at_mx, 1)
                    dve.wait_ge(at_mx, g + 1)
                    nc.vector.tensor_scalar(tiny[:, r, 1:2], tiny[:, r, 0:1], vcol("sink", l * 8 + h), -1.0,
                                            ALU.max, ALU.mult).then_inc(at_nm, 1)

                def normalise(u):
                    g, r = call * 16 + u, u % 2
                    dve.wait_ge(at_exp, g + 1)
                    nc.vector.tensor_tensor(tiny[:, r, 4:5], tiny[:, r, 2:3], tiny[:, r, 3:4], ALU.add)\
                        .then_inc(at_den, 1)
                    dve.wait_ge(at_den, g + 1)
                    nc.vector.reciprocal(tiny[:, r, 5:6], tiny[:, r, 4:5]).then_inc(at_rd, 1)
                    dve.wait_ge(at_rd, g + 1)
                    if g >= 2:
                        dve.wait_ge(at_tr, g - 1)
                    nc.vector.tensor_scalar(pn[:, r, 0:n_keys], probs[:, r, 0:n_keys], tiny[:, r, 5:6], None,
                                            ALU.mult).then_inc(at_pn, 1)

                for u in range(18):
                    if u < 16:
                        scores(u)
                    if 1 <= u <= 16:
                        normalise(u - 1)
                    g = ada_step(l, which, u)
                    if g is not None and g > ada_from[f"L{l}"]:
                        ada(g - 1)

            acall = 0
            for l in range(LAYERS):
                def modulation():
                    for g in range(ADA_FIRST - 3, ADA_FIRST):
                        ada(g)
                    gains(1, ADA_FIRST, [(0, 0)])

                if l == 0:
                    with dve.Fori(0, ADA_FIRST // 2 - 2) as i:
                        ada(0, i)
                        ada(1, i)
                    ada(ADA_FIRST - 4)
                    dve.wait_ge(in_loaded, 32)
                norm(("pre_mix", l, 0), x, gain_of(l, 0, 0), h2[:, :, 0:T], shifted=True,
                     also=modulation if l == 0 else None)
                norm(("pre_mix", l, 1), xc, gain_of(l, 0, 1), h2[:, :, T:2 * T], shifted=True)
                for g in fill(f"B{l}"):
                    ada(g)
                dve.wait_ge(const_loaded, 32)
                cos, sin = (const1(n)[:, None, :].to_broadcast([P, 5, T]) for n in ("cos", "sin"))
                dve.wait_ge(rope_rot, l + 1)
                rot = ps[:, 0:3, :].rearrange("p a (b t) -> p (a b) t", t=T)[:, 0:5, :]
                nc.vector.tensor_tensor(rtmp, rot, sin, ALU.mult).then_inc(rope_sin, 1)
                nc.vector.tensor_tensor(raw[:, :, 0:T], raw[:, :, 0:T], cos, ALU.mult).then_inc(rope_cos, 1)
                dve.wait_ge(rope_sin, l + 1)
                dve.wait_ge(rope_cos, l + 1)
                nc.vector.tensor_tensor(kall[:, 0:T], raw[:, 0, 0:T], rtmp[:, 0, :], ALU.add)
                nc.vector.tensor_tensor(qr, raw[:, 1:5, 0:T], rtmp[:, 1:5, :], ALU.add).then_inc(rope_out, 1)
                for which in ([0, 1] if l == 0 else [0]):
                    attention(acall, l, which)
                    acall += 1
                ada(ada_from[f"M{l}0"] - 1)
                gains(2 * l + 2, ada_from[f"M{l}0"], [(0, 1), (0, 2), (0, 3)] if l == 0 else [(1, 1), (1, 2)])
                for which in ([0, 1] if l == 0 else [0]):
                    res = x[:, :, :] if which == 0 else xc
                    mixed = mix[:, :, token_cols(l, which)]
                    norm(("post_mix", l, which), mixed, gain_of(l, 1, which), hn, onto=res)
                    dve.wait_ge(norm_out, n_id[("post_mix", l, which)] + 1)
                    g0, g1 = fill(f"M{l}{which}")
                    ada(g0)
                    dve.wait_ge(a_used, chunk0[f"ffn{2 * l + which}"])
                    norm_split(("pre_ffn", l, which), res, 2 * l + which)
                    ada(g1)
                    if (l, which) == (0, 1):
                        gains(3, ada_from["B1"], [(1, 0)])
                    if l == 1:
                        gains(5, LAYERS * NMOD // 2, [(1, 3)])
                    ffn(2 * l + which)
                    dve.wait_ge(ffn_out, 2 * l + which + 1)
                    norm(("post_ffn", l, which), mixed, gain_of(l, 3, which), hn, onto=res)

            def per_channel(name, l):
                return lambda k: vcol(f"{name}{l}", k)

            def v(name, l):
                dve.wait_ge(rw_v, RV.at(name, l))

            def half_onto_x():
                for b in range(PIECES):
                    xx = x[:, 2 * b:2 * b + 2, :]
                    nc.vector.scalar_tensor_tensor(xx, ps[:, b, :].rearrange("p (a t) -> p a t", t=T), 0.5, xx,
                                                   ALU.mult, ALU.add).then_inc(resid, 1)

            def wide(bank):
                return ps[:, bank:bank + 2, :].rearrange("p a (b t) -> p (a b) t", t=T)

            dve.wait_ge(norm_out, n_id[("post_ffn", 1, 0)] + 1)
            for l in range(LAYERS):
                norm_split(("ffn1", l, 0), x, 3 + 2 * l, per_channel("ffn1", l))
                ffn(3 + 2 * l)
                dve.wait_ge(dn_done, (4 + 2 * l) * FT)
                half_onto_x()
                dve.wait_ge(resid, PIECES * (3 * l + 1))
                norm_split(("mix", l, 0), x, None, per_channel("mix", l))

                zr, zk, zv = (z[:, a:a + QT, 1:T + 1] for a in (R0, K0, V0))
                p0 = l * NT2
                dve.wait_ge(t_free, p0 + MIXED)
                nc.vector.tensor_tensor(diff, z[:, 0:MIXED, 0:T], z[:, 0:MIXED, 1:T + 1], ALU.subtract)\
                    .then_inc(rw_v, 1)
                v("diff", l)
                for k in range(MIXED):
                    rows = slice(0, P) if k != MISC else slice(0, 32)
                    zz = z[rows, k, 1:T + 1]
                    ins = nc.vector.scalar_tensor_tensor(zz, diff[rows, k, :], vcol(f"mu{l}", k)[rows], zz,
                                                         ALU.mult, ALU.add)
                ins.then_inc(rw_v, 1)
                v("mix", l)
                for j in range(QT):
                    ins = nc.vector.tensor_scalar(kk[:, j, :], zk[:, j, :], vcol(f"k_k{l}", j), None, ALU.mult)
                ins.then_inc(rw_v, 1)
                v("kk", l)
                nc.vector.tensor_tensor(e0, kk, kk, ALU.mult).then_inc(rw_v, 1)
                dve.wait_ge(rw_a, RA.at("sw", l))
                nc.vector.tensor_scalar(lw, lw, -float(np.exp(-0.5)), None, ALU.mult).then_inc(rw_v, 1)
                v("lw", l)
                for j in range(QT):
                    ins = nc.vector.tensor_tensor_scan(lcum[:, j, :], const("restart"), lw[:, j, :], 0.0,
                                                       ALU.mult, ALU.add)
                ins.then_inc(rw_v, 1)
                if l == 0:
                    nc.vector.tensor_copy(vfirst[:, :, :], zv)
                else:
                    dve.wait_ge(vres_a, 1)
                    nc.vector.tensor_tensor(e1, vfirst[:, :, :], zv, ALU.subtract).then_inc(vres_v, 1)
                    dve.wait_ge(vres_v, VV.at("d", 0))
                    nc.vector.tensor_tensor(e1, e1, vg, ALU.mult).then_inc(vres_v, 1)
                    dve.wait_ge(vres_v, VV.at("m", 0))
                    nc.vector.tensor_tensor(zv, zv, e1, ALU.add).then_inc(vres_v, 1)
                dve.wait_ge(rw_a, RA.at("aa", l))
                dve.wait_ge(kab, 1)
                if l:
                    dve.wait_ge(vres_v, VV.at("v", 0))
                for j in range(QT):
                    ins = nc.vector.tensor_scalar(e1[:, j, :], aa[:, j, :], vcol(f"k_a{l}", j),
                                                  omka[:, l * QT + j:l * QT + j + 1], ALU.mult, ALU.add)
                ins.then_inc(rw_v, 1)
                v("ka", l)
                nc.vector.tensor_tensor(zk, zk, e1, ALU.mult).then_inc(rw_v, 1)
                v("kp", l)
                for j in range(QT):
                    ins = nc.vector.scalar_tensor_tensor(bon[:, j, :], zr[:, j, :], vcol(f"r_k{l}", j), zk[:, j, :],
                                                         ALU.mult, ALU.mult)
                ins.then_inc(rw_v, 1)
                dve.wait_ge(rw_a, RA.at("rsq", l))
                nc.vector.tensor_scalar(tmp[0:8, 3, :], tmp[0:8, 3, :], 1e-12, None, ALU.max).then_inc(rw_v, 1)
                v("rnmax", l)
                nc.vector.reciprocal(inv_norm, tmp[0:8, 3, :]).then_inc(rw_v, 1)
                v("scan", l)
                nc.vector.tensor_tensor(e0, lcum, lw, ALU.subtract).then_inc(rw_v, 1)
                dve.wait_ge(rw_p, RP.at("rnb", l))
                nc.vector.tensor_tensor(kk, kk, wide(0), ALU.mult).then_inc(rw_v, 1)
                v("kkn", l)
                nc.vector.tensor_tensor(bb, kk, aa, ALU.mult).then_inc(rw_v, 1)
                dve.wait_ge(rw_p, RP.at("bon", l))
                nc.vector.tensor_tensor(bon, wide(2), zv, ALU.mult).then_inc(rw_v, 1)
                v("b", l)
                dve.wait_ge(rw_a, RA.at("e2", l))
                nc.vector.tensor_tensor(kt, kk, e0, ALU.mult).then_inc(rw_v, 1)
                nc.vector.tensor_tensor(bh, bb, e2, ALU.mult).then_inc(rw_v, 1)
                v("kt", l)
                nc.vector.tensor_tensor(kh, zk, e2, ALU.mult).then_inc(rw_v, 1)
                nc.vector.tensor_tensor(zr, zr, e1, ALU.mult).then_inc(rw_v, 1)
                v("kh", l)
                pc = units(e1)[:, :, CHUNK - 1:CHUNK].to_broadcast([P, UNITS, CHUNK])
                nc.vector.tensor_tensor(units(khc), units(kh), pc, ALU.mult).then_inc(rw_v, 1)
                nc.vector.tensor_tensor(units(bhc), units(bh), pc, ALU.mult).then_inc(rw_v, 1)

                dve.wait_ge(t_free, p0 + MK + QT)
                for tap in range(4):
                    if tap:
                        dve.wait_ge(ml_v, MVS.at(f"c{tap - 1}", l))
                    for k in range(2 * QT):
                        zz = z[:, MQ + k, 1:T + 1 - tap]
                        if tap == 0:
                            ins = nc.vector.tensor_scalar(nsq[:, k, :], zz, vcol(f"tap3{l}", k),
                                                          vcol(f"conv_b{l}", k), ALU.mult, ALU.add)
                        else:
                            ins = nc.vector.scalar_tensor_tensor(nsq[:, k, tap:T], zz, vcol(f"tap{3 - tap}{l}", k),
                                                                 nsq[:, k, tap:T], ALU.mult, ALU.add)
                    ins.then_inc(ml_v, 1)
                def m(name):
                    dve.wait_ge(ml_v, MVS.at(name, l))

                dve.wait_ge(ml_p, MP.at("if", l))
                dve.wait_ge(ml_a, MA.at("ln", l))
                nc.vector.tensor_scalar(row_f, ps[0:4, 6, T:2 * T], vcol(f"fb{l}", 0)[0:4], 0.0, ALU.add, ALU.min)\
                    .then_inc(ml_v, 1)
                m("mn")
                nc.vector.tensor_tensor(row_g, row_f, row_m, ALU.subtract).then_inc(ml_v, 1)
                m("lf")
                ones_row = const("one")[0:4].to_broadcast([4, T])
                nc.vector.tensor_tensor_scan(row_f, ones_row, row_g, 0.0, ALU.mult, ALU.add).then_inc(ml_v, 1)
                m("F")
                nc.vector.scalar_tensor_tensor(row_g, ps[0:4, 6, 0:T], vcol(f"ib{l}", 0)[0:4], row_f,
                                               ALU.add, ALU.subtract).then_inc(ml_v, 1)
                m("g")
                nc.vector.tensor_tensor_scan(row_m, ones_row, row_g, 0.0, ALU.mult, ALU.max).then_inc(ml_v, 1)
                m("M")
                nc.vector.tensor_tensor(row_f, row_f, row_m, ALU.add).then_inc(ml_v, 1)
                m("fm")
                nc.vector.tensor_scalar(row_m, row_m, -1.0, None, ALU.mult).then_inc(ml_v, 1)

                def masked(dst, bank, mask):
                    return nc.vector.tensor_tensor(
                        dst.rearrange("p j (c t) -> p j c t", t=CHUNK),
                        ps[:, bank:bank + 2, :].rearrange("p b (j c t) -> p (b j) c t", c=NC_, t=CHUNK),
                        const(mask)[:, None, None, :].to_broadcast([P, QT, NC_, CHUNK]), ALU.mult)

                def next_level(i):
                    nc.vector.tensor_tensor(
                        units(aoff), units(at_), const(f"lev{LEVELS[i]}")[:, None, :].to_broadcast([P, UNITS, CHUNK]),
                        ALU.mult).then_inc(lev_g, 1)

                eye = const("eye")[:, None, :].to_broadcast([P, UNITS, CHUNK])
                dve.wait_ge(rw_p, RP.at("at", l))
                masked(at_, 4, "strict").then_inc(rw_v, 1)
                dve.wait_ge(rw_p, RP.at("a", l))
                masked(xs, 0, "low1").then_inc(rw_v, 1)
                v("at", l)
                nc.vector.tensor_tensor(units(xt), units(at_),
                                        const("up1")[:, None, :].to_broadcast([P, UNITS, CHUNK]), ALU.mult)\
                    .then_inc(rw_v, 1)
                v("xt1", l)
                nc.vector.tensor_tensor(units(xs), eye, units(xs), ALU.subtract).then_inc(rw_v, 1)
                nc.vector.tensor_tensor(units(xt), eye, units(xt), ALU.subtract).then_inc(rw_v, 1)
                dve.wait_ge(rw_p, RP.at("mrt", l))
                masked(mrt, 2, "incl").then_inc(rw_v, 1)

                dve.wait_ge(rw_p, RP.at("mt", l))
                masked(mt, 6, "strict").then_inc(rw_v, 1)
                dve.wait_ge(rw_p, RP.at("art", l))
                masked(art, 4, "incl").then_inc(rw_v, 1)
                for h in range(5):
                    r = l * 4 + h
                    if h < 4:
                        dve.wait_ge(mh_arg, r + 1)
                        if r >= 2:
                            dve.wait_ge(mh_ee, r - 1)
                        nc.vector.tensor_tensor(am[:, h % 2, :], ps[:, h % 2, 0:T + P], const("tri"), ALU.add)\
                            .then_inc(mh_am, 1)
                        dve.wait_ge(mh_ee, r + 1)
                        dve.wait_ge(mh_s, r + 1)
                        if r >= 2:
                            dve.wait_ge(mh_nd, r - 1)
                        nc.vector.scalar_tensor_tensor(pm[:, h % 2, :], ps[:, 2 + h % 2, 0:T + P], float(P) ** -0.5,
                                                       ee[:, h % 2, :], ALU.mult, ALU.mult).then_inc(mh_pm, 1)
                    if h >= 1:
                        r, o = r - 1, (h - 1) % 2
                        dve.wait_ge(mh_ems, r + 1)
                        dve.wait_ge(mh_nd, r + 1)
                        nc.vector.scalar_tensor_tensor(dn[:, o, :], ps[:, 6 + o, T:2 * T], -1.0, ems[:, o, :],
                                                       ALU.mult, ALU.max).then_inc(mh_dn, 1)
                        dve.wait_ge(mh_dn, r + 1)
                        nc.vector.tensor_tensor(dn[:, o, :], ps[:, 6 + o, T:2 * T], dn[:, o, :], ALU.max)\
                            .then_inc(mh_abs, 1)
                        dve.wait_ge(mh_abs, r + 1)
                        nc.vector.reciprocal(dn[:, o, :], dn[:, o, :]).then_inc(mh_rc, 1)
                        dve.wait_ge(mh_rc, r + 1)
                        nc.vector.tensor_tensor(hN[:, h - 1, :], ps[:, 6 + o, 0:T], dn[:, o, :], ALU.mult)\
                            .then_inc(mh_h, 1)
                dve.wait_ge(ml_p, MP.at("mu", l))
                nc.vector.scalar_tensor_tensor(hc, wide(0), -1.0 / P, hN, ALU.mult, ALU.add).then_inc(ml_v, 1)
                next_level(0)

                def standardise(j):
                    nc.vector.reciprocal(yb[:, j, :], yb[:, j, :]).then_inc(ml_v, 1)
                    m(f"rec{j}")
                    nc.vector.tensor_tensor(hc[:, j, :], hc[:, j, :], yb[:, j, :], ALU.mult).then_inc(ml_v, 1)
                    m(f"hs{j}")
                    nc.vector.scalar_tensor_tensor(yb[:, j, :], hc[:, j, :], vcol(f"ml_w{l}", j),
                                                   z[:, MO + j, 1:T + 1], ALU.mult, ALU.mult).then_inc(ml_v, 1)

                for i in range(len(LEVELS)):
                    step = l * len(LEVELS) + i
                    if i + 1 < len(LEVELS):
                        dve.wait_ge(lev_p, LP.at("w1", step))
                        next_level(i + 1)
                    for half in range(2):
                        us = slice(half * 8, half * 8 + 8)
                        dve.wait_ge(lev_p, LP.at(f"x{half}", step))
                        for buf, bank in ((xs, 2), (xt, 4))[i == len(LEVELS) - 1:]:
                            ins = nc.vector.tensor_tensor(
                                units(buf)[:, us, :], units(buf)[:, us, :],
                                ps[:, bank + half, :].rearrange("p (u t) -> p u t", t=CHUNK), ALU.subtract)
                        ins.then_inc(lev_v, 1)
                    if i < QT:
                        if i == 0:
                            dve.wait_ge(ml_a, MA.at("so", l))
                        standardise(i)
                pcs = units(e1)[:, :, CHUNK - 1:CHUNK]
                for c in range(NC_):
                    step = l * NC_ + c
                    if c == 0:
                        nc.vector.memset(state[:, 0], 0.0).then_inc(ch_v, 1)
                    elif c < NC_ - 1:
                        dve.wait_ge(ch_v, CV.at("s", step - 1))
                        nc.vector.tensor_tensor(
                            sdec, state[:, c % 2],
                            e1[:, :, c * CHUNK + CHUNK - 1:c * CHUNK + CHUNK].to_broadcast([P, QT, HD]),
                            ALU.mult).then_inc(ch_v, 1)
                    dve.wait_ge(ch_p, CP.at("u", step))
                    nc.vector.tensor_scalar(nu[:, :, c * CHUNK:(c + 1) * CHUNK],
                                            ps[:, 1, 0:QT * HD].rearrange("p (j v) -> p j v", v=HD), -1.0, None,
                                            ALU.mult).then_inc(ch_v, 1 if c < NC_ - 1 else CV.count)
                    if c == NC_ - 1:
                        continue
                    dve.wait_ge(ch_p, CP.at("s", step))
                    sp_ = ps[:, 4, 0:QT * HD].rearrange("p (j v) -> p j v", v=HD)
                    if c:
                        dve.wait_ge(ch_v, CV.at("nu", step))
                        nc.vector.tensor_tensor(state[:, (c + 1) % 2], sp_, sdec, ALU.add).then_inc(ch_v, 1)
                    else:
                        nc.vector.tensor_copy(state[:, 1], sp_).then_inc(ch_v, 1)
                yps = ps[:, 2:4, :].rearrange("p b (u t) -> p (b u) t", t=HD)
                stat = lambda i: small_y[:, i, :]
                wide_stat = lambda i: small_y[:, i, :][:, :, None].to_broadcast([P, UNITS, HD])
                dve.wait_ge(ch_p, CP.at("y", l * NC_ + NC_ - 1))
                nc.vector.reduce_sum(stat(0), yps, AX_X).then_inc(rw_v, 1)
                v("s1", l)
                nc.vector.tensor_scalar(stat(1), stat(0), -1.0 / HD, None, ALU.mult).then_inc(rw_v, 1)
                v("ym", l)
                nc.vector.tensor_tensor(units(yy), yps, wide_stat(1), ALU.add).then_inc(rw_v, 1)
                v("yc", l)
                nc.vector.tensor_tensor(units(yq), units(yy), units(yy), ALU.mult).then_inc(rw_v, 1)
                v("yq", l)
                nc.vector.reduce_sum(stat(3), units(yq), AX_X).then_inc(rw_v, 1)
                dve.wait_ge(rw_a, RA.at("ysd", l))
                nc.vector.reciprocal(stat(5), stat(4)).then_inc(rw_v, 1)
                v("yr", l)
                nc.vector.tensor_tensor(units(yy), units(yy), wide_stat(5), ALU.mult).then_inc(rw_v, 1)
                dve.wait_ge(rw_a, RA.at("yT", l))
                for j in range(QT):
                    ins = nc.vector.tensor_scalar(tmp[:, j, :], tmp[:, j, :], vcol(f"gn_w{l}", j),
                                                  vcol(f"gn_b{l}", j), ALU.mult, ALU.add)
                ins.then_inc(rw_v, 1)
                v("gn", l)
                nc.vector.tensor_tensor(tmp, tmp, bon, ALU.add).then_inc(rw_v, 1)
                v("gb", l)
                nc.vector.tensor_tensor(ya, tmp, gg, ALU.mult).then_inc(rw_v, 1)

                dve.wait_ge(t_free, (l + 1) * NT2)
                for n in range(KD):
                    r = l * KD + n
                    if n % 2:
                        dve.wait_ge(a_used, chunk0[f"br{l}"] + n // 2 + 1)
                    else:
                        dve.wait_ge(br_ready, r // 2 + 1)
                    nc.vector.tensor_tensor(umix[:, n, :], ps[:, 4 + n % 2, 0:T], gate_a[:, n, :], ALU.mult)\
                        .then_inc(br_part, 1)
                    nc.vector.tensor_tensor(xs[:, n % 2, :], ps[:, 4 + n % 2, T:2 * T], gate_b[:, n, :], ALU.mult)\
                        .then_inc(br_part, 1)
                    dve.wait_ge(br_part, 2 * r + 2)
                    nc.vector.tensor_tensor(umix[:, n, :], umix[:, n, :], xs[:, n % 2, :], ALU.add).then_inc(br_free, 1)
                for n in range(KD // 2):
                    dve.wait_ge(a_used, chunk0[f"out2{l}"] + n + 1)
                    xx = x[:, 2 * n:2 * n + 2, :]
                    nc.vector.tensor_tensor(xx, xx, ps[:, n, :].rearrange("p (a b) -> p a b", b=T), ALU.add)\
                        .then_inc(resid, 1)
                dve.wait_ge(resid, PIECES * (3 * l + 2))
                norm_split(("ffn2", l, 0), x, 4 + 2 * l, per_channel("ffn2", l))
                ffn(4 + 2 * l)
                dve.wait_ge(dn_done, (5 + 2 * l) * FT)
                half_onto_x()
                dve.wait_ge(resid, PIECES * (3 * l + 3))
            norm(("final", 0, 0), x, lambda k: vcol("final", k), nsq)

        @block.tensor
        def _(pe):
            ones, ident = const("ones"), const("ident")

            def chunk_here(c, slot, i=None):
                n = 16 * (c // 2 + 1)
                pe.wait_ge(a_loaded[slot], n if i is None else i * 16 + n)

            pe.wait_ge(cs_ready, 1)

            def ada(g, halfway=None):
                u, n = g % 2, early_chunk(g)
                if n is not None:
                    pe.wait_ge(early_loaded[n], 16)
                    tiles, done = early[:, n], ada_early
                else:
                    c = ada_chunk(g)
                    chunk_here(c, c % 2)
                    tiles, done = ring_a[:, c % 2], a_used
                if g >= 2:
                    pe.wait_ge(ada_free, g - 1)
                for k in range(KD):
                    if k == KD // 2 and halfway is not None:
                        ada_turn(halfway)
                    mm = nc.tensor.matmul(ps[0:2, 4 + u, 0:T].rearrange("p (a b) -> p a b", b=P), cs[:, k, :],
                                          tiles[:, :, k, :], start=(k == 0), stop=(k == KD - 1))
                mm.then_inc(done, 1)

            def ada_turn(g):
                u = g % 2
                pe.wait_ge(ada_row, g + 1)
                for h in range(2):
                    mm = nc.tensor.matmul(ps[:, 4 + u, T + 2 * h:T + 2 * h + 2], ada_rows[0:2, u, h * P:(h + 1) * P],
                                          ident[0:2, 0:2], start=True, stop=True)
                mm.then_inc(ada_turned, 1)

            def norm(key):
                n = n_id[key]
                if n:
                    pe.wait_ge(norm_rt, n)
                for k in range(KD):
                    pe.wait_ge(norm_sq, PIECES * n + k * PIECES // KD + 1)
                    mm = nc.tensor.matmul(ps[:, 6, 0:T], ones, nsq[:, k, :], start=(k == 0), stop=(k == KD - 1))
                mm.then_inc(norm_sum, 1)

            def split_product(out, parts, start, stop):
                hi, lo, to_hi, to_lo = parts
                nc.tensor.matmul(out, hi, to_hi, start=start, stop=False, skip_group_check=True)
                nc.tensor.matmul(out, hi, to_lo, start=False, stop=False, skip_group_check=True)
                return nc.tensor.matmul(out, lo, to_hi, start=False, stop=stop, skip_group_check=True)

            def split_here(key, k):
                if k < KD - 1:
                    pe.wait_ge(hl_ready, split_id[key] * (KD - 1) + k + 1)
                else:
                    pe.wait_ge(norm_out, n_id[key] + 1)

            def ffn(call, key):
                c0, d0 = chunk0[f"ffn{call}"], call * FT

                def gate_up(f, i=None):
                    c, t = c0 + f, d0 + f
                    wait(pe, a_used, c + 1, i)
                    if f >= 2 or call:
                        wait(pe, hid_mul, t - 1, i)
                    for k in range(KD):
                        if f == 0:
                            split_here(key, k)
                        for part in range(2):
                            mm = split_product(ps[:, 4 + f % 2, part * T:part * T + T],
                                               (w_hi[:, f % 2, part, k, :], w_lo[:, f % 2, part, k, :],
                                                h_hi[:, k, :], h_lo[:, k, :]),
                                               start=(k == 0 and part == 0), stop=(k == KD - 1))
                    mm.then_inc(gu_done, 1)

                def down(f, i=None):
                    d = d0 + f
                    wait(pe, d_used, d + 1, i)
                    wait(pe, hid_ready, d + 1, i)
                    for n in range(KD):
                        mm = split_product(ps[:, n // 2, n % 2 * T:n % 2 * T + T],
                                           (d_hi[:, f % 2, n, :], d_lo[:, f % 2, n, :],
                                            hid_hi[:, f % 2, :], hid_lo[:, f % 2, :]),
                                           start=(f == 0 and n % 2 == 0), stop=(f == FT - 1))
                    mm.then_inc(dn_done, 1)

                gate_up(0)
                gate_up(1)
                down(0)
                with pe.Fori(0, (FT - 2) // 2) as i:
                    for u in range(2):
                        gate_up(2 + u, i)
                        down(1 + u, i)
                down(FT - 1)

            def tile_done(mm, stage, i):
                mm.then_inc(a_used if i % 2 else proj_ready, 1)

            def project(stage, i, h, cols):
                p, slot = tile0[stage] + i, (chunk0[stage] + i // 2) % 2
                if i % 2 == 0:
                    chunk_here(chunk0[stage] + i // 2, slot)
                if p >= 2:
                    pe.wait_ge(proj_free, p - 1)
                for k in range(KD):
                    mm = nc.tensor.matmul(ps[:, 4 + p % 2, 0:cols.stop - cols.start], ring_a[:, slot, i % 2, k, :],
                                          h[:, k, cols], start=(k == 0), stop=(k == KD - 1))
                tile_done(mm, stage, i)

            def project_tokens(stage, i, h, blocks):
                p, slot = tile0[stage] + i, (chunk0[stage] + i // 2) % 2
                if i % 2 == 0:
                    chunk_here(chunk0[stage] + i // 2, slot)
                if p >= 2:
                    pe.wait_ge(proj_free, p - 1)
                for b in range(blocks):
                    for k in range(KD):
                        mm = nc.tensor.matmul(ps[:, 4 + p % 2, b * P:(b + 1) * P], h[:, k, b * P:(b + 1) * P],
                                              ring_a[:, slot, i % 2, k, :], start=(k == 0), stop=(k == KD - 1))
                tile_done(mm, stage, i)

            def fourier(call, l, which):
                wait_u = tile0[f"proj1{l}"] + 10
                pe.wait_ge(proj_free, wait_u)
                pe.wait_ge(rope_sin, l + 1)
                if call:
                    pe.wait_ge(fo_out, call * QT)
                if which:
                    pe.wait_ge(at_pt, (call) * 16)
                    pe.wait_ge(at_s, (call) * 16)
                for j in range(QT):
                    for b in range(2):
                        mm = nc.tensor.matmul(ps[:, j, :], u_tok[:, 2 * which + b, j * P:(j + 1) * P],
                                              const1("dft")[:, b * 2 * T:(b + 1) * 2 * T], start=(b == 0), stop=(b == 1))
                    mm.then_inc(fo_dft, 1)
                for j in range(QT):
                    pe.wait_ge(fo_fu, call * QT + j + 1)
                    nc.tensor.matmul(ps[:, j, 0:T], const1("chc"), fu[:, j, 0:T], start=True, stop=False)
                    nc.tensor.matmul(ps[:, j, 0:T], const1("chs"), fu[:, j, T:2 * T], start=False, stop=True)\
                        .then_inc(fo_ch, 1)
                for j in range(QT):
                    pe.wait_ge(fo_fm, call * QT + j + 1)
                    nc.tensor.matmul(ps[:, j, T:2 * T], wfour[:, l * QT + j, :], fm[:, j, :], start=True, stop=True)\
                        .then_inc(fo_w, 1)

            def attention(call, l, which):
                n_keys = 2 * T if which == 0 else T
                keys = kall if which == 0 else kall[:, T:2 * T]
                pe.wait_ge(fo_out, (call + 1) * QT)
                pe.wait_ge(rope_out, l + 1)

                def scores(u):
                    g, blk, j, kv = call * 16 + u, u // 8, u // 2 % 4, u % 2
                    half = slice(kv * HD, kv * HD + HD)
                    if g >= 2:
                        pe.wait_ge(at_s, g - 1)
                    q = qr[half, j, blk * P:(blk + 1) * P] if which == 0 else \
                        raw[half, 1 + j, T + blk * P:T + (blk + 1) * P]
                    nc.tensor.matmul(ps[:, u % 2, 0:n_keys], q, keys[half, :], start=True, stop=True).then_inc(at_sc, 1)

                def turn(u):
                    g = call * 16 + u
                    pe.wait_ge(at_pn, g + 1)
                    if g >= 2:
                        pe.wait_ge(at_pt, g - 1)
                    for b in range(n_keys // P):
                        mm = nc.tensor.transpose(ps[:, 2 + u % 2, b * P:(b + 1) * P], pn[:, u % 2, b * P:(b + 1) * P],
                                                 ident)
                    mm.then_inc(at_tr, 1)

                def values(u):
                    g, w, kv = call * 16 + u, u // 2, u % 2
                    half = slice(kv * HD, kv * HD + HD)
                    pe.wait_ge(at_pt, g + 1)
                    if call * 8 + w >= 2:
                        pe.wait_ge(at_o, call * 8 + w - 1)
                    nb = n_keys // P
                    for b in range(nb):
                        mm = nc.tensor.matmul(ps[half, 6 + w % 2, 0:P], v_tok[:, 4 - nb + b, half], pt[:, u % 2, b, :],
                                              start=(b == 0), stop=(b == nb - 1))
                    mm.then_inc(at_pv, 1)

                scores(0)
                for u in range(18):
                    if u + 1 < 16:
                        scores(u + 1)
                    g = ada_step(l, which, u)
                    if g is not None:
                        ada(g)
                        if g > ada_from[f"L{l}"]:
                            ada_turn(g - 1)
                    if 1 <= u <= 16:
                        turn(u - 1)
                    if u >= 2:
                        values(u - 2)

            ada(0)
            pe.wait_ge(c2_loaded, 16)
            for g in range(1, ADA_FIRST):
                ada(g, g - 1)
                if g >= ADA_FIRST - 3 and g < ADA_FIRST - 1:
                    norm(("pre_mix", 0, g - (ADA_FIRST - 3)))
            ada_turn(ADA_FIRST - 1)
            fcall = 0
            for l in range(LAYERS):
                if l:
                    norm(("pre_mix", l, 0))
                    norm(("pre_mix", l, 1))
                    pe.wait_ge(hid_mul, 2 * FT)
                for g in fill(f"B{l}"):
                    ada(g)
                for g in fill(f"B{l}"):
                    ada_turn(g)
                pe.wait_ge(norm_out, n_id[("pre_mix", l, 1)] + 1)
                pe.wait_ge(ada_free, ada_from[f"L{l}"])
                stage, n_q = f"proj1{l}", (2 * T, T)[l]
                for i in range(10):
                    if i == 0:
                        project(stage, i, h2, slice(0, 2 * T))
                    elif i <= QT:
                        project(stage, i, h2, slice(0, n_q))
                    else:
                        project_tokens(stage, i, h2, 4 if i == QT + 1 else n_q // P)
                    if i == 6:
                        pe.wait_ge(proj_free, tile0[stage] + 5)
                        pe.wait_ge(const_loaded, 32)
                        for j in range(5):
                            mm = nc.tensor.matmul(ps[:, j // 2, j % 2 * T:j % 2 * T + T], const1("rot"), raw[:, j, 0:T],
                                                  start=True, stop=True)
                        mm.then_inc(rope_rot, 1)
                for which in ([0, 1] if l == 0 else [0]):
                    fourier(fcall, l, which)
                    attention(fcall, l, which)
                    fcall += 1
                ada_turn(ada_from[f"M{l}0"] - 1)
                pe.wait_ge(ada_free, ada_from[f"M{l}0"])
                pe.wait_ge(at_o, fcall * 8)
                for i in range(KD):
                    project(f"out1{l}", i, mixin, slice(0, n_q))
                for which in ([0, 1] if l == 0 else [0]):
                    norm(("post_mix", l, which))
                    g0, g1 = fill(f"M{l}{which}")
                    if which == 0:
                        pe.wait_ge(proj_free, tile0[f"out1{l}"] + KD)
                    else:
                        pe.wait_ge(hid_mul, FT)
                    ada(g0)
                    ada(g1)
                    ada_turn(g0)
                    norm(("pre_ffn", l, which))
                    ada_turn(g1)
                    pe.wait_ge(ada_free, g1 + 1)
                    ffn(2 * l + which, ("pre_ffn", l, which))
                    norm(("post_ffn", l, which))

            heads = [(slice(0, 64), 0), (slice(64, 128), 1)]

            for l in range(LAYERS):
                norm(("ffn1", l, 0))
                ffn(3 + 2 * l, ("ffn1", l, 0))
                norm(("mix", l, 0))
                p0, c0 = l * NT2, chunk0[f"proj2{l}"]

                def tile_here(t, part, i=None):
                    if part == 0:
                        wait(pe, t_half, p0 + t + 1, i, 4)
                    elif last_of_chunk(t):
                        wait(pe, a_used, c0 + t // 2 + 1, i, 2)
                    else:
                        wait(pe, t_even, l * ((NT2 - 1) // 2) + t // 2 + 1, i, 2)

                def tile(t, i=None, bank=4):
                    wait(pe, t_free, p0 + t - 1, i, 4)
                    for k in range(KD):
                        if t == 0:
                            split_here(("mix", l, 0), k)
                        if k % (KD // 2) == 0:
                            tile_here(t, k // (KD // 2), i)
                        mm = split_product(ps[:, bank + t % 2, 0:T],
                                           (t_hi[:, t % 2, k, :], t_lo[:, t % 2, k, :], h_hi[:, k, :], h_lo[:, k, :]),
                                           start=(k == 0), stop=(k == KD - 1))
                    mm.then_inc(t_done, 1)

                def value_tiles(t):
                    pe.wait_ge(t_free, p0 + t)
                    for u in range(2):
                        for part in range(2):
                            tile_here(t + u, part)
                    for b in range(2):
                        for k in range(KD):
                            cols = slice(b * P, (b + 1) * P)
                            out = ps[:, 5 if t == MV else 7, b * T:(b + 1) * T].rearrange("p (a n) -> p a n", n=P)
                            for i, (act_, w) in enumerate(((h_hi, t_hi), (h_lo, t_hi), (h_hi, t_lo))):
                                mm = nc.tensor.matmul(out, act_[:, k, cols], w[:, :, k, :],
                                                      start=(k == 0 and i == 0), stop=(k == KD - 1 and i == 2))
                    mm.then_inc(t_done, 2)

                for t in range(4):
                    tile(t)
                with pe.Fori(0, 4) as i:
                    for u in range(4):
                        tile(4 + u, i)
                wa_up, g_up, m_up = (small[:, SM[n][0]:SM[n][1]] for n in ("waup", "gup", "mup"))
                pe.wait_ge(rw_a, RA.at("sgx", l))
                pe.wait_ge(small_loaded, 16 * (l + 1))
                half = lambda j: slice(j % 2 * T, j % 2 * T + T)
                cols = lambda j: slice(j * P, j * P + P)
                for j in range(QT):
                    mm = nc.tensor.matmul(ps[:, j // 2, half(j)], wa_up[0:64, cols(j)], tmp[0:64, 0, :],
                                          start=True, stop=True)
                mm.then_inc(rw_p, 1)
                for j in range(QT):
                    mm = nc.tensor.matmul(ps[:, 2 + j // 2, half(j)], wa_up[64:128, cols(j)], z[64:128, XWA, 1:T + 1],
                                          start=True, stop=True)
                mm.then_inc(rw_p, 1)
                for j in range(QT):
                    nc.tensor.matmul(ps[:, 6 + j // 2, half(j)], g_up[:, cols(j)], tmp[:, 1, :], start=True, stop=False)
                    mm = nc.tensor.matmul(ps[:, 6 + j // 2, half(j)], m_up[0:32, cols(j)], tmp[0:32, 2, :],
                                          start=False, stop=True)
                mm.then_inc(rw_p, 1)
                for t in range(20, 24):
                    tile(t)
                if l:
                    pe.wait_ge(rw_a, RA.at("sw", l))
                    for j in range(QT):
                        mm = nc.tensor.matmul(ps[:, j // 2, half(j)], m_up[VROW:P, cols(j)], z[VROW:P, MISC, 1:T + 1],
                                              start=True, stop=True, tile_position=(VROW, 0))
                    mm.then_inc(vres_p, 1)
                for t in range(24, MV):
                    tile(t)
                pe.wait_ge(rw_v, RV.at("kq", l))
                pe.wait_ge(rw_a, RA.at("aa", l))
                hs = const("headsum")
                for j in range(QT):
                    mm = nc.tensor.matmul(ps[0:8, 2, 0:T], hs[:, j * 8:(j + 1) * 8], e0[:, j, :],
                                          start=(j == 0), stop=(j == QT - 1))
                mm.then_inc(rw_p, 1)
                pe.wait_ge(rw_v, RV.at("rn", l))
                if l:
                    pe.wait_ge(vres_a, 1)
                hr = const("headrow")
                for j in range(QT):
                    mm = nc.tensor.matmul(ps[:, j // 2, half(j)], hr[0:8, cols(j)], inv_norm, start=True, stop=True)
                mm.then_inc(rw_p, 1)
                pe.wait_ge(rw_v, RV.at("rkr", l))
                for j in range(QT):
                    mm = nc.tensor.matmul(ps[:, 2 + j // 2, half(j)], const("headones"), bon[:, j, :],
                                          start=True, stop=True)
                mm.then_inc(rw_p, 1)
                def to_tokens(src, bank):
                    for j in range(QT):
                        for b in range(2):
                            mm = nc.tensor.transpose(ps[:, bank + j // 2, (j % 2 * 2 + b) * P:(j % 2 * 2 + b + 1) * P],
                                                     src[:, j, b * P:(b + 1) * P], ident)
                    return mm

                value_tiles(MV)
                pe.wait_ge(rw_v, RV.at("bon", l))
                to_tokens(z[:, V0:V0 + QT, 1:T + 1], 2).then_inc(rw_p, 1)
                pe.wait_ge(rw_a, RA.at("gg", l))
                pe.wait_ge(t_free, p0 + MISC + 1)
                nc.tensor.matmul(ps[0:4, 6, 0:T], const("seli"), z[:, MISC, 1:T + 1], start=True, stop=True)
                nc.tensor.matmul(ps[0:4, 6, T:2 * T], const("self"), z[:, MISC, 1:T + 1], start=True, stop=True)\
                    .then_inc(ml_p, 1)

                pe.wait_ge(rw_v, RV.at("bhc", l))
                to_tokens(khc, 0).then_inc(rw_p, 1)
                pe.wait_ge(t_free, p0 + MV + 2)
                to_tokens(bhc, 4).then_inc(rw_p, 1)
                value_tiles(MV + 2)

                pe.wait_ge(rw_v, RV.at("bhc", l))

                def unit(v, u, h):
                    j, c = u // NC_, u % NC_
                    return v[h * HD:h * HD + HD, j, c * CHUNK:(c + 1) * CHUNK]

                def out_unit(bank, u, h):
                    return ps[h * HD:h * HD + HD, bank + u // 8, u % 8 * CHUNK:(u % 8 + 1) * CHUNK]

                def per_unit(bank, left, right, us=range(UNITS)):
                    for u in us:
                        for h in range(2):
                            mm = nc.tensor.matmul(out_unit(bank, u, h), unit(left, u, h), unit(right, u, h),
                                                  start=True, stop=True)
                    return mm

                rt = z[:, R0:R0 + QT, 1:T + 1]
                pe.wait_ge(rw_a, RA.at("bhct", l))
                per_unit(4, bh, kt).then_inc(rw_p, 1)
                per_unit(0, kt, bh).then_inc(rw_p, 1)
                per_unit(2, kh, rt).then_inc(rw_p, 1)
                pe.wait_ge(ml_v, MVS.at("g", l))
                pe.wait_ge(t_free, p0 + GATES)
                per_unit(6, kh, kt).then_inc(rw_p, 1)
                pe.wait_ge(rw_v, RV.at("at", l))
                per_unit(4, bh, rt).then_inc(rw_p, 1)

                pe.wait_ge(ml_v, MVS.at("nm", l))
                pe.wait_ge(ml_a, MA.at("silu", l))
                pe.wait_ge(rw_v, RV.at("art", l))

                def front(h):
                    r, o = l * 4 + h, h % 2
                    pick = ident[0:4, h:h + 1]
                    g, neg_m, f_m = row_g, row_m, row_f
                    if h >= 2:
                        pe.wait_ge(mh_am, r - 1)
                    for b in range(2):
                        c = slice(0, T) if b == 0 else slice(T, T + P)
                        w = c.stop - c.start
                        nc.tensor.matmul(ps[:, o, c], g[:, b * P:(b + 1) * P], pick.to_broadcast([4, w]),
                                         start=True, stop=False)
                        mm = nc.tensor.matmul(ps[:, o, c], pick.to_broadcast([4, P]), neg_m[:, b * P:T],
                                              start=False, stop=True)
                    mm.then_inc(mh_arg, 1)
                    if h >= 2:
                        pe.wait_ge(mh_pm, r - 1)
                    for b in range(2):
                        c = slice(0, T) if b == 0 else slice(T, T + P)
                        mm = nc.tensor.matmul(ps[:, 2 + o, c], nsq[:, QT + h, b * P:(b + 1) * P], nsq[:, h, b * P:T],
                                              start=True, stop=True)
                    mm.then_inc(mh_s, 1)
                    if h >= 2:
                        pe.wait_ge(mh_ems, r - 1)
                    nc.tensor.matmul(ps[:, 4 + o, 0:T], pick.to_broadcast([4, P]), f_m, start=True, stop=True)\
                        .then_inc(mh_em, 1)

                front(0)
                for h in range(4):
                    r, o = l * 4 + h, h % 2
                    if h < 3:
                        front(h + 1)
                    pe.wait_ge(mh_pm, r + 1)
                    if h >= 2:
                        pe.wait_ge(mh_h, r - 1)
                    for c0_, left in ((0, lambda b: mv[:, b, h * P:(h + 1) * P]), (T, lambda b: ones)):
                        nc.tensor.matmul(ps[:, 6 + o, c0_:c0_ + T], left(0), pm[:, o, 0:T], start=True, stop=False)
                        mm = nc.tensor.matmul(ps[:, 6 + o, c0_ + P:c0_ + T], left(1), pm[:, o, T:T + P],
                                              start=False, stop=True)
                    mm.then_inc(mh_nd, 1)
                pe.wait_ge(mh_ems, l * 4 + 4)
                tile(gates_at("mean", 0)[0])
                pe.wait_ge(mh_h, l * 4 + 4)
                for j in range(QT):
                    mm = nc.tensor.matmul(ps[:, j // 2, half(j)], ones, hN[:, j, :], start=True, stop=True)
                mm.then_inc(ml_p, 1)
                tile(gates_at("mean", 1)[0])
                pe.wait_ge(ml_a, MA.at("hq", l))
                for j in range(QT):
                    mm = nc.tensor.matmul(ps[:, 2 + j // 2, half(j)], ones, hN[:, j, :], start=True, stop=True)
                mm.then_inc(ml_p, 1)

                pe.wait_ge(ml_a, MA.at("hsd", l))
                for i in range(len(LEVELS)):
                    step = l * len(LEVELS) + i
                    pe.wait_ge(lev_g, step + 1)
                    for b in range(2):
                        if i:
                            pe.wait_ge(lev_v, LV.at(f"x{b}", step - 1))
                        per_unit(0, aoff, xs, range(b * 8, b * 8 + 8)).then_inc(lev_p, 1)
                    for t in gates_at("level", i)[:1]:
                        tile(t, bank=6)
                    for b in range(2):
                        us = range(b * 8, b * 8 + 8)
                        pe.wait_ge(lev_a, LA.at(f"w{b}", step))
                        if i < len(LEVELS) - 1:
                            per_unit(2, xt, ws, us)
                        per_unit(4, ws, xt, us).then_inc(lev_p, 1)
                    for t in gates_at("level", i)[1:]:
                        tile(t, bank=6)

                pe.wait_ge(lev_v, LV.at("x1", l * len(LEVELS) + len(LEVELS) - 1))
                pe.wait_ge(rw_a, RA.at("bhct", l))
                for c in range(NC_):
                    step = l * NC_ + c

                    def sums(out, pairs):
                        for j in range(QT):
                            for h in range(2):
                                rows = slice(h * HD, h * HD + HD)
                                for i, (left, right) in enumerate(pairs):
                                    mm = nc.tensor.matmul(out(j, rows), left(j, rows), right(j, rows), start=(i == 0),
                                                          stop=(i == len(pairs) - 1))
                        return mm

                    def here(v):
                        return lambda j, rows: v[rows, j, c * CHUNK:(c + 1) * CHUNK]

                    old = lambda j, rows: state[rows, c % 2, j, :]
                    narrow = lambda bank: lambda j, rows: ps[rows, bank, j * HD:(j + 1) * HD]
                    if c:
                        pe.wait_ge(ch_v, CV.at("s", step - 1))
                    carried = [(here(kt), old)] if c else []
                    sums(narrow(0), [(here(mt), here(v_t))] + carried).then_inc(ch_p, 1)
                    tile(gates_at("chunk", c)[0], bank=6)
                    pe.wait_ge(ch_a, step + 1)
                    sums(narrow(1), [(here(xt), here(rr))]).then_inc(ch_p, 1)
                    pe.wait_ge(ch_v, CV.at("nu", step))
                    if c < NC_ - 1:
                        sums(narrow(4), [(here(khc_t), here(v_t)), (here(bhc_t), here(nu))]).then_inc(ch_p, 1)
                    carried = [(here(rt), old)] if c else []
                    sums(lambda j, rows: ps[rows, 2 + j // 2, j % 2 * T + c * CHUNK:j % 2 * T + (c + 1) * CHUNK],
                         carried + [(here(mrt), here(v_t)), (here(art), here(nu))])\
                        .then_inc(ch_p, 1 if c < NC_ - 1 else 2)
                def branch(n, part):
                    c, y = chunk0[f"br{l}"] + n // 2, (ya, yb)[part]
                    for k in range(QT):
                        mm = nc.tensor.matmul(ps[:, 4 + n % 2, part * T:(part + 1) * T],
                                              ring_a[:, c % 2, n % 2, part * QT + k, :], y[:, k, :],
                                              start=(k == 0), stop=(k == QT - 1))
                    return mm

                tile(gates_at("y", 0)[0], bank=6)
                pe.wait_ge(ml_v, MVS.at(f"yb{QT - 1}", l))
                chunk_here(chunk0[f"br{l}"], chunk0[f"br{l}"] % 2)
                pe.wait_ge(ch_v, CV.at("s", l * NC_ + NC_ - 1))
                branch(0, 1)
                branch(1, 1)
                pe.wait_ge(rw_v, RV.at("yn", l))
                for u in range(UNITS):
                    j, c = u // NC_, u % NC_
                    mm = nc.tensor.transpose(ps[0:64, u // 4, u % 4 * P:(u % 4 + 1) * P],
                                             yy[:, j, c * CHUNK:(c + 1) * CHUNK], ident)
                mm.then_inc(rw_p, 1)

                tile(gates_at("y", 1)[0], bank=6)

                pe.wait_ge(rw_v, RV.at("ya", l))
                for n in range(KD):
                    c = chunk0[f"br{l}"] + n // 2
                    if n >= 2:
                        if n % 2 == 0:
                            chunk_here(c, c % 2)
                        pe.wait_ge(br_free, l * KD + n - 1)
                        branch(n, 1)
                    branch(n, 0).then_inc(a_used if n % 2 else br_ready, 1)
                for n in range(KD // 2):
                    c = chunk0[f"out2{l}"] + n
                    chunk_here(c, c % 2)
                    for i in range(2):
                        for k in range(KD):
                            if n == 0 and i == 0:
                                pe.wait_ge(br_free, l * KD + k + 1)
                            mm = nc.tensor.matmul(ps[:, n, i * T:(i + 1) * T], ring_a[:, c % 2, i, k, :], umix[:, k, :],
                                                  start=(k == 0), stop=(k == KD - 1))
                    mm.then_inc(a_used, 1)
                norm(("ffn2", l, 0))
                ffn(4 + 2 * l, ("ffn2", l, 0))
            norm(("final", 0, 0))


def tiles_of(w):
    k, n = w.shape
    return w.reshape(k // P, P, n // P, P).transpose(2, 1, 0, 3)


def chunks_of(tiles):
    if len(tiles) % 2:
        tiles = np.concatenate([tiles, np.zeros_like(tiles[:1])])
    n, p, k, c = tiles.shape
    return tiles.reshape(n // 2, 2, p, k, c).transpose(0, 2, 1, 3, 4).reshape(n // 2, p, -1)


def columns(v):
    return np.asarray(v).reshape(-1, P).T


def lay_out(a):
    zeros = lambda *s: np.zeros(s, np.float32)
    ffn_chunks = lambda g, u: np.stack([tiles_of(g), tiles_of(u)], 1).reshape(-1, P, KD, P)
    wa = [chunks_of(tiles_of(a["w_ada"][l])) for l in range(LAYERS)]
    q_heads = [h for j in range(4) for h in (j, j + 4)]
    q_cols = np.concatenate([np.arange(h * HD, h * HD + HD) for h in q_heads])
    for l in range(LAYERS):
        w = a["w_in"][l]
        w = np.concatenate([w[:, 512:640], w[:, q_cols], w[:, 640:768], w[:, 768:1280]], 1)
        w_out = np.concatenate([a["w_out"][l][q_cols], a["w_out"][l][512:]], 0)
        wa += [chunks_of(tiles_of(w)), chunks_of(tiles_of(w_out)),
               chunks_of(ffn_chunks(a["w_gate"][l], a["w_up"][l]))]
    small, mus = [], []
    for l in range(LAYERS):
        w = a["w_in_2"][l]
        at = 0
        part = {}
        for name, n in (("r", 512), ("k", 512), ("v", 512), ("xw", 64), ("xa", 64), ("xg", 160), ("mq", 512),
                        ("mk", 512), ("mv", 512), ("mo", 512), ("mi", 4), ("mf", 4), ("g", 2048)):
            part[name] = w[:, at:at + n]
            at += n
        down = a["vres_down_2"][l - 1] if l else zeros(D, 32)
        misc = np.concatenate([part["xg"][:, P:], part["mi"], zeros(D, 28), part["mf"], zeros(D, 28), down], 1)
        w = np.concatenate([part["r"], part["k"], part["v"], part["xw"], part["xa"], part["xg"][:, :P], misc,
                            part["mq"], part["mk"], part["mo"], part["mv"], part["g"]], 1)
        br = np.concatenate([tiles_of(a["br_a_2"][l]), tiles_of(a["br_b_2"][l])], 2)
        f1, f2 = a["ffn1_w_in_2"][l], a["ffn2_w_in_2"][l]
        wa += [chunks_of(ffn_chunks(f1[:, :FFN], f1[:, FFN:])), chunks_of(tiles_of(w)), chunks_of(br),
               chunks_of(tiles_of(a["w_out_2"][l])), chunks_of(ffn_chunks(f2[:, :FFN], f2[:, FFN:]))]
        up = a["vres_up_2"][l - 1] if l else zeros(32, 512)
        g_up = a["rw_g_up_2"][l]
        small.append(np.concatenate([np.concatenate([a["rw_w_up_2"][l], a["rw_a_up_2"][l]], 0), g_up[:P],
                                     np.concatenate([g_up[P:], zeros(64, 512), up], 0)], 1))
        mu = a["shift_mu_2"][l]
        mus.append(np.concatenate([mu, zeros(96)]))
    wd = np.concatenate([a["w_down"], np.stack([a[f"ffn{i}_w_out_2"][l] for l in range(LAYERS) for i in (1, 2)])])
    wd = wd.reshape(-1, P, D)

    vec = {"c": np.stack([a["c"][0].reshape(KD, P), a["c_ctx"].reshape(KD, P)], 1).reshape(-1, P).T,
           "b_ada": columns(a["b_ada"].reshape(-1)), "final": columns(a["final_norm_2"]),
           "vbias1": columns(a["vres_bias_2"][0]),
           "sink": np.broadcast_to(a["sink"].reshape(1, -1), (P, LAYERS * 8))}
    for l in range(LAYERS):
        for name, src in (("pre_mix", "norm_pre_mix"), ("post_mix", "norm_post_mix"), ("pre_ffn", "norm_pre_ffn"),
                          ("post_ffn", "norm_post_ffn"), ("ffn1", "ffn1_norm_2"), ("mix", "mix_norm_2"),
                          ("ffn2", "ffn2_norm_2"), ("conv_b", "ml_conv_b_2"), ("w0", "rw_w0_2"), ("a0", "rw_a0_2"),
                          ("k_k", "rw_k_k_2"), ("k_a", "rw_k_a_2"), ("r_k", "rw_r_k_2"), ("gn_w", "rw_gn_w_2"),
                          ("gn_b", "rw_gn_b_2"), ("ml_w", "ml_norm_w_2")):
            vec[f"{name}{l}"] = columns(a[src][l].reshape(-1))
        for t in range(4):
            vec[f"tap{t}{l}"] = columns(a["ml_conv_w_2"][l, t])
        vec[f"mu{l}"] = columns(mus[l])
        for name, src in (("ib", "ml_i_bias_2"), ("fb", "ml_f_bias_2")):
            vec[f"{name}{l}"] = np.concatenate([a[src][l], zeros(P - 4)])[:, None]
    vec = np.concatenate([vec[n] for n in V], 1)
    four = np.zeros((LAYERS, QT, 2, HD, 2, HD), np.float32)
    w4 = a["w_fourier"].reshape(LAYERS, QT, 2, HD, HD)
    for h in range(2):
        four[:, :, h, :, h, :] = w4[:, :, h]
    four = four.reshape(LAYERS * QT, P, P).transpose(1, 0, 2).reshape(P, -1)
    c1, c2 = constants()
    rows = lambda v: np.asarray(v[0]).T.reshape(KD, P, T).transpose(1, 0, 2)
    full = np.ascontiguousarray
    return {"wa": full(np.concatenate(wa)), "wd": full(wd), "c1": full(c1), "c2": full(c2), "vec": full(vec),
            "small": full(np.stack(small)), "four": full(four), "x": full(rows(a["x"])), "ctx": full(rows(a["ctx"]))}


def kernel(**inputs):
    import concourse.bacc as bacc
    from concourse.bass_utils import run_bass_kernel_spmd

    arrays = lay_out({n: np.asarray(v) for n, v in inputs.items()})
    nc = bacc.Bacc("TRN2", target_bir_lowering=False, num_devices=1)
    args = [nc.dram_tensor(f"in_{n}", v.shape, F32, kind="ExternalInput").ap() for n, v in arrays.items()]
    out = nc.dram_tensor("out", (P, KD, T), F32, kind="ExternalOutput").ap()
    program(nc, *args, out)
    got = run_bass_kernel_spmd(nc, [{f"in_{n}": v for n, v in arrays.items()}], core_ids=[0])
    return np.ascontiguousarray(got.results[0]["out"].transpose(2, 1, 0).reshape(1, T, D))
```
